# Optimizing a Trainium2 kernel written in Bass

```python
import math
import jax, jax.numpy as jnp
from jax import lax
import numpy as np

D_MODEL = 2048
BATCH = 1
SEQ = 256
DEPTH = 1

HEAD_DIM = 64
D_MIX = D_MODEL
N_MIX_HEADS = D_MIX // HEAD_DIM
N_CONV_GROUPS = N_MIX_HEADS // 4
N_FOX_HEADS = (N_MIX_HEADS - N_CONV_GROUPS) // 2
N_NSA_HEADS = N_MIX_HEADS - N_CONV_GROUPS - N_FOX_HEADS
NSA_GROUP = 4
N_NSA_KV = N_NSA_HEADS // NSA_GROUP
D_FOX = N_FOX_HEADS * HEAD_DIM
D_NSA = N_NSA_HEADS * HEAD_DIM
D_NSA_KV = N_NSA_KV * HEAD_DIM
D_CONV = N_CONV_GROUPS * HEAD_DIM
IN_SPLITS = (D_FOX, D_FOX, D_FOX, N_FOX_HEADS,
             D_NSA, D_NSA_KV, D_NSA_KV, D_NSA_KV, D_NSA_KV, D_NSA_KV, D_NSA_KV, 3 * N_NSA_HEADS,
             D_CONV, D_CONV)
D_IN = sum(IN_SPLITS)
D_FF = 4 * D_MODEL
Q_BLOCK = 128
CMP_LEN = 32
CMP_STRIDE = 16
SEL_LEN = 64
N_SEL = 16
WINDOW = 512
CONV_WIDTH = 31
N_BUCKETS = 32
MAX_DISTANCE = 128
EPS = 1e-6
NEG = -1e30
BIG = 1e9

kernel_name = "hybrid_fox_nsa_conformer_adaln_trunk"

def rms_norm(x, g):
    xf = x.astype(jnp.float32)
    y = xf * lax.rsqrt(jnp.mean(xf * xf, axis=-1, keepdims=True) + EPS)
    return (y * g.astype(jnp.float32)).astype(x.dtype)

def layer_norm(x, g, b):
    xf = x.astype(jnp.float32)
    mu = jnp.mean(xf, axis=-1, keepdims=True)
    var = jnp.mean(jnp.square(xf - mu), axis=-1, keepdims=True)
    y = (xf - mu) * lax.rsqrt(var + EPS) * g.astype(jnp.float32) + b.astype(jnp.float32)
    return y.astype(x.dtype)

def masked_softmax(s, mask):
    p = jax.nn.softmax(jnp.where(mask, s, NEG), axis=-1)
    return jnp.where(mask, p, 0.0)

def t5_bucket(dist):
    n = jnp.maximum(dist, 0)
    max_exact = N_BUCKETS // 2
    nf = jnp.maximum(n, 1).astype(jnp.float32)
    large = max_exact + (jnp.log(nf / max_exact) / math.log(MAX_DISTANCE / max_exact)
                         * (N_BUCKETS - max_exact)).astype(jnp.int32)
    large = jnp.minimum(large, N_BUCKETS - 1)
    return jnp.where(n < max_exact, n, large)

def qk_bias(table, dist):
    q_len, k_len = dist.shape
    b = table[t5_bucket(dist)]
    return b.reshape(q_len, k_len, N_NSA_KV, NSA_GROUP).transpose(2, 3, 0, 1)

def fox_attention(q, k, v, log_f):
    B, S, H, Dh = q.shape
    scale = Dh ** -0.5
    Fh = jnp.cumsum(log_f, axis=1).transpose(0, 2, 1)
    kpos = jnp.arange(S)

    def block(i):
        t0 = i * Q_BLOCK
        qpos = t0 + jnp.arange(Q_BLOCK)
        qb = lax.dynamic_slice_in_dim(q, t0, Q_BLOCK, axis=1)
        Fq = lax.dynamic_slice_in_dim(Fh, t0, Q_BLOCK, axis=2)
        s = jnp.einsum('bqhd,bkhd->bhqk', qb, k, preferred_element_type=jnp.float32) * scale
        s = s + Fq[..., :, None] - Fh[..., None, :]
        p = masked_softmax(s, kpos[None, :] <= qpos[:, None])
        return jnp.einsum('bhqk,bkhd->bqhd', p.astype(v.dtype), v)

    out = lax.map(block, jnp.arange(S // Q_BLOCK))
    return out.transpose(1, 0, 2, 3, 4).reshape(B, S, H * Dh)

def nsa_attention(q, kc, vc, ks, vs, kw, vw, gates, w_cmp_k, w_cmp_v, pos_cmp, rel_bias):
    B, S, H, Dh = q.shape
    G, R = N_NSA_KV, NSA_GROUP
    scale = Dh ** -0.5
    n_cmp = (S - CMP_LEN) // CMP_STRIDE + 1
    n_sel = S // SEL_LEN
    n_top = min(N_SEL, n_sel)
    T = n_top * SEL_LEN
    cidx = jnp.arange(n_cmp)[:, None] * CMP_STRIDE + jnp.arange(CMP_LEN)[None, :]
    cmp_end = cidx[:, -1]
    pos = pos_cmp[None, None, :, None, :]
    k_cmp = jnp.einsum('bnlgd,lde->bnge', kc[:, cidx] + pos, w_cmp_k)
    v_cmp = jnp.einsum('bnlgd,lde->bnge', vc[:, cidx] + pos, w_cmp_v)
    sel_start = jnp.arange(n_sel) * SEL_LEN
    overlap = ((cidx[:, 0][:, None] < sel_start[None, :] + SEL_LEN)
               & (cmp_end[:, None] >= sel_start[None, :])).astype(jnp.float32)
    ks_t = ks.transpose(0, 2, 1, 3)
    vs_t = vs.transpose(0, 2, 1, 3)
    pad = ((0, 0), (WINDOW, 0), (0, 0), (0, 0))
    kw_pad = jnp.pad(kw, pad)
    vw_pad = jnp.pad(vw, pad)
    table = rel_bias.astype(jnp.float32)
    tbl_g = table.reshape(N_BUCKETS, G, R).transpose(1, 0, 2)
    gates = gates.reshape(B, S, H, 3)
    gather = jax.vmap(jax.vmap(lambda a, ix: a[ix]))
    lookup = jax.vmap(lambda tb, bk: tb[bk], in_axes=(0, 1), out_axes=1)
    j = jnp.arange(n_sel)

    def block(i):
        t0 = i * Q_BLOCK
        qpos = t0 + jnp.arange(Q_BLOCK)
        qg = lax.dynamic_slice_in_dim(q, t0, Q_BLOCK, axis=1).reshape(B, Q_BLOCK, G, R, Dh)
        gb = lax.dynamic_slice_in_dim(gates, t0, Q_BLOCK, axis=1).reshape(B, Q_BLOCK, G, R, 3)
        s_c = jnp.einsum('bqgrd,bngd->bgrqn', qg, k_cmp, preferred_element_type=jnp.float32) * scale
        s_c = s_c + qk_bias(table, qpos[:, None] - cmp_end[None, :])
        p_c = masked_softmax(s_c, cmp_end[None, :] <= qpos[:, None])
        o_c = jnp.einsum('bgrqn,bngd->bqgrd', p_c.astype(v_cmp.dtype), v_cmp)
        imp = jnp.einsum('bgrqn,nj->bgqj', p_c, overlap)
        cur = qpos // SEL_LEN
        forced = (j[None, :] == 0) | (j[None, :] == cur[:, None]) | (j[None, :] == cur[:, None] - 1)
        valid = sel_start[None, :] <= qpos[:, None]
        imp = jnp.where(forced, BIG, jnp.where(valid, imp, NEG))
        _, top = lax.top_k(imp, n_top)
        tok = (top[..., None] * SEL_LEN + jnp.arange(SEL_LEN)).reshape(B, G, Q_BLOCK, T)
        flat = tok.reshape(B, G, Q_BLOCK * T)
        k_sel = gather(ks_t, flat).reshape(B, G, Q_BLOCK, T, Dh)
        v_sel = gather(vs_t, flat).reshape(B, G, Q_BLOCK, T, Dh)
        b_sel = lookup(tbl_g, t5_bucket(qpos[None, None, :, None] - tok))
        s_s = jnp.einsum('bqgrd,bgqtd->bgrqt', qg, k_sel, preferred_element_type=jnp.float32) * scale
        s_s = s_s + b_sel.transpose(0, 1, 4, 2, 3)
        p_s = masked_softmax(s_s, (tok <= qpos[None, None, :, None])[:, :, None])
        o_s = jnp.einsum('bgrqt,bgqtd->bqgrd', p_s.astype(v_sel.dtype), v_sel)
        kwb = lax.dynamic_slice_in_dim(kw_pad, t0, WINDOW + Q_BLOCK, axis=1)
        vwb = lax.dynamic_slice_in_dim(vw_pad, t0, WINDOW + Q_BLOCK, axis=1)
        kpos = t0 - WINDOW + jnp.arange(WINDOW + Q_BLOCK)
        dist = qpos[:, None] - kpos[None, :]
        s_w = jnp.einsum('bqgrd,bkgd->bgrqk', qg, kwb, preferred_element_type=jnp.float32) * scale
        s_w = s_w + qk_bias(table, dist)
        p_w = masked_softmax(s_w, (dist >= 0) & (dist < WINDOW) & (kpos[None, :] >= 0))
        o_w = jnp.einsum('bgrqk,bkgd->bqgrd', p_w.astype(vwb.dtype), vwb)
        g = jax.nn.sigmoid(gb.astype(jnp.float32))
        out = g[..., 0:1] * o_c + g[..., 1:2] * o_s + g[..., 2:3] * o_w
        return out.astype(q.dtype)

    out = lax.map(block, jnp.arange(S // Q_BLOCK))
    return out.transpose(1, 0, 2, 3, 4, 5).reshape(B, S, H * Dh)

def conformer_conv(a, gate, w_dw, b_dw, ln_g, ln_b):
    u = a * jax.nn.sigmoid(gate)
    y = lax.conv_general_dilated(u, w_dw[:, None, :], window_strides=(1,),
                                 padding=[(CONV_WIDTH - 1, 0)],
                                 dimension_numbers=('NWC', 'WIO', 'NWC'),
                                 feature_group_count=u.shape[-1])
    y = layer_norm(y + b_dw, ln_g, ln_b)
    return jax.nn.silu(y)

def split_in(z):
    pts = np.cumsum(np.array(IN_SPLITS))[:-1].tolist()
    return jnp.split(z, pts, axis=-1)

def setup_inputs(seed: int = 0) -> dict:
    key = jax.random.key(seed)
    ks = jax.random.split(key, 24)
    n = jax.random.normal
    f32 = jnp.float32
    L, Dh = CMP_LEN, HEAD_DIM
    return {
        "x": n(ks[0], (BATCH, SEQ, D_MODEL), f32),
        "c": n(ks[1], (BATCH, D_MODEL), f32),
        "w_mod": n(ks[2], (DEPTH, D_MODEL, 6 * D_MODEL), f32) * (0.5 * D_MODEL ** -0.5),
        "b_mod": n(ks[3], (DEPTH, 6 * D_MODEL), f32) * 0.02,
        "norm1_g": 1.0 + 0.05 * n(ks[4], (DEPTH, D_MODEL), f32),
        "w_in": n(ks[5], (DEPTH, D_MODEL, D_IN), f32) * D_MODEL ** -0.5,
        "b_f": jax.random.uniform(ks[6], (DEPTH, N_FOX_HEADS), f32, 3.0, 6.0),
        "w_cmp_k": n(ks[7], (DEPTH, L, Dh, Dh), f32) * (L * Dh) ** -0.5,
        "w_cmp_v": n(ks[8], (DEPTH, L, Dh, Dh), f32) * (L * Dh) ** -0.5,
        "pos_cmp": n(ks[9], (DEPTH, L, Dh), f32) * 0.5,
        "conv_w": n(ks[10], (DEPTH, CONV_WIDTH, D_CONV), f32) * CONV_WIDTH ** -0.5,
        "conv_b": n(ks[11], (DEPTH, D_CONV), f32) * 0.02,
        "conv_ln_g": 1.0 + 0.05 * n(ks[12], (DEPTH, D_CONV), f32),
        "conv_ln_b": n(ks[13], (DEPTH, D_CONV), f32) * 0.02,
        "w_out": n(ks[14], (DEPTH, D_MIX, D_MODEL), f32) * D_MIX ** -0.5,
        "norm2_g": 1.0 + 0.05 * n(ks[15], (DEPTH, D_MODEL), f32),
        "w_mlp1": n(ks[16], (DEPTH, D_MODEL, D_FF), f32) * D_MODEL ** -0.5,
        "w_mlp2": n(ks[17], (DEPTH, D_FF, D_MODEL), f32) * D_FF ** -0.5,
        "rel_bias": n(ks[18], (N_BUCKETS, N_NSA_HEADS), f32) * 0.5,
        "final_g": 1.0 + 0.05 * n(ks[19], (D_MODEL,), f32),
    }

def reference(x, c, w_mod, b_mod, norm1_g, w_in, b_f, w_cmp_k, w_cmp_v, pos_cmp,
              conv_w, conv_b, conv_ln_g, conv_ln_b, w_out, norm2_g, w_mlp1, w_mlp2,
              rel_bias, final_g):
    B, S, _ = x.shape
    c_act = jax.nn.silu(c)
    for l in range(DEPTH):
        mod = (c_act @ w_mod[l] + b_mod[l])[:, None, :]
        sh1, sc1, g1, sh2, sc2, g2 = jnp.split(mod, 6, axis=-1)
        h = rms_norm(x, norm1_g[l]) * (1.0 + sc1) + sh1
        (fq, fk, fv, ff, nq, kc, vc, ksl, vsl, kwn, vwn, ng, ca, cg) = split_in(h @ w_in[l])
        hd = lambda t: t.reshape(B, S, -1, HEAD_DIM)
        log_f = jax.nn.log_sigmoid(ff.astype(jnp.float32) + b_f[l].astype(jnp.float32))
        o_fox = fox_attention(hd(fq), hd(fk), hd(fv), log_f)
        o_nsa = nsa_attention(hd(nq), hd(kc), hd(vc), hd(ksl), hd(vsl), hd(kwn), hd(vwn), ng,
                              w_cmp_k[l], w_cmp_v[l], pos_cmp[l], rel_bias)
        o_conv = conformer_conv(ca, cg, conv_w[l], conv_b[l], conv_ln_g[l], conv_ln_b[l])
        mixed = jnp.concatenate([o_fox, o_nsa, o_conv], axis=-1)
        x = x + g1 * (mixed @ w_out[l])
        h = rms_norm(x, norm2_g[l]) * (1.0 + sc2) + sh2
        x = x + g2 * (jnp.square(jax.nn.relu(h @ w_mlp1[l])) @ w_mlp2[l])
    return rms_norm(x, final_g)


_drawn_inputs = setup_inputs


def setup_inputs(seed=0):
    import zlib

    import numpy as np

    out = dict(_drawn_inputs(seed))
    spreads = {}
    factors = {'norm1_g': 6.885,
     'b_f': 4.004,
     'conv_b': 29.718,
     'conv_ln_g': 24.863,
     'conv_ln_b': 62.929,
     'rel_bias': 2.702,
     'norm2_g': 4.973,
     'pos_cmp': 3.029}
    for name, (base, spread) in spreads.items():
        noise = np.random.default_rng([zlib.crc32(name.encode()), seed]).standard_normal(out[name].shape)
        drawn = base * np.exp(spread * noise) if base else spread * noise
        out[name] = __import__('jax').numpy.asarray(drawn.astype(out[name].dtype))
    for name, factor in factors.items():
        out[name] = (out[name] * factor).astype(out[name].dtype)
    return out
```

```python
import math
from contextlib import ExitStack

import numpy as np
import concourse.bass as bass
from concourse import mybir

P = 128
D = 2048
S = 256
TT = S // P
KT = D // P
FF = 4 * D
HD = 64
NFOX = 12
NNSA = 12
NKV = 3
NCMP = 15
NCMP0 = 7
CMP_STRIDE = 16
CMP_LEN = 32
CONV_W = 31
CT = 4
D_CONV = CT * P
GW = 512
TAIL = 176
NB = 32
NEG = -1e30
EPS = 1e-6
QUARTERS = 4
HALVES = 8
N_IN = 11
G_OUT = N_IN
G_MLP = G_OUT + 4
N_GROUPS = G_MLP + 8 * QUARTERS
VCOLS = 2 * GW + TAIL
COL_F = 1152
COL_G = COL_F + NFOX
BPAD = 384
CONV_STEPS = CT * CONV_W


def view(ap, dims, shift=0):
    return bass.AP(ap.tensor, ap.offset + shift, [list(ap.ap[0])] + [list(d) for d in dims])


def build(nc, x_d, c_d, wmod_d, bmod_d, n1_d, n2_d, fg_d, main_d, tail_d, bf_d, wck_d, wcv_d, pos_d,
          convw_d, convb_d, lng_d, lnb_d, rel_d, onehot_d, out_d):
    f32, f32r = mybir.dt.float32, mybir.dt.float32r
    ALU, ACT, AX = mybir.AluOpType, mybir.ActivationFunctionType, mybir.AxisListType
    bias_scratch = nc.dram_tensor("bias_scratch", (NNSA, BPAD), f32, kind="Internal").ap()

    ctx = ExitStack()
    with ctx:
        def sb(name, shape, dt=f32, where=ctx):
            return where.enter_context(nc.sbuf_tensor(name, shape, dt))

        def sem(name):
            return ctx.enter_context(nc.semaphore(name))

        raw = [sb(f"raw{i}", [P, 4 * GW]) for i in range(4)]
        w_hi = [sb(f"w_hi{i}", [P, 2 * GW], f32r) for i in range(4)]
        w_lo = [sb(f"w_lo{i}", [P, 2 * GW], f32r) for i in range(4)]
        mod_raw = [sb(f"mod_raw{i}", [P, 4 * GW]) for i in range(2)]
        acc = [sb(f"acc{i}", [P, D]) for i in range(2)]
        ident = sb("ident", [P, P])
        ones = sb("ones", [P, P])
        ones_conv = sb("ones_conv", [P, P])
        tri = sb("tri", [P, P])
        causal = sb("causal", [P, S])
        neg_id = sb("neg_id", [P, NFOX])
        seen = sb("seen", [P, 1])
        c_col = sb("c_col", [P, KT])
        c_tmp = sb("c_tmp", [P, KT])
        c_act = sb("c_act", [P, KT])
        n1 = sb("n1", [P, KT])
        n2 = sb("n2", [P, KT])
        scale_h = sb("scale_h", [P, KT])
        shift_h = sb("shift_h", [P, KT])
        shift2 = sb("shift2", [P, KT])
        ssq = sb("ssq", [P, 3 * TT])
        mean_sq = sb("mean_sq", [P, TT])
        root = sb("root", [P, TT])
        rstd = sb("rstd", [P, TT])
        newton = sb("newton", [P, TT])
        bf_b = sb("bf_b", [P, NFOX])
        convw = sb("convw", [P, CT, CONV_W])
        convb = sb("convb", [P, CT])
        lng = sb("lng", [P, CT])
        lnb = sb("lnb", [P, CT])
        pos_t = sb("pos_t", [P, CMP_LEN])
        rel_t = sb("rel_t", [NB, NNSA])

        region = ExitStack()
        act_hi = sb("act_hi", [P, KT, S], f32r, region)
        act_lo = sb("act_lo", [P, KT, S], f32r, region)
        region.close()
        region = ExitStack()
        bias_t = sb("bias_t", [P, NNSA, S], f32, region)
        wck = sb("wck", [P, CMP_STRIDE, HD], f32, region)
        wcv = sb("wcv", [P, CMP_STRIDE, HD], f32, region)
        cmp_in = sb("cmp_in", [P, 6, S], f32, region)
        region.close()
        hold = sb("hold", [P, 2 * KT * S])
        phase = ExitStack()
        x_a = sb("x_a", [P, TT, D], f32, phase)
        xn_t = sb("xn_t", [P, KT, S], f32, phase)
        onehot = sb("onehot", [NB, S], f32, phase)
        bias_p = sb("bias_p", [NNSA, BPAD], f32, phase)
        h_f = [sb(f"h_f{i}", [P, 2 * S], f32, phase) for i in range(2)]
        sq_a = sb("sq_a", [P, D], f32, phase)
        phase.close()
        phase = ExitStack()
        z_t = sb("z_t", [P, 24, S], f32, phase)
        val = sb("val", [P, TT, VCOLS], f32, phase)
        conv_in = sb("conv_in", [P, CT, CONV_W - 1 + S], f32, phase)
        conv_y = sb("conv_y", [P, CT, S], f32, phase)
        k_swap = sb("k_swap", [P, 3, S], f32, phase)
        score = [sb(f"score{i}", [P, 3 * P], f32, phase) for i in range(3)]
        prob_t = [sb(f"prob_t{i}", [P, 3 * P], f32, phase) for i in range(2)]
        mix = sb("mix", [P, TT, NFOX * HD + NNSA * HD], f32, phase)
        add_t = sb("add_t", [P, TT * 4 * HD], f32, phase)
        neg_max = sb("neg_max", [P, 72], f32, phase)
        row_sum = sb("row_sum", [P, 72], f32, phase)
        row_r = sb("row_r", [P, 72], f32, phase)
        log_f = sb("log_f", [P, TT, NFOX], f32, phase)
        lf = [sb(f"lf{i}", [P, TT, NFOX], f32, phase) for i in range(5)]
        gate = sb("gate", [P, TT, 3 * NNSA], f32, phase)
        f_q = sb("f_q", [P, TT, NFOX], f32, phase)
        f_t = sb("f_t", [P, S], f32, phase)
        k_cmp = sb("k_cmp", [P, NKV, NCMP], f32, phase)
        v_cmp_t = sb("v_cmp_t", [HD, NKV, P], f32, phase)
        v_cmp = sb("v_cmp", [P, NKV, HD], f32, phase)
        cmp_m = sb("cmp_m", [P, TT * NNSA], f32, phase)
        cmp_r = sb("cmp_r", [P, TT * NNSA], f32, phase)
        phase.close()
        phase = ExitStack()
        x2 = sb("x2", [P, TT, D], f32, phase)
        upd = sb("upd", [P, TT * GW], f32, phase)
        late = ExitStack()
        xn2 = sb("xn2", [P, TT, D], f32, late)
        h2_f = [sb(f"h2_f{i}", [P, 2 * S], f32, late) for i in range(2)]
        late.close()
        u_hi = sb("u_hi", [P, KT, S], f32r, phase)
        u_lo = sb("u_lo", [P, KT, S], f32r, phase)
        relu = sb("relu", [P, 4 * S], f32, phase)
        phase.close()
        y_out = [raw[i] for i in range(4)]
        p_cmp_t = z_t[:, 18:21, :]
        p_cmp = z_t[:, 0:3, :].rearrange("p k t -> p (k t)").rearrange("p (t h n) -> p t h n", t=TT, h=NNSA)
        s_cmp = z_t[:, 3:5, :].rearrange("p k t -> p (k t)")[:, 0:TT * NNSA * 16]\
            .rearrange("p (t h n) -> p t h n", t=TT, h=NNSA)
        var_b, root_b, inv_b, newton_b = (conv_in[:, i, 0:S] for i in range(4))

        pair = [ctx.enter_context(nc.psum_tensor(f"pair{i}", [P, 2 * GW], f32)) for i in range(2)]
        aux = [ctx.enter_context(nc.psum_tensor(f"aux{i}", [P, GW], f32)) for i in range(4)]
        t_bank = [pair[1][:, 0:GW], pair[1][:, GW:2 * GW]]
        o_bank = [pair[0][:, 0:GW], pair[0][:, GW:2 * GW]]

        small_in = sem("small_in")
        x_in = sem("x_in")
        consts = sem("consts")
        raw_full = [sem(f"raw_full{i}") for i in range(4)]
        mod_full = [sem(f"mod_full{i}") for i in range(2)]
        hi_done = sem("hi_done")
        lo_done = sem("lo_done")
        pe_half = sem("pe_half")
        evac_act = sem("evac_act")
        evac_dve = sem("evac_dve")
        mod_step = sem("mod_step")
        acc_zero = sem("acc_zero")
        acc_init = [sem(f"acc_init{i}") for i in range(6)]
        pe_mod = sem("pe_mod")
        c_sig = sem("c_sig")
        act_sq = sem("act_sq")
        act_root = sem("act_root")
        dve_ms = sem("dve_ms")
        rstd_ok = sem("rstd_ok")
        xn_ok = sem("xn_ok")
        xt_ps = sem("xt_ps")
        xt_ok = sem("xt_ok")
        col_ok = sem("col_ok")
        h_ok = sem("h_ok")
        h_ready = sem("h_ready")
        h2_ready = sem("h2_ready")
        mix_ready = sem("mix_ready")
        u_ready = sem("u_ready")
        dve_c = sem("dve_c")
        pool_c = sem("pool_c")
        bias_ps = sem("bias_ps")
        bias_row = sem("bias_row")
        bias_out = sem("bias_out")
        bias_in = sem("bias_in")
        cmp_w_in = sem("cmp_w_in")
        gate_row = sem("gate_row")
        conv_e = sem("conv_e")
        conv_sem = sem("conv_sem")
        ln_ps = sem("ln_ps")
        ln_root = sem("ln_root")
        ln_sig = sem("ln_sig")
        ln_sq = sem("ln_sq")
        ln_var = sem("ln_var")
        ln_y = sem("ln_y")
        lf_in = sem("lf_in")
        lf_exp = sem("lf_exp")
        gate_ok = sem("gate_ok")
        lf_ok = sem("lf_ok")
        f_ps = sem("f_ps")
        f_sb = sem("f_sb")
        s_ready = sem("s_ready")
        s_biased = sem("s_biased")
        p_ready = sem("p_ready")
        t_ready = sem("t_ready")
        t_act = sem("t_act")
        t_dve = sem("t_dve")
        o_ready = sem("o_ready")
        o_used = sem("o_used")
        swap_ok = sem("swap_ok")
        cmp_x = sem("cmp_x")
        cmp_ps = sem("cmp_ps")
        cmp_sb = sem("cmp_sb")
        cmp_exp = sem("cmp_exp")
        mix_done = sem("mix_done")
        mt_ps = sem("mt_ps")
        mt_hi = sem("mt_hi")
        h_hi = sem("h_hi")
        relu_ok = sem("relu_ok")
        u_step = sem("u_step")
        x2_in = sem("x2_in")
        x2_sum = sem("x2_sum")
        fg_in = sem("fg_in")
        y_ok = sem("y_ok")
        y_out_s = sem("y_out_s")

        N_SMALL = 12

        def block_half(tensor, j, width):
            return tensor[(j // 2) % 4][:, (j % 2) * 2 * width:(j % 2 + 1) * 2 * width]

        block = ctx.enter_context(nc.Block())

        @block.sync
        def _(sp):
            def weights(g, q, source=None):
                if not (isinstance(g, int) and g == 0):
                    sp.wait_ge(lo_done, (g - 1) * 8 + 2 * q + 2)
                if source is None:
                    sp.dma_start(raw[q][:, :], main_d[g * 4 + q, :, :]).then_inc(raw_full[q], 16)
                else:
                    sp.dma_start(raw[q][:, 0:4 * TAIL], source).then_inc(raw_full[q], 16)

            def modulation(m, slot):
                if not (isinstance(m, int) and m < 2):
                    sp.wait_ge(mod_step, (m - 1) * 4 + 1)
                sp.dma_start(mod_raw[slot][:, :], wmod_d[m, :, :]).then_inc(mod_full[slot], 16)

            for tt in range(TT):
                sp.dma_start(x_a[:, tt, :], x_d[tt * P:(tt + 1) * P, :]).then_inc(x_in, 16)
            modulation(0, 0)
            modulation(1, 1)
            with sp.Fori(1, 16) as i:
                modulation(i * 2, 0)
                modulation(i * 2 + 1, 1)
            for g in range(N_IN):
                for q in range(4):
                    if g == 8:
                        weights(g, q, tail_d[q, :, :])
                    else:
                        weights(g, q)
                    if g < 8:
                        modulation(32 + 4 * g + q, q % 2)
            for i in range(4):
                for q in range(4):
                    weights(G_OUT + i, q)
                    modulation(64 + 4 * i + q, q % 2)
                if i == 0:
                    sp.wait_ge(mix_ready, 8)
                    for tt in range(TT):
                        sp.dma_start(x2[:, tt, :], x_d[tt * P:(tt + 1) * P, :]).then_inc(x2_in, 16)
            for i in range(4):
                for q in range(4):
                    weights(G_MLP + i, q)
                    modulation(80 + 4 * i + q, q % 2)
            sp.wait_ge(pe_mod, 5)
            sp.dma_start(acc[1][:, :], fg_d.to_broadcast([P, D])).then_inc(fg_in, 16)
            with sp.Fori(G_MLP + 4, N_GROUPS) as g:
                for q in range(4):
                    weights(g, q)
            for i in range(4):
                tt, half = i // 2, i % 2
                sp.wait_ge(y_ok, i + 1)
                sp.dma_start(out_d[tt * P:(tt + 1) * P, half * D // 2:(half + 1) * D // 2],
                             y_out[i][:, 0:D // 2]).then_inc(y_out_s, 16)
            sp.wait_ge(y_out_s, 4 * 16)

        @block.gpsimd
        def _(pool):
            n = 0

            def step(ins):
                nonlocal n
                ins.then_inc(pool_c, 1)
                n += 1
                pool.wait_ge(pool_c, n)

            step(nc.gpsimd.memset(ident[:, :], 0.0))
            step(nc.gpsimd.affine_select(out=ident[:, :], in_=ident[:, :], compare_op=ALU.not_equal, fill=1.0,
                                         base=0, pattern=[[-1, P]], channel_multiplier=1))
            step(nc.gpsimd.memset(ones[:, :], 1.0))
            step(nc.gpsimd.memset(ones_conv[:, :], 1.0 / D_CONV))
            step(nc.gpsimd.memset(tri[:, :], 1.0))
            step(nc.gpsimd.affine_select(out=tri[:, :], in_=tri[:, :], compare_op=ALU.is_ge, fill=0.0,
                                         base=0, pattern=[[1, P]], channel_multiplier=-1))
            step(nc.gpsimd.memset(causal[:, :], 0.0))
            step(nc.gpsimd.affine_select(out=causal[:, :], in_=causal[:, :], compare_op=ALU.is_ge, fill=NEG,
                                         base=P, pattern=[[-1, S]], channel_multiplier=1))
            step(nc.gpsimd.memset(neg_id[:, :], 0.0))
            for base in (0, HD):
                step(nc.gpsimd.affine_select(out=neg_id[:, :], in_=neg_id[:, :], compare_op=ALU.not_equal,
                                             fill=-1.0, base=-base, pattern=[[-1, NFOX]], channel_multiplier=1))
            step(nc.gpsimd.memset(seen[:, :], 1.0))
            step(nc.gpsimd.affine_select(out=seen[:, :], in_=seen[:, :], compare_op=ALU.is_ge, fill=0.0,
                                         base=-(CMP_LEN - 1), pattern=[[0, 1]], channel_multiplier=1))
            nc.gpsimd.memset(bias_p[:, :], NEG).then_inc(consts, 1)

            for s, a in enumerate([0, 1, 0, 1, 1, 0]):
                if s in (2, 3):
                    pool.wait_ge(pe_mod, s - 1)
                if s == 4:
                    pool.wait_ge(pe_mod, 4)
                if s == 5:
                    pool.wait_ge(evac_dve, 4)
                nc.gpsimd.memset(acc[a][:, :], 0.0).then_inc(acc_zero, 1)
                pool.wait_ge(acc_zero, s + 1)
                pool.dma_start(acc[a][0:1, :], bmod_d[s:s + 1, :]).then_inc(acc_init[s], 16)

        @block.scalar
        def _(act):
            A = nc.scalar.activation

            loads = [(c_col[:, :], c_d), (n1[:, :], n1_d), (n2[:, :], n2_d),
                     (rel_t[:, :], rel_d), (onehot[:, :], onehot_d),
                     (bf_b[:, :], bf_d.to_broadcast([P, NFOX])), (convw[:, :, :], convw_d),
                     (convb[:, :], convb_d), (lng[:, :], lng_d), (lnb[:, :], lnb_d),
                     (pos_t[0:HD, :], pos_d), (pos_t[HD:P, :], pos_d)]
            for dst, src in loads:
                act.dma_start(dst, src).then_inc(small_in, 16)
            assert len(loads) == N_SMALL
            act.wait_ge(small_in, 16 * N_SMALL)
            A(c_tmp[:, :], c_col[:, :], ACT.Sigmoid).then_inc(c_sig, 1)

            act.wait_ge(x_in, 16 * TT)
            for tt in range(TT):
                if tt:
                    act.wait_ge(act_sq, tt)
                A(sq_a[:, :], x_a[:, tt, :], ACT.Square, accum_out=ssq[:, tt:tt + 1]).then_inc(act_sq, 1)
            act.wait_ge(dve_ms, 1)
            A(root[:, :], mean_sq[:, :], ACT.Sqrt).then_inc(act_root, 1)
            act.wait_ge(rstd_ok, 1)
            for tt in range(TT):
                A(x_a[:, tt, :], x_a[:, tt, :], ACT.Copy, scale=rstd[:, tt:tt + 1]).then_inc(xn_ok, 1)
            act.wait_ge(bias_ps, 1)
            act.wait_ge(consts, 1)
            A(bias_p[:, P - 1:P - 1 + S], aux[3][0:NNSA, 0:S], ACT.Copy).then_inc(bias_row, 1)
            act.wait_ge(bias_row, 1)
            act.dma_start(bias_scratch[:, :], bias_p[:, :]).then_inc(bias_out, 16)
            for b in range(KT // 2):
                act.wait_ge(xt_ps, b + 1)
                A(xn_t[:, 2 * b:2 * b + 2, :], aux[b % 2][:, :].rearrange("p (k t) -> p k t", k=2),
                  ACT.Copy).then_inc(xt_ok, 1)
            act.wait_ge(col_ok, 2)
            for b in range(KT // 2):
                if b >= 2:
                    act.wait_ge(h_ready, b - 1)
                for k in (2 * b, 2 * b + 1):
                    A(h_f[b % 2][:, (k % 2) * S:(k % 2 + 1) * S], xn_t[:, k, :], ACT.Identity,
                      bias=shift_h[:, k:k + 1], scale=scale_h[:, k:k + 1]).then_inc(h_ok, 1)

            def weight_hi(g, j, width=GW, first=False):
                act.wait_ge(raw_full[j // 2], (g + 1) * 16)
                if not (first and j < 4):
                    act.wait_ge(pe_half, g * 8 + j - 3)
                A(w_hi[j % 4][:, 0:2 * width], block_half(raw, j, width), ACT.Copy).then_inc(hi_done, 1)

            def evacuate(g):
                act.wait_ge(pe_half, 8 * (g + 1))
                if g == 0:
                    A(conv_in[:, :, CONV_W - 1:], pair[0][:, :].rearrange("p (k t) -> p k t", k=CT),
                      ACT.Copy).then_inc(evac_act, 1)
                elif g == 1:
                    A(conv_y[:, :, :], pair[1][:, :].rearrange("p (k t) -> p k t", k=CT),
                      ACT.Sigmoid).then_inc(evac_act, 1)
                elif g < 8:
                    A(z_t[:, 4 * (g - 2):4 * (g - 1), :], pair[g % 2][:, :].rearrange("p (k t) -> p k t", k=4),
                      ACT.Copy, scale=HD ** -0.5 if g < 5 else 1.0).then_inc(evac_act, 1)
                else:
                    at, width = {8: (2 * GW, TAIL), 9: (0, GW), 10: (GW, GW)}[g]
                    A(val[:, :, at:at + width],
                      pair[g % 2][:, :].rearrange("p (t n) -> p t n", t=TT)[:, :, 0:width],
                      ACT.Copy).then_inc(evac_act, 1)

            act.wait_ge(bias_out, 16)
            for g in range(N_IN):
                for j in range(HALVES):
                    if j == 4 and g:
                        evacuate(g - 1)
                    weight_hi(g, j, TAIL if g == 8 else GW, first=g == 0)
                    if g == 9 and j == 5:
                        act.wait_ge(evac_act, 9)
                        A(gate[:, :, :], val[:, :, COL_G:COL_G + 3 * NNSA], ACT.Sigmoid)\
                            .then_inc(gate_ok, 1)
                        act.wait_ge(lf_in, 1)
                        A(lf[1][:, :, :], lf[1][:, :, :], ACT.Exp, scale=-1.0).then_inc(lf_exp, 1)
            evacuate(N_IN - 1)
            act.wait_ge(pe_half, 8 * N_IN)
            act.wait_ge(bias_out, 16)
            diag = bass.AP(bias_scratch.tensor, bias_scratch.offset, [[1, P], [BPAD, NNSA], [1, S]])
            act.dma_start(bias_t[:, :, :], diag).then_inc(bias_in, 16)
            for h in range(2):
                act.dma_start(wck[h * HD:(h + 1) * HD, :, :], wck_d[h, :, :, :]).then_inc(cmp_w_in, 16)
                act.dma_start(wcv[h * HD:(h + 1) * HD, :, :], wcv_d[h, :, :, :]).then_inc(cmp_w_in, 16)
            act.wait_ge(evac_act, 8)
            A(k_swap[HD:P, :, :], z_t[0:HD, 21:24, :], ACT.Copy).then_inc(swap_ok, 1)
            A(k_swap[0:HD, :, :], z_t[HD:P, 21:24, :], ACT.Copy).then_inc(swap_ok, 1)
            for cg in range(4):
                act.wait_ge(pe_mod, 3)
                A(acc[0][:, cg * GW:(cg + 1) * GW], pair[cg // 2][:, (cg % 2) * GW:(cg % 2 + 1) * GW],
                  ACT.Copy).then_inc(gate_row, 1)

            def conv_norm(part):
                if part == 0:
                    act.wait_ge(ln_var, 1)
                    A(root_b, var_b, ACT.Sqrt).then_inc(ln_root, 1)
                else:
                    act.wait_ge(ln_y, 1)
                    A(conv_in[:, :, 0:S], conv_y[:, :, :], ACT.Sigmoid).then_inc(ln_sig, 1)

            def attend(a):
                if a < 36:
                    sign = 1.0 if a < NFOX else -1.0
                    act.wait_ge(s_biased, a + 1)
                    A(score[a % 3][:, 0:P], score[a % 3][:, 0:P], ACT.Exp, scale=sign,
                      bias=neg_max[:, 2 * a:2 * a + 1], accum_out=row_sum[:, 2 * a:2 * a + 1])
                    A(score[a % 3][:, P:3 * P], score[a % 3][:, P:3 * P], ACT.Exp, scale=sign,
                      bias=neg_max[:, 2 * a + 1:2 * a + 2], accum_out=row_sum[:, 2 * a + 1:2 * a + 2])\
                        .then_inc(p_ready, 1)
                b = a - 2
                if 0 <= b < 36 and b % 2 == 0:
                    act.wait_ge(t_ready, b + 1)
                    if b >= 2:
                        act.wait_ge(o_ready, b - 1)
                    A(prob_t[0][:, :], t_bank[0][:, 0:3 * P], ACT.Copy).then_inc(t_act, 1)

            for a in range(36 + 2):
                attend(a)
                if a == 4:
                    conv_norm(0)
                if a == 8:
                    conv_norm(1)
                if a == 26:
                    act.wait_ge(cmp_x, 2)
                    A(p_cmp[:, :, :, 0:16], s_cmp[:, :, :, :], ACT.Exp).then_inc(cmp_exp, 1)

            for b in range(8):
                if b < 6:
                    act.wait_ge(mt_ps, b + 1)
                    A(act_hi[:, 2 * b:2 * b + 2, :], aux[b % 2][:, :].rearrange("p (k t) -> p k t", k=2),
                      ACT.Copy).then_inc(mt_hi, 1)
                else:
                    if b == 6:
                        act.wait_ge(mt_ps, 6)
                    A(act_hi[:, 2 * b:2 * b + 2, :], conv_y[:, 2 * (b - 6):2 * (b - 6) + 2, :],
                      ACT.Copy).then_inc(mt_hi, 1)

            for i in range(4):
                for j in range(HALVES):
                    weight_hi(G_OUT + i, j)

            for tt in range(TT):
                act.wait_ge(x2_sum, 4)
                A(xn2[:, tt, :], x2[:, tt, :], ACT.Square, accum_out=ssq[:, TT + tt:TT + tt + 1]).then_inc(act_sq, 1)
            act.wait_ge(dve_ms, 2)
            A(root[:, :], mean_sq[:, :], ACT.Sqrt).then_inc(act_root, 1)
            act.wait_ge(act_sq, 2 * TT)
            act.wait_ge(rstd_ok, 2)
            for tt in range(TT):
                A(xn2[:, tt, :], x2[:, tt, :], ACT.Copy, scale=rstd[:, tt:tt + 1]).then_inc(xn_ok, 1)
            act.wait_ge(col_ok, 4)
            for b in range(KT // 2):
                act.wait_ge(xt_ps, KT // 2 + b + 1)
                if b >= 2:
                    act.wait_ge(h2_ready, b - 1)
                for k in (2 * b, 2 * b + 1):
                    A(h2_f[b % 2][:, (k % 2) * S:(k % 2 + 1) * S], aux[b % 2][:, (k % 2) * S:(k % 2 + 1) * S],
                      ACT.Identity, bias=shift2[:, k:k + 1], scale=scale_h[:, k:k + 1]).then_inc(h_ok, 1)

            def mlp_quarter(q):
                for i in range(8):
                    g = q * 8 + (G_MLP + i)
                    for j in range(HALVES):
                        if j == 4 and 1 <= i <= 4:
                            act.wait_ge(pe_half, g * 8)
                            if not (isinstance(q, int) and i == 1):
                                act.wait_ge(u_ready, q * 4 + (i - 1))
                            A(relu[:, :], pair[i % 2][:, :], ACT.Relu).then_inc(evac_act, 1)
                        if j == 4 and isinstance(q, int) and i == 5:
                            act.wait_ge(pe_mod, 6)
                            for cg in range(4):
                                A(acc[0][:, cg * GW:(cg + 1) * GW], aux[cg][:, :], ACT.Copy)\
                                    .then_inc(gate_row, 1)
                        weight_hi(g, j)

            mlp_quarter(0)
            with act.Fori(1, QUARTERS) as q:
                mlp_quarter(q)

            act.wait_ge(x2_sum, 4 * (QUARTERS + 1))
            for tt in range(TT):
                A(mod_raw[tt][:, :], x2[:, tt, :], ACT.Square, accum_out=ssq[:, 2 * TT + tt:2 * TT + tt + 1]).then_inc(act_sq, 1)
            act.wait_ge(dve_ms, 3)
            A(root[:, :], mean_sq[:, :], ACT.Sqrt).then_inc(act_root, 1)

        @block.tensor
        def _(pe):
            mm = nc.tensor.matmul

            def transposed_group(g, par, ready, reach):
                for j in range(HALVES):
                    if ready is not None:
                        pe.wait_ge(ready, reach(j))
                    pe.wait_ge(lo_done, g * 8 + (j + 1))
                    for kk in range(2):
                        k = 2 * j + kk
                        for m in range(4):
                            out = pair[par][:, m * S:(m + 1) * S]
                            cols = slice(kk * GW + m * P, kk * GW + (m + 1) * P)
                            hi, lo = w_hi[j % 4][:, cols], w_lo[j % 4][:, cols]
                            mm(out, hi, act_hi[:, k, :], start=k == 0 and m % 2 == 0, stop=False,
                               skip_group_check=True)
                            mm(out, hi, act_lo[:, k, :], start=False, stop=False, skip_group_check=True)
                            last = mm(out, lo, act_hi[:, k, :], start=False, stop=k == KT - 1,
                                      skip_group_check=True)
                    last.then_inc(pe_half, 1)

            def straight_group(g, par, a_hi, a_lo, ready, reach, width=GW):
                for j in range(HALVES):
                    if ready is not None:
                        pe.wait_ge(ready, reach(j))
                    pe.wait_ge(lo_done, g * 8 + (j + 1))
                    for kk in range(2):
                        k = 2 * j + kk
                        for tt in range(TT):
                            out = pair[par][:, tt * GW:tt * GW + width]
                            cols = slice(kk * width, (kk + 1) * width)
                            hi, lo = w_hi[j % 4][:, cols], w_lo[j % 4][:, cols]
                            t_hi, t_lo = a_hi[:, k, tt * P:(tt + 1) * P], a_lo[:, k, tt * P:(tt + 1) * P]
                            mm(out, t_hi, hi, start=k == 0, stop=False)
                            mm(out, t_hi, lo, start=False, stop=False)
                            last = mm(out, t_lo, hi, start=False, stop=k == KT - 1)
                    last.then_inc(pe_half, 1)

            def columns(a, bank, at):
                for k in range(KT):
                    last = mm(bank[:, at + k:at + k + 1], acc[a][:, k * P:(k + 1) * P], ones[:, 0:1],
                              start=True, stop=True)
                last.then_inc(pe_mod, 1)

            def rows(a, banks):
                for cg in range(4):
                    last = mm(banks[cg], ones[:, :], acc[a][:, cg * GW:(cg + 1) * GW], start=True, stop=True)
                last.then_inc(pe_mod, 1)

            pe.wait_ge(small_in, 16 * N_SMALL)
            mm(aux[3][0:NNSA, 0:S], rel_t[:, :], onehot[:, :], start=True, stop=True).then_inc(bias_ps, 1)
            pe.wait_ge(consts, 1)
            pe.wait_ge(xn_ok, TT)
            for b in range(KT // 2):
                if b >= 2:
                    pe.wait_ge(xt_ok, b - 1)
                for kk in range(2):
                    for tt in range(TT):
                        k = 2 * b + kk
                        last = nc.tensor.transpose(aux[b % 2][:, kk * S + tt * P:kk * S + (tt + 1) * P],
                                                   x_a[:, tt, k * P:(k + 1) * P], ident[:, :])
                last.then_inc(xt_ps, 1)
            pe.wait_ge(mod_step, 4 * 16 + 1)
            columns(0, aux[2], 0)
            pe.wait_ge(mod_step, 4 * 32 + 1)
            pe.wait_ge(col_ok, 1)
            columns(1, aux[2], KT)

            transposed_group(0, 0, h_ready, lambda j: j + 1)
            transposed_group(1, 1, None, None)
            with pe.Fori(1, 4) as i:
                for par in range(2):
                    pe.wait_ge(evac_act, i * 2 + (par - 1))
                    transposed_group(i * 2 + par, par, None, None)
            for g in range(8, N_IN):
                pe.wait_ge(evac_act, g - 1)
                straight_group(g, g % 2, act_hi, act_lo, None, None, TAIL if g == 8 else GW)

            pe.wait_ge(lf_ok, 1)
            mm(aux[0][:, 0:NFOX], tri[:, :], log_f[:, 0, :], start=True, stop=True)
            mm(aux[0][:, NFOX:2 * NFOX], ones[:, :], log_f[:, 0, :], start=True, stop=False)
            mm(aux[0][:, NFOX:2 * NFOX], tri[:, :], log_f[:, 1, :], start=False, stop=True)
            for n, base in enumerate((0, HD)):
                out = aux[1 + n][base:base + NFOX, 0:S]
                mm(out[:, 0:P], log_f[:, 0, :], tri[:, :], start=True, stop=True)
                mm(out[:, P:S], log_f[:, 0, :], ones[:, :], start=True, stop=False)
                last = mm(out[:, P:S], log_f[:, 1, :], tri[:, :], start=False, stop=True)
            last.then_inc(f_ps, 1)
            pe.wait_ge(conv_sem, CONV_STEPS)
            for ct in range(CT):
                last = mm(aux[3][:, 0:S], ones_conv[:, :], conv_y[:, ct, :], start=ct == 0, stop=ct == CT - 1)
            last.then_inc(ln_ps, 1)
            pe.wait_ge(evac_act, N_IN)
            rows(0, [pair[cg // 2][:, (cg % 2) * GW:(cg % 2 + 1) * GW] for cg in range(4)])
            pe.wait_ge(f_sb, 2)
            columns(1, aux[2], 0)

            def key_of(a, base):
                if a < NFOX:
                    return z_t[base:base + HD, 12 + a // 2, :]
                n = (a - NFOX) // NNSA * NKV + (a - NFOX) % NNSA // 4
                if n % 2 == a % 2:
                    return z_t[base:base + HD, 21 + n // 2, :]
                return k_swap[base:base + HD, n // 2, :]

            def scores(a):
                base = HD * (a % 2)
                out = aux[a % 3]
                query = z_t[base:base + HD, a // 2 if a < NFOX else 6 + (a - NFOX) % NNSA // 2, :]
                key = key_of(a, base)
                if a == 0:
                    pe.wait_ge(evac_act, 8)
                if a == 2:
                    pe.wait_ge(col_ok, 3)
                if a >= 3:
                    pe.wait_ge(s_biased, a - 2)
                if a == NFOX:
                    pe.wait_ge(swap_ok, 2)
                if a == 24:
                    pe.wait_ge(cmp_sb, 4)
                for tt, (at, n) in enumerate(((0, P), (P, S))):
                    last = mm(out[:, at:at + n], query[:, tt * P:(tt + 1) * P], key[:, 0:n], start=True,
                              stop=a >= NFOX)
                    if a < NFOX:
                        last = mm(out[:, at:at + n], neg_id[base:base + NFOX, a:a + 1].to_broadcast([NFOX, P]),
                                  f_t[base:base + NFOX, 0:n], start=False, stop=True)
                last.then_inc(s_ready, 1)

            def transposes(a):
                pe.wait_ge(p_ready, a + 1)
                if a == 0:
                    pe.wait_ge(gate_row, 4)
                if a >= 2:
                    pe.wait_ge(t_dve if a % 2 else t_act, a // 2)
                for n in range(3):
                    last = nc.tensor.transpose(t_bank[a % 2][:, n * P:(n + 1) * P],
                                               score[a % 3][:, n * P:(n + 1) * P], ident[:, :])
                last.then_inc(t_ready, 1)

            def outputs(a):
                pe.wait_ge(t_dve if a % 2 else t_act, a // 2 + 1)
                unit, r = a // 4, a % 4
                if r == 0 and unit >= 2:
                    pe.wait_ge(o_used, unit - 1)
                at = a * HD if a < NFOX else NFOX * HD + ((a - NFOX) // NNSA * NKV + (a - NFOX) % NNSA // 4) * HD
                out = [o_bank[unit % 2][:, (tt * 4 + r) * HD:(tt * 4 + r + 1) * HD] for tt in range(TT)]
                pt = prob_t[a % 2]
                mm(out[0], pt[:, 0:P], val[:, 0, at:at + HD], start=True, stop=True)
                mm(out[1], pt[:, P:2 * P], val[:, 0, at:at + HD], start=True, stop=False)
                mm(out[1], pt[:, 2 * P:3 * P], val[:, 1, at:at + HD], start=False, stop=True).then_inc(o_ready, 1)

            for a in range(36 + 3):
                if a == 4:
                    pe.wait_ge(ln_sq, 1)
                    for ct in range(CT):
                        last = mm(aux[3][:, S:2 * S], ones_conv[:, :], conv_in[:, ct, 0:S], start=ct == 0,
                                  stop=ct == CT - 1)
                    last.then_inc(ln_ps, 1)
                if a == 14:
                    pe.wait_ge(ln_var, 1)
                    pe.wait_ge(cmp_x, 1)
                    pe.wait_ge(cmp_w_in, 4 * 16)
                    for n, w in enumerate((wck, wcv)):
                        for l in range(CMP_STRIDE):
                            tokens = view(cmp_in[:, 3 * n:3 * n + 3, :],
                                          [[S, NKV], [CMP_STRIDE, NCMP]], l)
                            last = mm(aux[3][0:HD, HD * n:HD * n + NKV * NCMP], w[:, l, :], tokens,
                                      start=l == 0, stop=l == CMP_STRIDE - 1)
                    last.then_inc(cmp_ps, 1)
                if a == 18:
                    pe.wait_ge(cmp_sb, 2)
                    for g in range(NKV):
                        last = nc.tensor.transpose(aux[3][:, P + g * HD:P + (g + 1) * HD], v_cmp_t[:, g, :],
                                                   ident[0:HD, 0:HD])
                    last.then_inc(cmp_ps, 1)
                if a == 24:
                    pe.wait_ge(cmp_sb, 3)
                    pe.wait_ge(s_biased, 22)
                    for odd in range(2):
                        for tt, count in enumerate((NCMP0, NCMP)):
                            for h in range(odd, NNSA, 2):
                                at = (tt * NNSA + h) * 16
                                last = mm((aux[0] if odd else aux[3])[:, at:at + count],
                                          z_t[HD * odd:HD * odd + HD, 6 + h // 2, tt * P:(tt + 1) * P],
                                          k_cmp[HD * odd:HD * odd + HD, h // 4, 0:count], start=True, stop=True)
                    last.then_inc(cmp_ps, 1)
                if a in (30, 34):
                    tt = (a - 30) // 4
                    pe.wait_ge(cmp_exp, 1)
                    if tt:
                        pe.wait_ge(cmp_sb, 5)
                    for g in range(NKV):
                        last = nc.tensor.transpose(
                            aux[3][:, g * P:(g + 1) * P],
                            p_cmp[:, tt, 4 * g:4 * g + 4, :].rearrange("p h n -> p (h n)"), ident[:, :])
                    last.then_inc(cmp_ps, 1)
                if a < 36:
                    scores(a)
                if 0 <= a - 2 < 36:
                    transposes(a - 2)
                if a >= 3:
                    outputs(a - 3)
            pe.wait_ge(cmp_sb, 6)
            pe.wait_ge(s_biased, 36)
            for r in range(4):
                rows_r = slice(32 * r, 32 * r + 32)
                for tt in range(TT):
                    for g in range(NKV):
                        at = (tt * NKV + g) * HD
                        last = mm(aux[r][:, at:at + HD], p_cmp_t[rows_r, :, :].rearrange("p a b -> p (a b)")
                                  [:, (tt * NKV + g) * P:(tt * NKV + g + 1) * P],
                                  v_cmp[rows_r, g, :], start=True, stop=True, tile_position=(32 * r, 0))
            last.then_inc(cmp_ps, 1)
            pe.wait_ge(mix_done, 4)
            for b in range(6):
                if b >= 2:
                    pe.wait_ge(mix_ready, b - 1)
                for kk in range(2):
                    for tt in range(TT):
                        k = 2 * b + kk
                        last = nc.tensor.transpose(aux[b % 2][:, kk * S + tt * P:kk * S + (tt + 1) * P],
                                                   mix[:, tt, k * P:(k + 1) * P], ident[:, :])
                last.then_inc(mt_ps, 1)

            for i in range(4):
                if i >= 2:
                    pe.wait_ge(evac_dve, i - 1)
                straight_group(G_OUT + i, (1 + i) % 2, act_hi, act_lo, mix_ready, lambda j: j + 1)
            pe.wait_ge(mod_step, 4 * 80 + 1)
            columns(1, aux[2], KT)
            pe.wait_ge(xn_ok, 2 * TT)
            for b in range(KT // 2):
                if b >= 2:
                    pe.wait_ge(h_ok, 2 * (KT // 2 + b - 1))
                for kk in range(2):
                    for tt in range(TT):
                        k = 2 * b + kk
                        last = nc.tensor.transpose(aux[b % 2][:, kk * S + tt * P:kk * S + (tt + 1) * P],
                                                   xn2[:, tt, k * P:(k + 1) * P], ident[:, :])
                last.then_inc(xt_ps, 1)

            def mlp_up(q):
                with pe.Fori(0, 2) as i:
                    for par in range(2):
                        pe.wait_ge(evac_dve, q * 4 + (3 + par))
                        pe.wait_ge(evac_act, q * 4 + i * 2 + (N_IN - 1 + par))
                        transposed_group(q * 8 + i * 2 + (G_MLP + par), (1 + par) % 2, h2_ready, lambda j: j + 1)

            def mlp_down(q, i, par):
                pe.wait_ge(evac_act, q * 4 + (N_IN + 3 + par))
                pe.wait_ge(evac_dve, q * 4 + i + 3)
                straight_group(q * 8 + i + (G_MLP + 4), (1 + par) % 2, u_hi, u_lo, u_ready,
                               lambda j: q * 4 + (j // 2 + 1))

            mlp_up(0)
            for i in range(4):
                mlp_down(0, i, i % 2)
                if i == 0:
                    pe.wait_ge(mod_step, 4 * 96 + 1)
                    rows(0, [aux[cg][:, :] for cg in range(4)])
            with pe.Fori(1, QUARTERS) as q:
                mlp_up(q)
                with pe.Fori(0, 2) as i:
                    for par in range(2):
                        mlp_down(q, i * 2 + par, par)

        @block.vector
        def _(dve):
            v = nc.vector
            TS, TTn, STT = v.tensor_scalar, v.tensor_tensor, v.scalar_tensor_tensor
            chain = [0]

            def link(ins):
                ins.then_inc(dve_c, 1)
                chain[0] += 1
                dve.wait_ge(dve_c, chain[0])

            def weight_lo(g, j, width=GW):
                dve.wait_ge(hi_done, g * 8 + (j + 1))
                TTn(w_lo[j % 4][:, 0:2 * width], block_half(raw, j, width),
                    w_hi[j % 4][:, 0:2 * width].bitcast(f32), ALU.subtract).then_inc(lo_done, 1)

            def modulation(m, r, a, cg, section=None):
                dve.wait_ge(mod_full[r % 2], mod_arrivals(m, r))
                if section is not None:
                    dve.wait_ge(acc_init[section], 16)
                out = acc[a][:, bass.ds(cg * GW, GW)]
                for kk in range(4):
                    dve.wait_ge(mod_step, m * 4 + (kk + 1))
                    STT(out, mod_raw[r % 2][:, kk * GW:(kk + 1) * GW], c_act[:, 4 * r + kk:4 * r + kk + 1], out,
                        ALU.mult, ALU.add).then_inc(mod_step, 1)

            def mod_arrivals(m, r):
                return (m - r) * 8 + 16 * (r // 2 + 1)

            def inverse_rms(n):
                dve.wait_ge(act_sq, TT * (n + 1))
                TS(mean_sq[:, :], ssq[:, TT * n:TT * (n + 1)], 1.0 / D, EPS, ALU.mult, ALU.add).then_inc(dve_ms, 1)
                dve.wait_ge(act_root, n + 1)
                link(v.reciprocal(rstd[:, :], root[:, :]))
                link(TTn(newton[:, :], rstd[:, :], rstd[:, :], ALU.mult))
                link(TTn(newton[:, :], newton[:, :], mean_sq[:, :], ALU.mult))
                link(TS(newton[:, :], newton[:, :], -0.5, 1.5, ALU.mult, ALU.add))
                TTn(rstd[:, :], rstd[:, :], newton[:, :], ALU.mult).then_inc(rstd_ok, 1)

            dve.wait_ge(c_sig, 1)
            TTn(c_act[:, :], c_tmp[:, :], c_col[:, :], ALU.mult).then_inc(mod_step, 1)

            with dve.Fori(0, 4) as cg:
                for r in range(4):
                    modulation(cg * 4 + r, r, 0, cg, 0)
            inverse_rms(0)
            with dve.Fori(4, 8) as cg:
                for r in range(4):
                    modulation(cg * 4 + r, r, 1, cg - 4, 1)
            dve.wait_ge(pe_mod, 1)
            v.tensor_copy(shift_h[:, :], aux[2][:, 0:KT]).then_inc(col_ok, 1)
            dve.wait_ge(pe_mod, 2)
            STT(scale_h[:, :], aux[2][:, KT:2 * KT], 1.0, n1[:, :], ALU.add, ALU.mult).then_inc(col_ok, 1)

            def split_h(n, source, ready):
                for b in range(KT // 2):
                    dve.wait_ge(h_ok, KT * n + 2 * b + 2)
                    src = source[b % 2][:, :].rearrange("p (k t) -> p k t", k=2)
                    v.tensor_copy(act_hi[:, 2 * b:2 * b + 2, :], src).then_inc(h_hi, 1)
                    dve.wait_ge(h_hi, KT // 2 * n + b + 1)
                    TTn(act_lo[:, 2 * b:2 * b + 2, :], src, act_hi[:, 2 * b:2 * b + 2, :].bitcast(f32),
                        ALU.subtract).then_inc(ready, 1)

            def taps():
                dve.wait_ge(evac_act, 2)
                link(TTn(conv_in[:, :, CONV_W - 1:], conv_in[:, :, CONV_W - 1:], conv_y[:, :, :], ALU.mult))
                yield
                for n in range(CONV_STEPS):
                    t, ct = divmod(n, CT)
                    x_t = conv_in[:, ct, t:t + S]
                    if t == 0:
                        TS(conv_y[:, ct, :], x_t, convw[:, ct, 0:1], convb[:, ct:ct + 1], ALU.mult, ALU.add)\
                            .then_inc(conv_sem, 1)
                    else:
                        dve.wait_ge(conv_sem, n - CT + 1)
                        STT(conv_y[:, ct, :], x_t, convw[:, ct, t:t + 1], conv_y[:, ct, :], ALU.mult, ALU.add)\
                            .then_inc(conv_sem, 1)
                    yield

            split_h(0, h_f, h_ready)
            dve.wait_ge(bias_out, 16)
            dve.wait_ge(h_ready, KT // 2)
            link(v.memset(conv_in[:, :, 0:CONV_W - 1], 0.0))
            conv = taps()

            for g in range(N_IN):
                for j in range(HALVES):
                    if g == 2 and j == 5:
                        next(conv)
                    if (g == 2 and j > 5) or g > 2:
                        for _ in range(3):
                            next(conv, None)
                    weight_lo(g, j, TAIL if g == 8 else GW)
                    if g < 8 and j % 2:
                        section = 2 + g // 4
                        modulation(32 + 4 * g + j // 2, j // 2, section - 2, g % 4,
                                   section if g % 4 == 0 and j == 1 else None)
                    if g == 9 and j == 4:
                        dve.wait_ge(evac_act, 9)
                        link(TTn(lf[0][:, :, :], val[:, :, COL_F:COL_F + NFOX],
                                 view(bf_b[:, :], [[0, TT], [1, NFOX]]), ALU.add))
                        STT(lf[1][:, :, :], lf[0][:, :, :], -1.0, lf[0][:, :, :], ALU.mult, ALU.max)\
                            .then_inc(lf_in, 1)
                    if g == 10 and j == 1:
                        e, r, r2, s = (lf[i][:, :, :] for i in (1, 2, 3, 4))
                        dve.wait_ge(lf_exp, 1)
                        link(TS(r, e, 2.0, None, ALU.add))
                        link(v.reciprocal(r, r))
                        link(TTn(r, r, e, ALU.mult))
                        link(TTn(r2, r, r, ALU.mult))
                        link(TS(s, r2, 1.0 / 15, None, ALU.mult))
                        for odd in (13, 11, 9, 7, 5, 3):
                            link(STT(s, s, 1.0 / odd, r2, ALU.add, ALU.mult))
                        link(STT(s, s, 1.0, r, ALU.add, ALU.mult))
                        link(TS(lf[0][:, :, :], lf[0][:, :, :], 0.0, None, ALU.min))
                        STT(log_f[:, :, :], s, -2.0, lf[0][:, :, :], ALU.mult, ALU.add).then_inc(lf_ok, 1)
                    if g == 10 and j == 3:
                        dve.wait_ge(gate_ok, 1)

            dve.wait_ge(f_ps, 1)
            v.tensor_copy(f_q[:, :, :], aux[0][:, 0:2 * NFOX].rearrange("p (t h) -> p t h", t=TT)).then_inc(f_sb, 1)
            v.tensor_copy(f_t[0:NFOX, :], aux[1][0:NFOX, 0:S])
            v.tensor_copy(f_t[HD:HD + NFOX, :], aux[2][HD:HD + NFOX, 0:S]).then_inc(f_sb, 1)
            dve.wait_ge(f_sb, 2)
            dve.wait_ge(ln_ps, 1)
            link(TTn(conv_y[:, :, :], conv_y[:, :, :], view(aux[3][:, 0:S], [[0, CT], [1, S]]), ALU.subtract))
            TTn(conv_in[:, :, 0:S], conv_y[:, :, :], conv_y[:, :, :], ALU.mult).then_inc(ln_sq, 1)
            dve.wait_ge(pe_mod, 4)
            v.tensor_copy(shift2[:, :], aux[2][:, 0:KT]).then_inc(col_ok, 1)

            def bias_of(h, tt):
                n = (tt + 1) * P
                return view(bias_t[:, h, :], [[-1, n]], n - 1)

            def cmp_bias(parity, tt, count):
                at = S - 1 - (CMP_LEN - 1) if tt else P - 1 - (CMP_LEN - 1)
                return view(bias_t[:, parity, :], [[2 * S, NNSA // 2], [-CMP_STRIDE, count]], at)

            def compress_inputs():
                dve.wait_ge(evac_act, 8)
                for n, (dst, tokens, blocks) in enumerate(((0, 0, 16), (1, 16, 15))):
                    for odd in range(2):
                        src = z_t[odd * HD:(odd + 1) * HD, 18:21, :]
                        pos = view(pos_t[odd * HD:(odd + 1) * HD, :], [[0, 3], [0, blocks], [1, 16]], 16 * dst)
                        out = view(cmp_in[dst * HD:(dst + 1) * HD, odd:odd + 1, :],
                                   [[2 * S, 3], [16, blocks], [1, 16]])
                        last = TTn(out, view(src, [[S, 3], [16, blocks], [1, 16]], tokens), pos, ALU.add)
                last.then_inc(cmp_x, 1)

            def outputs(unit):
                a = 4 * unit
                dve.wait_ge(o_ready, a + 4)
                link(v.reciprocal(row_r[:, 2 * a:2 * a + 8], row_sum[:, 2 * a:2 * a + 8]))
                if a >= NFOX:
                    h = (a - NFOX) % NNSA
                    branch = 1 + (a - NFOX) // NNSA
                    g = view(gate[:, :, :], [[3, 4], [3 * NNSA, TT]], 3 * h + branch)
                    r = view(row_r[:, :], [[2, 4], [1, TT]], 2 * a)
                    link(TTn(r, r, g, ALU.mult))
                    at = NFOX * HD + h * HD
                else:
                    at = a * HD
                r = view(row_r[:, :], [[1, TT], [2, 4], [0, HD]], 2 * a)
                out = view(mix[:, :, :], [[(NFOX + NNSA) * HD, TT], [HD, 4], [1, HD]], at)
                bank = view(o_bank[unit % 2], [[4 * HD, TT], [HD, 4], [1, HD]])
                if a < 24:
                    TTn(out, bank, r, ALU.mult).then_inc(o_used, 1)
                else:
                    t = view(add_t[:, :], [[4 * HD, TT], [HD, 4], [1, HD]])
                    TTn(t, bank, r, ALU.mult).then_inc(o_used, 1)
                    dve.wait_ge(o_used, unit + 1)
                    link(TTn(out, out, t, ALU.add))

            for a in range(36 + 5):
                if a < 36:
                    sc, ps = score[a % 3], aux[a % 3]
                    dve.wait_ge(s_ready, a + 1)
                    if a >= 3:
                        dve.wait_ge(t_ready, a - 2)
                    if a < NFOX:
                        for tt, (at, n) in enumerate(((0, P), (P, S))):
                            link(STT(sc[:, at:at + n], ps[:, at:at + n], f_q[:, tt, a:a + 1], causal[:, S - n:S],
                                     ALU.add, ALU.add))
                            last = v.tensor_reduce(neg_max[:, 2 * a + tt:2 * a + tt + 1], sc[:, at:at + n],
                                                   AX.X, ALU.max, negate=True)
                    else:
                        if a == NFOX:
                            dve.wait_ge(bias_in, 16)
                        h = (a - NFOX) % NNSA
                        for tt, (at, n) in enumerate(((0, P), (P, S))):
                            last = v.tensor_tensor_reduce(
                                out=sc[:, at:at + n], in0=ps[:, at:at + n], in1=bias_of(h, tt), scale=-1.0,
                                scalar=3e38, op0=ALU.add, op1=ALU.min,
                                accum_out=neg_max[:, 2 * a + tt:2 * a + tt + 1])
                    last.then_inc(s_biased, 1)
                b = a - 2
                if 0 <= b < 36 and b % 2:
                    dve.wait_ge(t_ready, b + 1)
                    if b >= 3:
                        dve.wait_ge(o_ready, b - 1)
                    v.tensor_copy(prob_t[1][:, :], t_bank[1][:, 0:3 * P]).then_inc(t_dve, 1)
                if a >= 5 and (a - 5) % 4 == 3:
                    outputs((a - 5) // 4)
                if a == 2:
                    dve.wait_ge(pe_half, 8 * N_IN)
                    compress_inputs()
                if a == 6:
                    dve.wait_ge(ln_ps, 2)
                    TS(var_b, aux[3][:, S:2 * S], EPS, None, ALU.add).then_inc(ln_var, 1)
                if a == 7:
                    dve.wait_ge(ln_root, 1)
                    link(v.reciprocal(inv_b, root_b))
                    link(TTn(newton_b, inv_b, inv_b, ALU.mult))
                    link(TTn(newton_b, newton_b, var_b, ALU.mult))
                    link(TS(newton_b, newton_b, -0.5, 1.5, ALU.mult, ALU.add))
                    link(TTn(inv_b, inv_b, newton_b, ALU.mult))
                    link(TTn(conv_y[:, :, :], conv_y[:, :, :], view(conv_in[:, 2, 0:S], [[0, CT], [1, S]]),
                             ALU.mult))
                    for ct in range(CT):
                        last = TS(conv_y[:, ct, :], conv_y[:, ct, :], lng[:, ct:ct + 1], lnb[:, ct:ct + 1],
                                  ALU.mult, ALU.add)
                    last.then_inc(ln_y, 1)
                if a == 10:
                    dve.wait_ge(ln_sig, 1)
                    link(TTn(conv_y[:, :, :], conv_y[:, :, :], conv_in[:, :, 0:S], ALU.mult))
                if a == 15:
                    link(v.memset(v_cmp_t[:, :, :], 0.0))
                    link(v.memset(s_cmp[:, :, :, :], NEG))
                    link(v.memset(p_cmp[:, :, :, 16:32], 0.0))
                    dve.wait_ge(cmp_ps, 1)
                    kc = aux[3][0:HD, 0:NKV * NCMP].rearrange("p (g n) -> p g n", g=NKV)
                    v.tensor_copy(k_cmp[0:HD, :, :], kc)
                    v.tensor_copy(k_cmp[HD:P, :, :], kc).then_inc(cmp_sb, 1)
                    for g in range(NKV):
                        last = v.tensor_copy(view(v_cmp_t[:, g, :], [[32, 4], [1, NCMP]]),
                                             view(aux[3][0:HD, :], [[0, 4], [1, NCMP]], HD + g * NCMP))
                    last.then_inc(cmp_sb, 1)
                if a == 19:
                    dve.wait_ge(cmp_ps, 2)
                    v.tensor_copy(v_cmp[:, :, :], aux[3][:, P:P + NKV * HD].rearrange("p (g d) -> p g d", g=NKV))\
                        .then_inc(cmp_sb, 1)
                if a == 23:
                    dve.wait_ge(cmp_ps, 3)
                    for odd in range(2):
                        bank = aux[0] if odd else aux[3]
                        for tt, count in enumerate((NCMP0, NCMP)):
                            at = (tt * NNSA + odd) * 16
                            last = TTn(view(s_cmp[:, :, :, :], [[32, NNSA // 2], [1, count]], at),
                                       view(bank[:, :], [[32, NNSA // 2], [1, count]], at),
                                       cmp_bias(odd, tt, count), ALU.add)
                    last.then_inc(cmp_sb, 1)
                    dve.wait_ge(cmp_sb, 4)
                    flat = s_cmp[:, :, :, :].rearrange("p t h n -> p (t h) n")
                    link(v.tensor_reduce(cmp_m[:, :], flat, AX.X, ALU.max))
                    TTn(flat, flat, view(cmp_m[:, :], [[1, TT * NNSA], [0, 16]]), ALU.subtract).then_inc(cmp_x, 1)
                if a == 27:
                    dve.wait_ge(cmp_exp, 1)
                    probs = view(p_cmp[:, :, :, :], [[32, TT * NNSA], [1, 16]])
                    link(v.tensor_reduce(cmp_m[:, :], probs, AX.X, ALU.add))
                    link(v.reciprocal(cmp_r[:, :], cmp_m[:, :]))
                    r3 = cmp_r[:, :].rearrange("p (t h) -> p t h", t=TT)
                    link(TTn(r3, r3, view(gate[:, :, :], [[3 * NNSA, TT], [3, NNSA]]), ALU.mult))
                    link(TS(cmp_r[:, 0:NNSA], cmp_r[:, 0:NNSA], seen[:, 0:1], None, ALU.mult))
                if a in (31, 35):
                    tt = (a - 31) // 4
                    dve.wait_ge(cmp_ps, 4 + tt)
                    v.tensor_copy(view(p_cmp_t, [[1, NKV * P]], tt * NKV * P), aux[3][:, 0:NKV * P])\
                        .then_inc(cmp_sb, 1)
            dve.wait_ge(cmp_ps, 6)
            for r in range(4):
                gated = view(cmp_r[:, :], [[NNSA, TT], [4, NKV], [0, HD]], r)
                t = view(add_t[:, :], [[NKV * HD, TT], [HD, NKV], [1, HD]])
                out = view(mix[:, :, :], [[(NFOX + NNSA) * HD, TT], [4 * HD, NKV], [1, HD]],
                           NFOX * HD + r * HD)
                link(TTn(t, view(aux[r][:, :], [[NKV * HD, TT], [HD, NKV], [1, HD]]), gated, ALU.mult))
                TTn(out, out, t, ALU.add).then_inc(mix_done, 1)
                dve.wait_ge(mix_done, r + 1)
            for b in range(8):
                dve.wait_ge(mt_hi, b + 1)
                src = (aux[b % 2][:, :].rearrange("p (k t) -> p k t", k=2) if b < 6
                       else conv_y[:, 2 * (b - 6):2 * (b - 6) + 2, :])
                TTn(act_lo[:, 2 * b:2 * b + 2, :], src, act_hi[:, 2 * b:2 * b + 2, :].bitcast(f32),
                    ALU.subtract).then_inc(mix_ready, 1)

            def residual(par, cg, evacuated):
                cols = bass.ds(cg * GW, GW)
                u3 = upd[:, :].rearrange("p (t n) -> p t n", t=TT)
                if not (isinstance(evacuated, int) and evacuated == 1):
                    dve.wait_ge(x2_sum, evacuated - 1)
                TTn(u3, pair[par][:, :].rearrange("p (t n) -> p t n", t=TT), gate_cols(cg), ALU.mult)\
                    .then_inc(evac_dve, 1)
                dve.wait_ge(evac_dve, evacuated)
                TTn(x2[:, :, cols], x2[:, :, cols], u3, ALU.add).then_inc(x2_sum, 1)

            def gate_cols(cg):
                return view(acc[0][:, bass.ds(cg * GW, GW)], [[0, TT], [1, GW]])

            def out_residual(i):
                dve.wait_ge(pe_half, 8 * (G_OUT + i + 1))
                if i == 0:
                    dve.wait_ge(x2_in, 16 * TT)
                    dve.wait_ge(gate_row, 4)
                residual((1 + i) % 2, i, i + 1)

            for i in range(4):
                for j in range(HALVES):
                    if j == 4 and i:
                        out_residual(i - 1)
                    weight_lo(G_OUT + i, j)
                    if j % 2:
                        modulation(64 + 4 * i + j // 2, j // 2, 1, i, 4 if i == 0 and j == 1 else None)
            out_residual(3)
            dve.wait_ge(pe_mod, 5)
            STT(scale_h[:, :], aux[2][:, KT:2 * KT], 1.0, n2[:, :], ALU.add, ALU.mult).then_inc(col_ok, 1)
            inverse_rms(1)
            split_h(1, h2_f, h2_ready)

            def square(q, i):
                tiles = slice(4 * i, 4 * i + 4)
                r3 = relu[:, :].rearrange("p (k t) -> p k t", k=4)
                dve.wait_ge(evac_act, q * 4 + (N_IN + i + 1))
                TTn(relu[:, :], relu[:, :], relu[:, :], ALU.mult).then_inc(u_step, 1)
                dve.wait_ge(u_step, q * 8 + (2 * i + 1))
                v.tensor_copy(u_hi[:, tiles, :], r3).then_inc(u_step, 1)
                dve.wait_ge(u_step, q * 8 + (2 * i + 2))
                TTn(u_lo[:, tiles, :], r3, u_hi[:, tiles, :].bitcast(f32), ALU.subtract).then_inc(u_ready, 1)

            def down_residual(q, cg):
                dve.wait_ge(pe_half, q * 64 + 8 * (G_MLP + 4 + cg + 1))
                dve.wait_ge(gate_row, 8)
                residual((1 + cg) % 2, cg, q * 4 + (4 + cg + 1))

            def mlp_quarter(q):
                for i in range(8):
                    for j in range(HALVES):
                        if j == 4 and i >= 5:
                            down_residual(q, i - 5)
                        if j == 4 and i == 0 and not isinstance(q, int):
                            down_residual(q - 1, 3)
                        if j == 5 and 1 <= i <= 4:
                            square(q, i - 1)
                        weight_lo(q * 8 + (G_MLP + i), j)
                        if isinstance(q, int) and i < 4 and j % 2:
                            modulation(80 + 4 * i + j // 2, j // 2, 0, i, 5 if i == 0 and j == 1 else None)

            mlp_quarter(0)
            with dve.Fori(1, QUARTERS) as q:
                mlp_quarter(q)
            down_residual(QUARTERS - 1, 3)
            inverse_rms(2)
            dve.wait_ge(fg_in, 16)
            dve.wait_ge(rstd_ok, 3)
            for i in range(4):
                tt, cols = i // 2, slice(i % 2 * (D // 2), (i % 2 + 1) * (D // 2))
                STT(y_out[i][:, 0:D // 2], x2[:, tt, cols], rstd[:, tt:tt + 1], acc[1][:, cols],
                    ALU.mult, ALU.mult).then_inc(y_ok, 1)


def t5_one_hot():
    n = np.arange(S)
    exact = NB // 2
    nf = np.maximum(n, 1).astype(np.float32)
    large = exact + (np.log(nf / np.float32(exact)) / np.float32(math.log(128 / exact))
                     * np.float32(NB - exact)).astype(np.int32)
    bucket = np.where(n < exact, n, np.minimum(large, NB - 1))
    return np.ascontiguousarray((np.arange(NB)[:, None] == bucket[None, :]).astype(np.float32))


def blocks(w):
    n = w.shape[1] // GW
    return w.reshape(4, 4, P, n, GW).transpose(3, 0, 2, 1, 4).reshape(n * 4, P, 4 * GW)


def by_partition(a, tiles):
    return np.ascontiguousarray(np.asarray(a).reshape(tiles, P).T)


def kernel(x, c, w_mod, b_mod, norm1_g, w_in, b_f, w_cmp_k, w_cmp_v, pos_cmp, conv_w, conv_b, conv_ln_g,
           conv_ln_b, w_out, norm2_g, w_mlp1, w_mlp2, rel_bias, final_g):
    import concourse.bacc as _bacc
    from concourse.bass_utils import run_bass_kernel_spmd as _run

    w_in = np.asarray(w_in)[0]
    names = ["fq", "fk", "fv", "f", "nq", "kc", "vc", "ks", "vs", "kw", "vw", "ng", "ca", "cg"]
    d_h, d_kv = NFOX * HD, NKV * HD
    sizes = [d_h, d_h, d_h, NFOX, NNSA * HD] + [d_kv] * 6 + [3 * NNSA, D_CONV, D_CONV]
    at = dict(zip(names, np.split(w_in, np.cumsum(sizes)[:-1], axis=1)))
    transposed = np.concatenate([at[n] for n in ("ca", "cg", "fq", "nq", "fk", "kc", "vc", "ks", "kw")], axis=1)
    straight = np.concatenate([at[n] for n in ("fv", "vs", "vw", "f", "ng")], axis=1)
    tail = straight[:, 2 * GW:]
    b_in = blocks(transposed)
    b_straight = blocks(straight[:, :2 * GW])
    w1, w2 = np.asarray(w_mlp1)[0], np.asarray(w_mlp2)[0]
    stream = [b_in, b_straight[:4], b_straight, blocks(np.asarray(w_out)[0])]
    for q in range(QUARTERS):
        stream += [blocks(w1[:, q * D:(q + 1) * D]), blocks(w2[q * D:(q + 1) * D])]
    w_cmp = [np.asarray(w)[0].reshape(2, CMP_STRIDE, HD, HD).transpose(0, 2, 1, 3) for w in (w_cmp_k, w_cmp_v)]
    host = {
        "x": np.asarray(x).reshape(S, D),
        "c": by_partition(c, KT),
        "w_mod": blocks(np.asarray(w_mod)[0]),
        "b_mod": np.asarray(b_mod).reshape(6, D),
        "norm1_g": by_partition(norm1_g, KT),
        "norm2_g": by_partition(norm2_g, KT),
        "final_g": np.asarray(final_g).reshape(1, D),
        "w_main": np.concatenate(stream),
        "w_tail": tail.reshape(4, 4, P, TAIL).transpose(0, 2, 1, 3).reshape(4, P, 4 * TAIL),
        "b_f": np.asarray(b_f).reshape(1, NFOX),
        "w_cmp_k": w_cmp[0],
        "w_cmp_v": w_cmp[1],
        "pos": np.asarray(pos_cmp)[0].T,
        "conv_w": np.asarray(conv_w)[0].reshape(CONV_W, CT, P).transpose(2, 1, 0),
        "conv_b": by_partition(conv_b, CT),
        "conv_ln_g": by_partition(conv_ln_g, CT),
        "conv_ln_b": by_partition(conv_ln_b, CT),
        "rel_bias": np.asarray(rel_bias),
        "bucket_one_hot": t5_one_hot(),
    }
    nc = _bacc.Bacc("TRN2", target_bir_lowering=False, num_devices=1)
    arrays, args = {}, []
    for name, a in host.items():
        a = np.ascontiguousarray(a)
        arrays[f"in_{name}"] = a
        args.append(nc.dram_tensor(f"in_{name}", a.shape, mybir.dt.from_np(a.dtype), kind="ExternalInput").ap())
    out = nc.dram_tensor("out", (S, D), mybir.dt.float32, kind="ExternalOutput").ap()
    order = ["x", "c", "w_mod", "b_mod", "norm1_g", "norm2_g", "final_g", "w_main", "w_tail", "b_f", "w_cmp_k",
             "w_cmp_v", "pos", "conv_w", "conv_b", "conv_ln_g", "conv_ln_b", "rel_bias", "bucket_one_hot"]
    by_name = dict(zip(host, args))
    build(nc, *[by_name[n] for n in order], out)
    r = _run(nc, [arrays], core_ids=[0])
    return r.results[0]["out"].reshape(1, S, D)
```

```python
import math
from contextlib import ExitStack

import numpy as np
import concourse.bass as bass
from concourse import mybir

P = 128
D = 2048
S = 256
TT = S // P
KT = D // P
FF = 4 * D
HD = 64
NFOX = 12
NNSA = 12
NKV = 3
NCMP = 15
NCMP0 = 7
CMP_STRIDE = 16
CMP_LEN = 32
CONV_W = 31
CT = 4
D_CONV = CT * P
GW = 512
TAIL = 176
NB = 32
NEG = -1e30
EPS = 1e-6
QUARTERS = 4
HALVES = 8
N_IN = 11
G_OUT = N_IN
G_MLP = G_OUT + 4
N_GROUPS = G_MLP + 8 * QUARTERS
VCOLS = 2 * GW + TAIL
COL_F = 1152
COL_G = COL_F + NFOX
BPAD = 384
CONV_STEPS = CT * CONV_W
SUMS = 4 + 8
MOD_FIRST = 2 * KT
MOD_IN = [4, 4, 2, 2, 2, 2, 2, 2, 0, 2, 2]
MOD_HEADS = [0, 1, 2, 3, 4, 5, 6, 7] + list(range(16, 36, 2))
MOD_OUT = [2, 2, 2, 0]
SECTION_ACC = [0, 1, 0, 1, 1, 0]
assert MOD_FIRST + sum(MOD_IN) + len(MOD_HEADS) + sum(MOD_OUT) == 5 * KT
assert 4 * KT - MOD_FIRST - sum(MOD_IN) == 8


def view(ap, dims, shift=0):
    return bass.AP(ap.tensor, ap.offset + shift, [list(ap.ap[0])] + [list(d) for d in dims])


def build(nc, x_d, c_d, wmod_d, bmod_d, n1_d, n2_d, fg_d, main_d, tail_d, bf_d, wck_d, wcv_d, pos_d,
          convw_d, convb_d, lng_d, lnb_d, rel_d, onehot_d, out_d):
    f32, f32r = mybir.dt.float32, mybir.dt.float32r
    ALU, ACT, AX = mybir.AluOpType, mybir.ActivationFunctionType, mybir.AxisListType
    bias_scratch = nc.dram_tensor("bias_scratch", (NNSA, BPAD), f32, kind="Internal").ap()

    ctx = ExitStack()
    with ctx:
        def sb(name, shape, dt=f32, where=ctx):
            return where.enter_context(nc.sbuf_tensor(name, shape, dt))

        def sem(name):
            return ctx.enter_context(nc.semaphore(name))

        raw = [sb(f"raw{i}", [P, 4 * GW]) for i in range(4)]
        w_hi = [sb(f"w_hi{i}", [P, 2 * GW], f32r) for i in range(4)]
        w_lo = [sb(f"w_lo{i}", [P, 2 * GW], f32r) for i in range(4)]
        mod_raw = [sb(f"mod_raw{i}", [P, D]) for i in range(2)]
        acc = [sb(f"acc{i}", [P, D]) for i in range(2)]
        ident = sb("ident", [P, P])
        ones = sb("ones", [P, P])
        ones_conv = sb("ones_conv", [P, P])
        tri = sb("tri", [P, P])
        causal = sb("causal", [P, S])
        neg_id = sb("neg_id", [P, NFOX])
        neg_id_r = sb("neg_id_r", [P, NFOX], f32r)
        seen = sb("seen", [P, 1])
        c_col = sb("c_col", [P, KT])
        c_tmp = sb("c_tmp", [P, KT])
        c_act = sb("c_act", [P, KT])
        n1 = sb("n1", [P, KT])
        n2 = sb("n2", [P, KT])
        scale_h = sb("scale_h", [P, KT])
        shift_h = sb("shift_h", [P, KT])
        shift2 = sb("shift2", [P, KT])
        ssq = sb("ssq", [P, 3, TT, 4])
        mean_sq = sb("mean_sq", [P, TT])
        root = sb("root", [P, TT])
        rstd = sb("rstd", [P, TT])
        newton = sb("newton", [P, TT])
        bf_b = sb("bf_b", [P, NFOX])
        convw = sb("convw", [P, CT, CONV_W])
        convb = sb("convb", [P, CT])
        lng = sb("lng", [P, CT])
        lnb = sb("lnb", [P, CT])
        pos_t = sb("pos_t", [P, CMP_LEN])
        rel_t = sb("rel_t", [NB, NNSA])

        region = ExitStack()
        act_hi = sb("act_hi", [P, KT, S], f32r, region)
        act_lo = sb("act_lo", [P, KT, S], f32r, region)
        region.close()
        region = ExitStack()
        bias_t = sb("bias_t", [P, NNSA, S], f32, region)
        wck = sb("wck", [P, CMP_STRIDE, HD], f32, region)
        wcv = sb("wcv", [P, CMP_STRIDE, HD], f32, region)
        cmp_in = sb("cmp_in", [P, 6, S], f32, region)
        region.close()
        hold = sb("hold", [P, 2 * KT * S])
        phase = ExitStack()
        x_a = sb("x_a", [P, TT, D], f32, phase)
        xn_t = sb("xn_t", [P, KT, S], f32, phase)
        onehot = sb("onehot", [NB, S], f32, phase)
        bias_p = sb("bias_p", [NNSA, BPAD], f32, phase)
        h_f = [sb(f"h_f{i}", [P, 2 * S], f32, phase) for i in range(2)]
        sq_a = sb("sq_a", [P, D], f32, phase)
        phase.close()
        phase = ExitStack()
        z_t = sb("z_t", [P, 24, S], f32, phase)
        val = sb("val", [P, TT, VCOLS], f32, phase)
        conv_in = sb("conv_in", [P, CT, CONV_W - 1 + S], f32, phase)
        conv_y = sb("conv_y", [P, CT, S], f32, phase)
        k_swap = sb("k_swap", [P, 3, S], f32, phase)
        score = [sb(f"score{i}", [P, 3 * P], f32, phase) for i in range(3)]
        prob_t = [sb(f"prob_t{i}", [P, 3 * P], f32, phase) for i in range(2)]
        mix = sb("mix", [P, TT, NFOX * HD + NNSA * HD], f32, phase)
        add_t = sb("add_t", [P, TT * 4 * HD], f32, phase)
        neg_max = sb("neg_max", [P, 72], f32, phase)
        row_sum = sb("row_sum", [P, 72], f32, phase)
        row_r = sb("row_r", [P, 72], f32, phase)
        log_f = sb("log_f", [P, TT, NFOX], f32, phase)
        lf = [sb(f"lf{i}", [P, TT, NFOX], f32, phase) for i in range(5)]
        gate = sb("gate", [P, TT, 3 * NNSA], f32, phase)
        f_q = sb("f_q", [P, TT, NFOX], f32, phase)
        f_hi = sb("f_hi", [P, S], f32r, phase)
        f_lo = sb("f_lo", [P, S], f32r, phase)
        k_cmp = sb("k_cmp", [P, NKV, NCMP], f32, phase)
        v_cmp_t = sb("v_cmp_t", [HD, NKV, P], f32, phase)
        v_cmp = sb("v_cmp", [P, NKV, HD], f32, phase)
        cmp_m = sb("cmp_m", [P, TT * NNSA], f32, phase)
        cmp_r = sb("cmp_r", [P, TT * NNSA], f32, phase)
        phase.close()
        phase = ExitStack()
        x2 = sb("x2", [P, TT, D], f32, phase)
        upd = sb("upd", [P, TT * GW], f32, phase)
        y = sb("y", [P, TT, D], f32, phase)
        late = ExitStack()
        xn2 = sb("xn2", [P, TT, D], f32, late)
        h2_f = [sb(f"h2_f{i}", [P, 2 * S], f32, late) for i in range(2)]
        late.close()
        u_hi = sb("u_hi", [P, KT, S], f32r, phase)
        u_lo = sb("u_lo", [P, KT, S], f32r, phase)
        relu = sb("relu", [P, 4 * S], f32, phase)
        phase.close()
        y_out = [raw[i] for i in range(4)]
        p_cmp_t = z_t[:, 18:21, :]
        p_cmp = z_t[:, 0:3, :].rearrange("p k t -> p (k t)").rearrange("p (t h n) -> p t h n", t=TT, h=NNSA)
        s_cmp = z_t[:, 3:5, :].rearrange("p k t -> p (k t)")[:, 0:TT * NNSA * 16]\
            .rearrange("p (t h n) -> p t h n", t=TT, h=NNSA)
        var_b, root_b, inv_b, newton_b = (conv_in[:, i, 0:S] for i in range(4))

        pair = [ctx.enter_context(nc.psum_tensor(f"pair{i}", [P, 2 * GW], f32)) for i in range(2)]
        aux = [ctx.enter_context(nc.psum_tensor(f"aux{i}", [P, GW], f32)) for i in range(4)]
        t_bank = [pair[1][:, 0:GW], pair[1][:, GW:2 * GW]]
        o_bank = [pair[0][:, 0:GW], pair[0][:, GW:2 * GW]]

        small_in = sem("small_in")
        x_in = sem("x_in")
        consts = sem("consts")
        raw_full = [sem(f"raw_full{i}") for i in range(4)]
        mod_full = [sem(f"mod_full{i}") for i in range(2)]
        hi_done = sem("hi_done")
        lo_done = sem("lo_done")
        pe_half = sem("pe_half")
        evac_act = sem("evac_act")
        evac_dve = sem("evac_dve")
        mod_step = sem("mod_step")
        acc_zero = sem("acc_zero")
        acc_init = [sem(f"acc_init{i}") for i in range(6)]
        pe_mod = sem("pe_mod")
        c_sig = sem("c_sig")
        act_sq = sem("act_sq")
        act_root = sem("act_root")
        dve_ms = sem("dve_ms")
        rstd_ok = sem("rstd_ok")
        xn_ok = sem("xn_ok")
        xt_ps = sem("xt_ps")
        xt_ok = sem("xt_ok")
        col_ok = sem("col_ok")
        h_ok = sem("h_ok")
        h_ready = sem("h_ready")
        h2_ready = sem("h2_ready")
        mix_ready = sem("mix_ready")
        u_ready = sem("u_ready")
        dve_c = sem("dve_c")
        pool_c = sem("pool_c")
        bias_ps = sem("bias_ps")
        bias_row = sem("bias_row")
        bias_out = sem("bias_out")
        bias_in = sem("bias_in")
        cmp_w_in = sem("cmp_w_in")
        gate_row = sem("gate_row")
        conv_e = sem("conv_e")
        conv_sem = sem("conv_sem")
        ln_ps = sem("ln_ps")
        ln_root = sem("ln_root")
        ln_sig = sem("ln_sig")
        ln_sq = sem("ln_sq")
        ln_var = sem("ln_var")
        ln_y = sem("ln_y")
        lf_in = sem("lf_in")
        lf_exp = sem("lf_exp")
        gate_ok = sem("gate_ok")
        lf_ok = sem("lf_ok")
        f_ps = sem("f_ps")
        f_sb = sem("f_sb")
        s_ready = sem("s_ready")
        s_biased = sem("s_biased")
        p_ready = sem("p_ready")
        t_ready = sem("t_ready")
        t_act = sem("t_act")
        t_dve = sem("t_dve")
        o_ready = sem("o_ready")
        o_used = sem("o_used")
        swap_ok = sem("swap_ok")
        cmp_x = sem("cmp_x")
        cmp_ps = sem("cmp_ps")
        cmp_sb = sem("cmp_sb")
        cmp_exp = sem("cmp_exp")
        mix_done = sem("mix_done")
        mt_ps = sem("mt_ps")
        mt_hi = sem("mt_hi")
        h_hi = sem("h_hi")
        relu_ok = sem("relu_ok")
        u_step = sem("u_step")
        x2_in = sem("x2_in")
        x2_sum = sem("x2_sum")
        fg_in = sem("fg_in")
        y_gain = sem("y_gain")
        y_ok = sem("y_ok")
        y_out_s = sem("y_out_s")

        N_SMALL = 12

        def block_half(tensor, j, width):
            return tensor[(j // 2) % 4][:, (j % 2) * 2 * width:(j % 2 + 1) * 2 * width]

        block = ctx.enter_context(nc.Block())

        @block.sync
        def _(sp):
            def weights(g, q, source=None):
                if isinstance(g, int) and g == 0:
                    sp.wait_ge(mod_step, MOD_FIRST - 4 + q + 2)
                else:
                    sp.wait_ge(lo_done, (g - 1) * 8 + 2 * q + 2)
                if source is None:
                    sp.dma_start(raw[q][:, :], main_d[g * 4 + q, :, :]).then_inc(raw_full[q], 16)
                else:
                    sp.dma_start(raw[q][:, 0:4 * TAIL], source).then_inc(raw_full[q], 16)

            def modulation(m, slot):
                if not (isinstance(m, int) and m < MOD_FIRST + 2):
                    sp.wait_ge(mod_step, m)
                sp.dma_start(mod_raw[slot][:, :], wmod_d[m, :, :]).then_inc(mod_full[slot], 16)

            for m in range(4):
                sp.dma_start(raw[m][:, :], wmod_d[m, :, :]).then_inc(raw_full[m], 16)

            def first_modulation(i):
                for r in range(4):
                    sp.wait_ge(mod_step, i * 4 + (r - 2))
                    sp.dma_start(raw[r][:, :], wmod_d[i * 4 + r, :, :]).then_inc(raw_full[r], 16)

            with sp.Fori(1, 4) as i:
                first_modulation(i)
            for tt in range(TT):
                sp.dma_start(x_a[:, tt, :], x_d[tt * P:(tt + 1) * P, :]).then_inc(x_in, 16)
            with sp.Fori(4, 8) as i:
                first_modulation(i)
            m = MOD_FIRST
            for g in range(N_IN):
                for q in range(4):
                    if g == 8:
                        weights(g, q, tail_d[q, :, :])
                    else:
                        weights(g, q)
                    if q < MOD_IN[g]:
                        modulation(m, m % 2)
                        m += 1
            for q in range(4):
                weights(G_OUT, q)
            for _ in range(len(MOD_HEADS) + MOD_OUT[0]):
                modulation(m, m % 2)
                m += 1
            sp.wait_ge(mix_ready, 8)
            for tt in range(TT):
                sp.dma_start(x2[:, tt, :], x_d[tt * P:(tt + 1) * P, :]).then_inc(x2_in, 16)
            for i in range(1, 4):
                for q in range(4):
                    weights(G_OUT + i, q)
                    if q < MOD_OUT[i]:
                        modulation(m, m % 2)
                        m += 1

            def mlp_loads(q):
                for i in range(8):
                    for r in range(4):
                        weights(q * 8 + (G_MLP + i), r)
                        if i < 4 and r == 1:
                            modulation(q * 4 + (5 * KT + i), i % 2)

            mlp_loads(0)
            sp.wait_ge(pe_mod, 5)
            sp.dma_start(acc[1][:, :], fg_d.to_broadcast([P, D])).then_inc(fg_in, 16)
            with sp.Fori(1, QUARTERS) as q:
                mlp_loads(q)
            for i in range(4):
                tt, half = i // 2, i % 2
                sp.wait_ge(y_ok, i + 1)
                sp.dma_start(out_d[tt * P:(tt + 1) * P, half * D // 2:(half + 1) * D // 2],
                             y_out[i][:, 0:D // 2]).then_inc(y_out_s, 16)
            sp.wait_ge(y_out_s, 4 * 16)

        @block.gpsimd
        def _(pool):
            n = 0

            def step(ins):
                nonlocal n
                ins.then_inc(pool_c, 1)
                n += 1
                pool.wait_ge(pool_c, n)

            step(nc.gpsimd.memset(ident[:, :], 0.0))
            step(nc.gpsimd.affine_select(out=ident[:, :], in_=ident[:, :], compare_op=ALU.not_equal, fill=1.0,
                                         base=0, pattern=[[-1, P]], channel_multiplier=1))
            step(nc.gpsimd.memset(ones[:, :], 1.0))
            step(nc.gpsimd.memset(ones_conv[:, :], 1.0 / D_CONV))
            step(nc.gpsimd.memset(tri[:, :], 1.0))
            step(nc.gpsimd.affine_select(out=tri[:, :], in_=tri[:, :], compare_op=ALU.is_ge, fill=0.0,
                                         base=0, pattern=[[1, P]], channel_multiplier=-1))
            step(nc.gpsimd.memset(causal[:, :], 0.0))
            step(nc.gpsimd.affine_select(out=causal[:, :], in_=causal[:, :], compare_op=ALU.is_ge, fill=NEG,
                                         base=P, pattern=[[-1, S]], channel_multiplier=1))
            step(nc.gpsimd.memset(neg_id[:, :], 0.0))
            for base in (0, HD):
                step(nc.gpsimd.affine_select(out=neg_id[:, :], in_=neg_id[:, :], compare_op=ALU.not_equal,
                                             fill=-1.0, base=-base, pattern=[[-1, NFOX]], channel_multiplier=1))
            step(nc.gpsimd.memset(seen[:, :], 1.0))
            step(nc.gpsimd.affine_select(out=seen[:, :], in_=seen[:, :], compare_op=ALU.is_ge, fill=0.0,
                                         base=-(CMP_LEN - 1), pattern=[[0, 1]], channel_multiplier=1))
            nc.gpsimd.memset(bias_p[:, :], NEG).then_inc(consts, 1)

            for s, a in enumerate(SECTION_ACC):
                if s in (2, 3):
                    pool.wait_ge(pe_mod, s - 1)
                if s == 4:
                    pool.wait_ge(pe_mod, 4)
                if s == 5:
                    pool.wait_ge(evac_dve, 4)
                nc.gpsimd.memset(acc[a][:, :], 0.0).then_inc(acc_zero, 1)
                pool.wait_ge(acc_zero, s + 1)
                pool.dma_start(acc[a][0:1, :], bmod_d[s:s + 1, :]).then_inc(acc_init[s], 16)

        @block.scalar
        def _(act):
            A = nc.scalar.activation

            loads = [(c_col[:, :], c_d), (n1[:, :], n1_d), (n2[:, :], n2_d),
                     (rel_t[:, :], rel_d), (onehot[:, :], onehot_d),
                     (bf_b[:, :], bf_d.to_broadcast([P, NFOX])), (convw[:, :, :], convw_d),
                     (convb[:, :], convb_d), (lng[:, :], lng_d), (lnb[:, :], lnb_d),
                     (pos_t[0:HD, :], pos_d), (pos_t[HD:P, :], pos_d)]
            for dst, src in loads:
                act.dma_start(dst, src).then_inc(small_in, 16)
            assert len(loads) == N_SMALL
            act.wait_ge(small_in, 16 * N_SMALL)
            A(c_tmp[:, :], c_col[:, :], ACT.Sigmoid).then_inc(c_sig, 1)

            act.wait_ge(x_in, 16 * TT)
            for n in range(4 * TT):
                tt, cg = n % TT, n // TT
                A(sq_a[:, n * GW // 2:(n + 1) * GW // 2].bitcast(mybir.dt.bfloat16),
                  x_a[:, tt, cg * GW:(cg + 1) * GW], ACT.Square, accum_out=ssq[:, 0, tt, cg:cg + 1])\
                    .then_inc(act_sq, 1)
            act.wait_ge(dve_ms, 1)
            A(root[:, :], mean_sq[:, :], ACT.Sqrt).then_inc(act_root, 1)
            act.wait_ge(rstd_ok, 1)
            for tt in range(TT):
                A(x_a[:, tt, :], x_a[:, tt, :], ACT.Copy, scale=rstd[:, tt:tt + 1]).then_inc(xn_ok, 1)
            act.wait_ge(bias_ps, 1)
            act.wait_ge(consts, 1)
            A(bias_p[:, P - 1:P - 1 + S], aux[3][0:NNSA, 0:S], ACT.Copy).then_inc(bias_row, 1)
            act.wait_ge(bias_row, 1)
            act.dma_start(bias_scratch[:, :], bias_p[:, :]).then_inc(bias_out, 16)
            for b in range(KT // 2):
                act.wait_ge(xt_ps, b + 1)
                A(xn_t[:, 2 * b:2 * b + 2, :], aux[b % 2][:, :].rearrange("p (k t) -> p k t", k=2),
                  ACT.Copy).then_inc(xt_ok, 1)
            act.wait_ge(col_ok, 2)
            for b in range(KT // 2):
                if b >= 2:
                    act.wait_ge(h_ready, b - 1)
                for k in (2 * b, 2 * b + 1):
                    A(h_f[b % 2][:, (k % 2) * S:(k % 2 + 1) * S], xn_t[:, k, :], ACT.Identity,
                      bias=shift_h[:, k:k + 1], scale=scale_h[:, k:k + 1]).then_inc(h_ok, 1)

            def weight_hi(g, j, width=GW, first=False):
                act.wait_ge(raw_full[j // 2], (g + (1 + MOD_FIRST // 4)) * 16)
                if not (first and j < 4):
                    act.wait_ge(pe_half, g * 8 + j - 3)
                A(w_hi[j % 4][:, 0:2 * width], block_half(raw, j, width), ACT.Copy).then_inc(hi_done, 1)

            def evacuate(g):
                act.wait_ge(pe_half, 8 * (g + 1))
                if g == 0:
                    A(conv_in[:, :, CONV_W - 1:], pair[0][:, :].rearrange("p (k t) -> p k t", k=CT),
                      ACT.Copy).then_inc(evac_act, 1)
                elif g == 1:
                    A(conv_y[:, :, :], pair[1][:, :].rearrange("p (k t) -> p k t", k=CT),
                      ACT.Sigmoid).then_inc(evac_act, 1)
                elif g < 8:
                    A(z_t[:, 4 * (g - 2):4 * (g - 1), :], pair[g % 2][:, :].rearrange("p (k t) -> p k t", k=4),
                      ACT.Copy, scale=HD ** -0.5 if g < 5 else 1.0).then_inc(evac_act, 1)
                else:
                    at, width = {8: (2 * GW, TAIL), 9: (0, GW), 10: (GW, GW)}[g]
                    A(val[:, :, at:at + width],
                      pair[g % 2][:, :].rearrange("p (t n) -> p t n", t=TT)[:, :, 0:width],
                      ACT.Copy).then_inc(evac_act, 1)

            act.wait_ge(bias_out, 16)
            for g in range(N_IN):
                for j in range(HALVES):
                    if j == 4 and g:
                        evacuate(g - 1)
                    weight_hi(g, j, TAIL if g == 8 else GW, first=g == 0)
                    if g == 9 and j == 5:
                        act.wait_ge(evac_act, 9)
                        A(gate[:, :, :], val[:, :, COL_G:COL_G + 3 * NNSA], ACT.Sigmoid)\
                            .then_inc(gate_ok, 1)
                        act.wait_ge(lf_in, 1)
                        A(lf[1][:, :, :], lf[1][:, :, :], ACT.Exp, scale=-1.0).then_inc(lf_exp, 1)
            evacuate(N_IN - 1)
            act.wait_ge(pe_half, 8 * N_IN)
            act.wait_ge(bias_out, 16)
            diag = bass.AP(bias_scratch.tensor, bias_scratch.offset, [[1, P], [BPAD, NNSA], [1, S]])
            act.dma_start(bias_t[:, :, :], diag).then_inc(bias_in, 16)
            for h in range(2):
                act.dma_start(wck[h * HD:(h + 1) * HD, :, :], wck_d[h, :, :, :]).then_inc(cmp_w_in, 16)
                act.dma_start(wcv[h * HD:(h + 1) * HD, :, :], wcv_d[h, :, :, :]).then_inc(cmp_w_in, 16)
            act.wait_ge(evac_act, 8)
            A(k_swap[HD:P, :, :], z_t[0:HD, 21:24, :], ACT.Copy).then_inc(swap_ok, 1)
            A(k_swap[0:HD, :, :], z_t[HD:P, 21:24, :], ACT.Copy).then_inc(swap_ok, 1)
            for cg in range(4):
                act.wait_ge(pe_mod, 3)
                A(acc[0][:, cg * GW:(cg + 1) * GW], pair[cg // 2][:, (cg % 2) * GW:(cg % 2 + 1) * GW],
                  ACT.Copy).then_inc(gate_row, 1)

            def conv_norm(part):
                if part == 0:
                    act.wait_ge(ln_var, 1)
                    A(root_b, var_b, ACT.Sqrt).then_inc(ln_root, 1)
                else:
                    act.wait_ge(ln_y, 1)
                    A(conv_in[:, :, 0:S], conv_y[:, :, :], ACT.Sigmoid).then_inc(ln_sig, 1)

            def attend(a):
                if a < 36:
                    sign = 1.0 if a < NFOX else -1.0
                    act.wait_ge(s_biased, a + 1)
                    A(score[a % 3][:, 0:P], score[a % 3][:, 0:P], ACT.Exp, scale=sign,
                      bias=neg_max[:, 2 * a:2 * a + 1], accum_out=row_sum[:, 2 * a:2 * a + 1])
                    A(score[a % 3][:, P:3 * P], score[a % 3][:, P:3 * P], ACT.Exp, scale=sign,
                      bias=neg_max[:, 2 * a + 1:2 * a + 2], accum_out=row_sum[:, 2 * a + 1:2 * a + 2])\
                        .then_inc(p_ready, 1)
                b = a - 2
                if 0 <= b < 36 and b % 2 == 0:
                    act.wait_ge(t_ready, b + 1)
                    if b >= 2:
                        act.wait_ge(o_ready, b - 1)
                    A(prob_t[0][:, :], t_bank[0][:, 0:3 * P], ACT.Copy).then_inc(t_act, 1)

            for a in range(36 + 2):
                attend(a)
                if a == 4:
                    conv_norm(0)
                if a == 8:
                    conv_norm(1)
                if a == 26:
                    act.wait_ge(cmp_x, 2)
                    A(p_cmp[:, :, :, 0:16], s_cmp[:, :, :, :], ACT.Exp).then_inc(cmp_exp, 1)

            for b in range(8):
                if b < 6:
                    act.wait_ge(mt_ps, b + 1)
                    A(act_hi[:, 2 * b:2 * b + 2, :], aux[b % 2][:, :].rearrange("p (k t) -> p k t", k=2),
                      ACT.Copy).then_inc(mt_hi, 1)
                else:
                    if b == 6:
                        act.wait_ge(mt_ps, 6)
                    A(act_hi[:, 2 * b:2 * b + 2, :], conv_y[:, 2 * (b - 6):2 * (b - 6) + 2, :],
                      ACT.Copy).then_inc(mt_hi, 1)

            def squares(n, cg, sums, junk):
                act.wait_ge(x2_sum, sums)
                for tt in range(TT):
                    A(junk[tt][:, cg * GW:(cg + 1) * GW], x2[:, tt, cg * GW:(cg + 1) * GW], ACT.Square,
                      accum_out=ssq[:, n, tt, cg:cg + 1]).then_inc(act_sq, 1)

            junk = [xn2[:, tt, :] for tt in range(TT)]
            for i in range(4):
                for j in range(HALVES):
                    if j == 7 and i:
                        squares(1, i - 1, i, junk)
                    weight_hi(G_OUT + i, j)

            squares(1, 3, 4, junk)
            act.wait_ge(dve_ms, 2)
            A(root[:, :], mean_sq[:, :], ACT.Sqrt).then_inc(act_root, 1)
            act.wait_ge(col_ok, 4)
            for b in range(KT // 2):
                act.wait_ge(xt_ps, KT // 2 + b + 1)
                if b >= 2:
                    act.wait_ge(h2_ready, b - 1)
                for k in (2 * b, 2 * b + 1):
                    A(h2_f[b % 2][:, (k % 2) * S:(k % 2 + 1) * S], aux[b % 2][:, (k % 2) * S:(k % 2 + 1) * S],
                      ACT.Identity, bias=shift2[:, k:k + 1], scale=scale_h[:, k:k + 1]).then_inc(h_ok, 1)

            def mlp_quarter(q, first=False, final=False):
                for i in range(8):
                    g = q * 8 + (G_MLP + i)
                    for j in range(HALVES):
                        if j == 4 and 1 <= i <= 4:
                            act.wait_ge(pe_half, g * 8)
                            if not (first and i == 1):
                                act.wait_ge(u_ready, q * 4 + (i - 1))
                            A(relu[:, :], pair[i % 2][:, :], ACT.Relu).then_inc(evac_act, 1)
                        if j == 7 and final and i >= 5:
                            squares(2, i - 5, SUMS - 4 + (i - 4), mod_raw)
                        if j == 4 and final and i == 4:
                            act.wait_ge(pe_mod, 6)
                            for cg in range(4):
                                A(acc[0][:, cg * GW:(cg + 1) * GW], aux[cg][:, :], ACT.Copy)\
                                    .then_inc(gate_row, 1)
                        weight_hi(g, j)

            mlp_quarter(0, first=True)
            with act.Fori(1, QUARTERS - 1) as q:
                mlp_quarter(q)
            mlp_quarter(QUARTERS - 1, final=True)
            squares(2, 3, SUMS, mod_raw)
            act.wait_ge(dve_ms, 3)
            A(root[:, :], mean_sq[:, :], ACT.Sqrt).then_inc(act_root, 1)

        @block.tensor
        def _(pe):
            mm = nc.tensor.matmul

            def transposed_group(g, par, ready, reach):
                for j in range(HALVES):
                    if ready is not None:
                        pe.wait_ge(ready, reach(j))
                    pe.wait_ge(lo_done, g * 8 + (j + 1))
                    for kk in range(2):
                        k = 2 * j + kk
                        for m in range(4):
                            out = pair[par][:, m * S:(m + 1) * S]
                            cols = slice(kk * GW + m * P, kk * GW + (m + 1) * P)
                            hi, lo = w_hi[j % 4][:, cols], w_lo[j % 4][:, cols]
                            mm(out, hi, act_hi[:, k, :], start=k == 0 and m % 2 == 0, stop=False,
                               skip_group_check=True)
                            mm(out, hi, act_lo[:, k, :], start=False, stop=False, skip_group_check=True)
                            last = mm(out, lo, act_hi[:, k, :], start=False, stop=k == KT - 1,
                                      skip_group_check=True)
                    last.then_inc(pe_half, 1)

            def straight_group(g, par, a_hi, a_lo, ready, reach, width=GW):
                for j in range(HALVES):
                    if ready is not None:
                        pe.wait_ge(ready, reach(j))
                    pe.wait_ge(lo_done, g * 8 + (j + 1))
                    for kk in range(2):
                        k = 2 * j + kk
                        for tt in range(TT):
                            out = pair[par][:, tt * GW:tt * GW + width]
                            cols = slice(kk * width, (kk + 1) * width)
                            hi, lo = w_hi[j % 4][:, cols], w_lo[j % 4][:, cols]
                            t_hi, t_lo = a_hi[:, k, tt * P:(tt + 1) * P], a_lo[:, k, tt * P:(tt + 1) * P]
                            mm(out, t_hi, hi, start=k == 0, stop=False)
                            mm(out, t_hi, lo, start=False, stop=False)
                            last = mm(out, t_lo, hi, start=False, stop=k == KT - 1)
                    last.then_inc(pe_half, 1)

            def columns(a, bank, at):
                for k in range(KT):
                    last = mm(bank[:, at + k:at + k + 1], acc[a][:, k * P:(k + 1) * P], ones[:, 0:1],
                              start=True, stop=True)
                last.then_inc(pe_mod, 1)

            def rows(a, banks):
                for cg in range(4):
                    last = mm(banks[cg], ones[:, :], acc[a][:, cg * GW:(cg + 1) * GW], start=True, stop=True)
                last.then_inc(pe_mod, 1)

            pe.wait_ge(small_in, 16 * N_SMALL)
            mm(aux[3][0:NNSA, 0:S], rel_t[:, :], onehot[:, :], start=True, stop=True).then_inc(bias_ps, 1)
            pe.wait_ge(consts, 1)
            pe.wait_ge(xn_ok, TT)
            for b in range(KT // 2):
                if b >= 2:
                    pe.wait_ge(xt_ok, b - 1)
                for kk in range(2):
                    for tt in range(TT):
                        k = 2 * b + kk
                        last = nc.tensor.transpose(aux[b % 2][:, kk * S + tt * P:kk * S + (tt + 1) * P],
                                                   x_a[:, tt, k * P:(k + 1) * P], ident[:, :])
                last.then_inc(xt_ps, 1)
            pe.wait_ge(mod_step, 16 + 1)
            columns(0, aux[2], 0)
            pe.wait_ge(mod_step, 32 + 1)
            pe.wait_ge(col_ok, 1)
            columns(1, aux[2], KT)

            transposed_group(0, 0, h_ready, lambda j: j + 1)
            transposed_group(1, 1, None, None)
            with pe.Fori(1, 4) as i:
                for par in range(2):
                    pe.wait_ge(evac_act, i * 2 + (par - 1))
                    transposed_group(i * 2 + par, par, None, None)
            for g in range(8, N_IN):
                pe.wait_ge(evac_act, g - 1)
                straight_group(g, g % 2, act_hi, act_lo, None, None, TAIL if g == 8 else GW)

            pe.wait_ge(lf_ok, 1)
            mm(aux[0][:, 0:NFOX], tri[:, :], log_f[:, 0, :], start=True, stop=True)
            mm(aux[0][:, NFOX:2 * NFOX], ones[:, :], log_f[:, 0, :], start=True, stop=False)
            mm(aux[0][:, NFOX:2 * NFOX], tri[:, :], log_f[:, 1, :], start=False, stop=True)
            for n, base in enumerate((0, HD)):
                out = aux[1 + n][base:base + NFOX, 0:S]
                mm(out[:, 0:P], log_f[:, 0, :], tri[:, :], start=True, stop=True)
                mm(out[:, P:S], log_f[:, 0, :], ones[:, :], start=True, stop=False)
                last = mm(out[:, P:S], log_f[:, 1, :], tri[:, :], start=False, stop=True)
            last.then_inc(f_ps, 1)
            pe.wait_ge(evac_act, N_IN)
            rows(0, [pair[cg // 2][:, (cg % 2) * GW:(cg % 2 + 1) * GW] for cg in range(4)])
            pe.wait_ge(f_sb, 2)

            def key_of(a, base):
                if a < NFOX:
                    return z_t[base:base + HD, 12 + a // 2, :]
                n = (a - NFOX) // NNSA * NKV + (a - NFOX) % NNSA // 4
                if n % 2 == a % 2:
                    return z_t[base:base + HD, 21 + n // 2, :]
                return k_swap[base:base + HD, n // 2, :]

            def scores(a):
                base = HD * (a % 2)
                out = aux[a % 3]
                query = z_t[base:base + HD, a // 2 if a < NFOX else 6 + (a - NFOX) % NNSA // 2, :]
                key = key_of(a, base)
                if a == 0:
                    pe.wait_ge(evac_act, 8)
                if a >= 3:
                    pe.wait_ge(s_biased, a - 2)
                if a == NFOX:
                    pe.wait_ge(swap_ok, 2)
                if a == 24:
                    pe.wait_ge(cmp_sb, 4)
                for tt, (at, n) in enumerate(((0, P), (P, S))):
                    last = mm(out[:, at:at + n], query[:, tt * P:(tt + 1) * P], key[:, 0:n], start=True,
                              stop=a >= NFOX)
                    if a < NFOX:
                        pick = neg_id_r[base:base + NFOX, a:a + 1].to_broadcast([NFOX, P])
                        mm(out[:, at:at + n], pick, f_hi[base:base + NFOX, 0:n], start=False, stop=False)
                        last = mm(out[:, at:at + n], pick, f_lo[base:base + NFOX, 0:n], start=False, stop=True)
                last.then_inc(s_ready, 1)

            def transposes(a):
                pe.wait_ge(p_ready, a + 1)
                if a == 0:
                    pe.wait_ge(gate_row, 4)
                if a >= 2:
                    pe.wait_ge(t_dve if a % 2 else t_act, a // 2)
                for n in range(3):
                    last = nc.tensor.transpose(t_bank[a % 2][:, n * P:(n + 1) * P],
                                               score[a % 3][:, n * P:(n + 1) * P], ident[:, :])
                last.then_inc(t_ready, 1)

            def outputs(a):
                pe.wait_ge(t_dve if a % 2 else t_act, a // 2 + 1)
                unit, r = a // 4, a % 4
                if r == 0 and unit >= 2:
                    pe.wait_ge(o_used, unit - 1)
                at = a * HD if a < NFOX else NFOX * HD + ((a - NFOX) // NNSA * NKV + (a - NFOX) % NNSA // 4) * HD
                out = [o_bank[unit % 2][:, (tt * 4 + r) * HD:(tt * 4 + r + 1) * HD] for tt in range(TT)]
                pt = prob_t[a % 2]
                mm(out[0], pt[:, 0:P], val[:, 0, at:at + HD], start=True, stop=True)
                mm(out[1], pt[:, P:2 * P], val[:, 0, at:at + HD], start=True, stop=False)
                mm(out[1], pt[:, 2 * P:3 * P], val[:, 1, at:at + HD], start=False, stop=True).then_inc(o_ready, 1)

            for a in range(36 + 3):
                if a == 2:
                    pe.wait_ge(conv_sem, CONV_STEPS)
                    for ct in range(CT):
                        last = mm(aux[3][:, 0:S], ones_conv[:, :], conv_y[:, ct, :], start=ct == 0,
                                  stop=ct == CT - 1)
                    last.then_inc(ln_ps, 1)
                if a == 5:
                    pe.wait_ge(ln_sq, 1)
                    for ct in range(CT):
                        last = mm(aux[3][:, S:2 * S], ones_conv[:, :], conv_in[:, ct, 0:S], start=ct == 0,
                                  stop=ct == CT - 1)
                    last.then_inc(ln_ps, 1)
                if a == 11:
                    pe.wait_ge(mod_step, 4 * KT + 1)
                    pe.wait_ge(ln_var, 1)
                    columns(1, aux[3], 0)
                if a == 14:
                    pe.wait_ge(col_ok, 3)
                    pe.wait_ge(cmp_x, 1)
                    pe.wait_ge(cmp_w_in, 4 * 16)
                    for n, w in enumerate((wck, wcv)):
                        for l in range(CMP_STRIDE):
                            tokens = view(cmp_in[:, 3 * n:3 * n + 3, :],
                                          [[S, NKV], [CMP_STRIDE, NCMP]], l)
                            last = mm(aux[3][0:HD, HD * n:HD * n + NKV * NCMP], w[:, l, :], tokens,
                                      start=l == 0, stop=l == CMP_STRIDE - 1)
                    last.then_inc(cmp_ps, 1)
                if a == 18:
                    pe.wait_ge(cmp_sb, 2)
                    for g in range(NKV):
                        last = nc.tensor.transpose(aux[3][:, P + g * HD:P + (g + 1) * HD], v_cmp_t[:, g, :],
                                                   ident[0:HD, 0:HD])
                    last.then_inc(cmp_ps, 1)
                if a == 24:
                    pe.wait_ge(cmp_sb, 3)
                    pe.wait_ge(s_biased, 22)
                    for odd in range(2):
                        for tt, count in enumerate((NCMP0, NCMP)):
                            for h in range(odd, NNSA, 2):
                                at = (tt * NNSA + h) * 16
                                last = mm((aux[0] if odd else aux[3])[:, at:at + count],
                                          z_t[HD * odd:HD * odd + HD, 6 + h // 2, tt * P:(tt + 1) * P],
                                          k_cmp[HD * odd:HD * odd + HD, h // 4, 0:count], start=True, stop=True)
                    last.then_inc(cmp_ps, 1)
                if a in (30, 34):
                    tt = (a - 30) // 4
                    pe.wait_ge(cmp_exp, 1)
                    if tt:
                        pe.wait_ge(cmp_sb, 5)
                    for g in range(NKV):
                        last = nc.tensor.transpose(
                            aux[3][:, g * P:(g + 1) * P],
                            p_cmp[:, tt, 4 * g:4 * g + 4, :].rearrange("p h n -> p (h n)"), ident[:, :])
                    last.then_inc(cmp_ps, 1)
                if a < 36:
                    scores(a)
                if 0 <= a - 2 < 36:
                    transposes(a - 2)
                if a >= 3:
                    outputs(a - 3)
            pe.wait_ge(cmp_sb, 6)
            pe.wait_ge(s_biased, 36)
            for r in range(4):
                rows_r = slice(32 * r, 32 * r + 32)
                for tt in range(TT):
                    for g in range(NKV):
                        at = (tt * NKV + g) * HD
                        last = mm(aux[r][:, at:at + HD], p_cmp_t[rows_r, :, :].rearrange("p a b -> p (a b)")
                                  [:, (tt * NKV + g) * P:(tt * NKV + g + 1) * P],
                                  v_cmp[rows_r, g, :], start=True, stop=True, tile_position=(32 * r, 0))
            last.then_inc(cmp_ps, 1)
            pe.wait_ge(mix_done, 4)
            for b in range(6):
                if b >= 2:
                    pe.wait_ge(mix_ready, b - 1)
                for kk in range(2):
                    for tt in range(TT):
                        k = 2 * b + kk
                        last = nc.tensor.transpose(aux[b % 2][:, kk * S + tt * P:kk * S + (tt + 1) * P],
                                                   mix[:, tt, k * P:(k + 1) * P], ident[:, :])
                last.then_inc(mt_ps, 1)

            for i in range(4):
                if i >= 2:
                    pe.wait_ge(evac_dve, i - 1)
                straight_group(G_OUT + i, (1 + i) % 2, act_hi, act_lo, mix_ready, lambda j: j + 1)
            pe.wait_ge(mod_step, 5 * KT + 1)
            columns(1, aux[2], KT)
            for b in range(KT // 2):
                pe.wait_ge(xn_ok, TT + (TT if b < 4 else 2 * TT))
                if b >= 2:
                    pe.wait_ge(h_ok, 2 * (KT // 2 + b - 1))
                for kk in range(2):
                    for tt in range(TT):
                        k = 2 * b + kk
                        last = nc.tensor.transpose(aux[b % 2][:, kk * S + tt * P:kk * S + (tt + 1) * P],
                                                   xn2[:, tt, k * P:(k + 1) * P], ident[:, :])
                last.then_inc(xt_ps, 1)

            def mlp_up(q):
                with pe.Fori(0, 2) as i:
                    for par in range(2):
                        pe.wait_ge(evac_dve, q * 4 + (3 + par))
                        pe.wait_ge(evac_act, q * 4 + i * 2 + (N_IN - 1 + par))
                        transposed_group(q * 8 + i * 2 + (G_MLP + par), (1 + par) % 2, h2_ready, lambda j: j + 1)

            def mlp_down(q, i, par):
                pe.wait_ge(evac_act, q * 4 + (N_IN + 3 + par))
                pe.wait_ge(evac_dve, q * 4 + i + 3)
                straight_group(q * 8 + i + (G_MLP + 4), (1 + par) % 2, u_hi, u_lo, u_ready,
                               lambda j: q * 4 + (j // 2 + 1))

            with pe.Fori(0, QUARTERS - 1) as q:
                mlp_up(q)
                with pe.Fori(0, 2) as i:
                    for par in range(2):
                        mlp_down(q, i * 2 + par, par)
            mlp_up(QUARTERS - 1)
            pe.wait_ge(mod_step, 6 * KT + 1)
            rows(0, [aux[cg][:, :] for cg in range(4)])
            for i in range(4):
                mlp_down(QUARTERS - 1, i, i % 2)

        @block.vector
        def _(dve):
            v = nc.vector
            TS, TTn, STT = v.tensor_scalar, v.tensor_tensor, v.scalar_tensor_tensor
            chain = [0]

            def link(ins):
                ins.then_inc(dve_c, 1)
                chain[0] += 1
                dve.wait_ge(dve_c, chain[0])

            def weight_lo(g, j, width=GW):
                dve.wait_ge(hi_done, g * 8 + (j + 1))
                TTn(w_lo[j % 4][:, 0:2 * width], block_half(raw, j, width),
                    w_hi[j % 4][:, 0:2 * width].bitcast(f32), ALU.subtract).then_inc(lo_done, 1)

            def modulation(m, k, section, src, full, arrivals, first=False):
                dve.wait_ge(full, arrivals)
                if first:
                    dve.wait_ge(acc_init[section], 16)
                dve.wait_ge(mod_step, m + 1)
                out = acc[SECTION_ACC[section]][:, :]
                STT(out, src[:, :], c_act[:, bass.ds(k, 1)], out, ALU.mult, ALU.add).then_inc(mod_step, 1)

            def later_modulation(m):
                n = m - MOD_FIRST
                modulation(m, m % KT, m // KT, mod_raw[n % 2], mod_full[n % 2], 16 * (n // 2 + 1), m % KT == 0)

            def inverse_rms(n):
                dve.wait_ge(act_sq, 4 * TT * (n + 1))
                link(v.tensor_reduce(newton[:, :], ssq[:, n, :, :], AX.X, ALU.add))
                TS(mean_sq[:, :], newton[:, :], 1.0 / D, EPS, ALU.mult, ALU.add).then_inc(dve_ms, 1)
                dve.wait_ge(act_root, n + 1)
                link(v.reciprocal(rstd[:, :], root[:, :]))
                link(TTn(newton[:, :], rstd[:, :], rstd[:, :], ALU.mult))
                link(TTn(newton[:, :], newton[:, :], mean_sq[:, :], ALU.mult))
                link(TS(newton[:, :], newton[:, :], -0.5, 1.5, ALU.mult, ALU.add))
                TTn(rstd[:, :], rstd[:, :], newton[:, :], ALU.mult).then_inc(rstd_ok, 1)

            dve.wait_ge(c_sig, 1)
            TTn(c_act[:, :], c_tmp[:, :], c_col[:, :], ALU.mult).then_inc(mod_step, 1)

            def first_modulation(i, k, section, first=False):
                for r in range(4):
                    modulation(i * 4 + r, k * 4 + r, section, raw[r], raw_full[r], i * 16 + 16,
                               first and r == 0)

            first_modulation(0, 0, 0, first=True)
            with dve.Fori(1, 4) as i:
                first_modulation(i, i, 0)
            first_modulation(4, 0, 1, first=True)
            first_modulation(5, 1, 1)
            inverse_rms(0)
            first_modulation(6, 2, 1)
            first_modulation(7, 3, 1)
            dve.wait_ge(pe_mod, 1)
            v.tensor_copy(shift_h[:, :], aux[2][:, 0:KT]).then_inc(col_ok, 1)
            dve.wait_ge(pe_mod, 2)
            STT(scale_h[:, :], aux[2][:, KT:2 * KT], 1.0, n1[:, :], ALU.add, ALU.mult).then_inc(col_ok, 1)

            def split_h(n, source, ready):
                for b in range(KT // 2):
                    dve.wait_ge(h_ok, KT * n + 2 * b + 2)
                    src = source[b % 2][:, :].rearrange("p (k t) -> p k t", k=2)
                    v.tensor_copy(act_hi[:, 2 * b:2 * b + 2, :], src).then_inc(h_hi, 1)
                    dve.wait_ge(h_hi, KT // 2 * n + b + 1)
                    TTn(act_lo[:, 2 * b:2 * b + 2, :], src, act_hi[:, 2 * b:2 * b + 2, :].bitcast(f32),
                        ALU.subtract).then_inc(ready, 1)

            def taps():
                dve.wait_ge(evac_act, 2)
                link(TTn(conv_in[:, :, CONV_W - 1:], conv_in[:, :, CONV_W - 1:], conv_y[:, :, :], ALU.mult))
                yield
                for n in range(CONV_STEPS):
                    t, ct = divmod(n, CT)
                    x_t = conv_in[:, ct, t:t + S]
                    if t == 0:
                        TS(conv_y[:, ct, :], x_t, convw[:, ct, 0:1], convb[:, ct:ct + 1], ALU.mult, ALU.add)\
                            .then_inc(conv_sem, 1)
                    else:
                        dve.wait_ge(conv_sem, n - CT + 1)
                        STT(conv_y[:, ct, :], x_t, convw[:, ct, t:t + 1], conv_y[:, ct, :], ALU.mult, ALU.add)\
                            .then_inc(conv_sem, 1)
                    yield

            split_h(0, h_f, h_ready)
            dve.wait_ge(bias_out, 16)
            dve.wait_ge(h_ready, KT // 2)
            link(v.memset(conv_in[:, :, 0:CONV_W - 1], 0.0))
            conv = taps()
            m = MOD_FIRST

            for g in range(N_IN):
                for j in range(HALVES):
                    if g == 2 and j == 5:
                        next(conv)
                    if (g == 2 and j > 5) or g > 2:
                        for _ in range(2):
                            next(conv, None)
                    weight_lo(g, j, TAIL if g == 8 else GW)
                    if j % 2 and j // 2 < MOD_IN[g]:
                        later_modulation(m)
                        m += 1
                    if g == 9 and j == 4:
                        dve.wait_ge(evac_act, 9)
                        link(TTn(lf[0][:, :, :], val[:, :, COL_F:COL_F + NFOX],
                                 view(bf_b[:, :], [[0, TT], [1, NFOX]]), ALU.add))
                        STT(lf[1][:, :, :], lf[0][:, :, :], -1.0, lf[0][:, :, :], ALU.mult, ALU.max)\
                            .then_inc(lf_in, 1)
                    if g == 10 and j == 1:
                        e, r, r2, s = (lf[i][:, :, :] for i in (1, 2, 3, 4))
                        dve.wait_ge(lf_exp, 1)
                        link(TS(r, e, 2.0, None, ALU.add))
                        link(v.reciprocal(r, r))
                        link(TTn(r, r, e, ALU.mult))
                        link(TTn(r2, r, r, ALU.mult))
                        link(TS(s, r2, 1.0 / 15, None, ALU.mult))
                        for odd in (13, 11, 9, 7, 5, 3):
                            link(STT(s, s, 1.0 / odd, r2, ALU.add, ALU.mult))
                        link(STT(s, s, 1.0, r, ALU.add, ALU.mult))
                        link(TS(lf[0][:, :, :], lf[0][:, :, :], 0.0, None, ALU.min))
                        STT(log_f[:, :, :], s, -2.0, lf[0][:, :, :], ALU.mult, ALU.add).then_inc(lf_ok, 1)
                    if g == 10 and j == 3:
                        dve.wait_ge(gate_ok, 1)

            dve.wait_ge(f_ps, 1)
            v.tensor_copy(f_q[:, :, :], aux[0][:, 0:2 * NFOX].rearrange("p (t h) -> p t h", t=TT)).then_inc(f_sb, 1)
            dve.wait_ge(consts, 1)
            v.tensor_copy(neg_id_r[:, :], neg_id[:, :])
            for bank, base in ((aux[1], 0), (aux[2], HD)):
                part = slice(base, base + NFOX)
                link(v.tensor_copy(f_hi[part, :], bank[part, 0:S]))
                last = TTn(f_lo[part, :], bank[part, 0:S], f_hi[part, :].bitcast(f32), ALU.subtract)
            last.then_inc(f_sb, 1)
            dve.wait_ge(f_sb, 2)

            def bias_of(h, tt):
                n = (tt + 1) * P
                return view(bias_t[:, h, :], [[-1, n]], n - 1)

            def cmp_bias(parity, tt, count):
                at = S - 1 - (CMP_LEN - 1) if tt else P - 1 - (CMP_LEN - 1)
                return view(bias_t[:, parity, :], [[2 * S, NNSA // 2], [-CMP_STRIDE, count]], at)

            def compress_inputs():
                dve.wait_ge(evac_act, 8)
                for n, (dst, tokens, blocks) in enumerate(((0, 0, 16), (1, 16, 15))):
                    for odd in range(2):
                        src = z_t[odd * HD:(odd + 1) * HD, 18:21, :]
                        pos = view(pos_t[odd * HD:(odd + 1) * HD, :], [[0, 3], [0, blocks], [1, 16]], 16 * dst)
                        out = view(cmp_in[dst * HD:(dst + 1) * HD, odd:odd + 1, :],
                                   [[2 * S, 3], [16, blocks], [1, 16]])
                        last = TTn(out, view(src, [[S, 3], [16, blocks], [1, 16]], tokens), pos, ALU.add)
                last.then_inc(cmp_x, 1)

            def outputs(unit):
                a = 4 * unit
                dve.wait_ge(o_ready, a + 4)
                link(v.reciprocal(row_r[:, 2 * a:2 * a + 8], row_sum[:, 2 * a:2 * a + 8]))
                if a >= NFOX:
                    h = (a - NFOX) % NNSA
                    branch = 1 + (a - NFOX) // NNSA
                    g = view(gate[:, :, :], [[3, 4], [3 * NNSA, TT]], 3 * h + branch)
                    r = view(row_r[:, :], [[2, 4], [1, TT]], 2 * a)
                    link(TTn(r, r, g, ALU.mult))
                    at = NFOX * HD + h * HD
                else:
                    at = a * HD
                r = view(row_r[:, :], [[1, TT], [2, 4], [0, HD]], 2 * a)
                out = view(mix[:, :, :], [[(NFOX + NNSA) * HD, TT], [HD, 4], [1, HD]], at)
                bank = view(o_bank[unit % 2], [[4 * HD, TT], [HD, 4], [1, HD]])
                if a < 24:
                    TTn(out, bank, r, ALU.mult).then_inc(o_used, 1)
                else:
                    t = view(add_t[:, :], [[4 * HD, TT], [HD, 4], [1, HD]])
                    TTn(t, bank, r, ALU.mult).then_inc(o_used, 1)
                    dve.wait_ge(o_used, unit + 1)
                    link(TTn(out, out, t, ALU.add))

            for a in range(36 + 5):
                if a < 36:
                    sc, ps = score[a % 3], aux[a % 3]
                    dve.wait_ge(s_ready, a + 1)
                    if a >= 3:
                        dve.wait_ge(t_ready, a - 2)
                    if a < NFOX:
                        for tt, (at, n) in enumerate(((0, P), (P, S))):
                            link(STT(sc[:, at:at + n], ps[:, at:at + n], f_q[:, tt, a:a + 1], causal[:, S - n:S],
                                     ALU.add, ALU.add))
                            last = v.tensor_reduce(neg_max[:, 2 * a + tt:2 * a + tt + 1], sc[:, at:at + n],
                                                   AX.X, ALU.max, negate=True)
                    else:
                        if a == NFOX:
                            dve.wait_ge(bias_in, 16)
                        h = (a - NFOX) % NNSA
                        for tt, (at, n) in enumerate(((0, P), (P, S))):
                            last = v.tensor_tensor_reduce(
                                out=sc[:, at:at + n], in0=ps[:, at:at + n], in1=bias_of(h, tt), scale=-1.0,
                                scalar=3e38, op0=ALU.add, op1=ALU.min,
                                accum_out=neg_max[:, 2 * a + tt:2 * a + tt + 1])
                    last.then_inc(s_biased, 1)
                b = a - 2
                if 0 <= b < 36 and b % 2:
                    dve.wait_ge(t_ready, b + 1)
                    if b >= 3:
                        dve.wait_ge(o_ready, b - 1)
                    v.tensor_copy(prob_t[1][:, :], t_bank[1][:, 0:3 * P]).then_inc(t_dve, 1)
                if a >= 5 and (a - 5) % 4 == 3:
                    outputs((a - 5) // 4)
                if a in MOD_HEADS:
                    later_modulation(m)
                    m += 1
                if a == 11:
                    dve.wait_ge(pe_mod, 4)
                    v.tensor_copy(shift2[:, :], aux[3][:, 0:KT]).then_inc(col_ok, 1)
                if a == 2:
                    dve.wait_ge(ln_ps, 1)
                    link(TTn(conv_y[:, :, :], conv_y[:, :, :], view(aux[3][:, 0:S], [[0, CT], [1, S]]),
                             ALU.subtract))
                    TTn(conv_in[:, :, 0:S], conv_y[:, :, :], conv_y[:, :, :], ALU.mult).then_inc(ln_sq, 1)
                if a == 12:
                    dve.wait_ge(pe_half, 8 * N_IN)
                    compress_inputs()
                if a == 6:
                    dve.wait_ge(ln_ps, 2)
                    TS(var_b, aux[3][:, S:2 * S], EPS, None, ALU.add).then_inc(ln_var, 1)
                if a == 7:
                    dve.wait_ge(ln_root, 1)
                    link(v.reciprocal(inv_b, root_b))
                    link(TTn(newton_b, inv_b, inv_b, ALU.mult))
                    link(TTn(newton_b, newton_b, var_b, ALU.mult))
                    link(TS(newton_b, newton_b, -0.5, 1.5, ALU.mult, ALU.add))
                    link(TTn(inv_b, inv_b, newton_b, ALU.mult))
                    link(TTn(conv_y[:, :, :], conv_y[:, :, :], view(conv_in[:, 2, 0:S], [[0, CT], [1, S]]),
                             ALU.mult))
                    for ct in range(CT):
                        last = TS(conv_y[:, ct, :], conv_y[:, ct, :], lng[:, ct:ct + 1], lnb[:, ct:ct + 1],
                                  ALU.mult, ALU.add)
                    last.then_inc(ln_y, 1)
                if a == 10:
                    dve.wait_ge(ln_sig, 1)
                    link(TTn(conv_y[:, :, :], conv_y[:, :, :], conv_in[:, :, 0:S], ALU.mult))
                if a == 15:
                    link(v.memset(v_cmp_t[:, :, :], 0.0))
                    link(v.memset(s_cmp[:, :, :, :], NEG))
                    link(v.memset(p_cmp[:, :, :, 16:32], 0.0))
                    dve.wait_ge(cmp_ps, 1)
                    kc = aux[3][0:HD, 0:NKV * NCMP].rearrange("p (g n) -> p g n", g=NKV)
                    v.tensor_copy(k_cmp[0:HD, :, :], kc)
                    v.tensor_copy(k_cmp[HD:P, :, :], kc).then_inc(cmp_sb, 1)
                    for g in range(NKV):
                        last = v.tensor_copy(view(v_cmp_t[:, g, :], [[32, 4], [1, NCMP]]),
                                             view(aux[3][0:HD, :], [[0, 4], [1, NCMP]], HD + g * NCMP))
                    last.then_inc(cmp_sb, 1)
                if a == 19:
                    dve.wait_ge(cmp_ps, 2)
                    v.tensor_copy(v_cmp[:, :, :], aux[3][:, P:P + NKV * HD].rearrange("p (g d) -> p g d", g=NKV))\
                        .then_inc(cmp_sb, 1)
                if a == 23:
                    dve.wait_ge(cmp_ps, 3)
                    for odd in range(2):
                        bank = aux[0] if odd else aux[3]
                        for tt, count in enumerate((NCMP0, NCMP)):
                            at = (tt * NNSA + odd) * 16
                            last = TTn(view(s_cmp[:, :, :, :], [[32, NNSA // 2], [1, count]], at),
                                       view(bank[:, :], [[32, NNSA // 2], [1, count]], at),
                                       cmp_bias(odd, tt, count), ALU.add)
                    last.then_inc(cmp_sb, 1)
                    dve.wait_ge(cmp_sb, 4)
                    flat = s_cmp[:, :, :, :].rearrange("p t h n -> p (t h) n")
                    link(v.tensor_reduce(cmp_m[:, :], flat, AX.X, ALU.max))
                    TTn(flat, flat, view(cmp_m[:, :], [[1, TT * NNSA], [0, 16]]), ALU.subtract).then_inc(cmp_x, 1)
                if a == 27:
                    dve.wait_ge(cmp_exp, 1)
                    probs = view(p_cmp[:, :, :, :], [[32, TT * NNSA], [1, 16]])
                    link(v.tensor_reduce(cmp_m[:, :], probs, AX.X, ALU.add))
                    link(v.reciprocal(cmp_r[:, :], cmp_m[:, :]))
                    r3 = cmp_r[:, :].rearrange("p (t h) -> p t h", t=TT)
                    link(TTn(r3, r3, view(gate[:, :, :], [[3 * NNSA, TT], [3, NNSA]]), ALU.mult))
                    link(TS(cmp_r[:, 0:NNSA], cmp_r[:, 0:NNSA], seen[:, 0:1], None, ALU.mult))
                if a in (31, 35):
                    tt = (a - 31) // 4
                    dve.wait_ge(cmp_ps, 4 + tt)
                    v.tensor_copy(view(p_cmp_t, [[1, NKV * P]], tt * NKV * P), aux[3][:, 0:NKV * P])\
                        .then_inc(cmp_sb, 1)
            dve.wait_ge(cmp_ps, 6)
            for r in range(4):
                gated = view(cmp_r[:, :], [[NNSA, TT], [4, NKV], [0, HD]], r)
                t = view(add_t[:, :], [[NKV * HD, TT], [HD, NKV], [1, HD]])
                out = view(mix[:, :, :], [[(NFOX + NNSA) * HD, TT], [4 * HD, NKV], [1, HD]],
                           NFOX * HD + r * HD)
                link(TTn(t, view(aux[r][:, :], [[NKV * HD, TT], [HD, NKV], [1, HD]]), gated, ALU.mult))
                TTn(out, out, t, ALU.add).then_inc(mix_done, 1)
                dve.wait_ge(mix_done, r + 1)
            for b in range(8):
                dve.wait_ge(mt_hi, b + 1)
                src = (aux[b % 2][:, :].rearrange("p (k t) -> p k t", k=2) if b < 6
                       else conv_y[:, 2 * (b - 6):2 * (b - 6) + 2, :])
                TTn(act_lo[:, 2 * b:2 * b + 2, :], src, act_hi[:, 2 * b:2 * b + 2, :].bitcast(f32),
                    ALU.subtract).then_inc(mix_ready, 1)

            def gated(bank3, cols, done):
                gate3 = view(acc[0][:, cols], [[0, TT], [1, GW]])
                if done:
                    dve.wait_ge(x2_sum, done)
                TTn(upd3, bank3, gate3, ALU.mult).then_inc(evac_dve, 1)

            upd3 = upd[:, :].rearrange("p (t n) -> p t n", t=TT)
            bank3 = [pair[i][:, :].rearrange("p (t n) -> p t n", t=TT) for i in range(2)]

            def out_residual(i):
                dve.wait_ge(pe_half, 8 * (G_OUT + i + 1))
                if i == 0:
                    dve.wait_ge(x2_in, 16 * TT)
                    dve.wait_ge(gate_row, 4)
                cols = slice(i * GW, (i + 1) * GW)
                gated(bank3[(1 + i) % 2], cols, i)
                dve.wait_ge(evac_dve, i + 1)
                TTn(x2[:, :, cols], x2[:, :, cols], upd3, ALU.add).then_inc(x2_sum, 1)

            for i in range(4):
                for j in range(HALVES):
                    if j == 4 and i:
                        out_residual(i - 1)
                    weight_lo(G_OUT + i, j)
                    if j % 2 and j // 2 < MOD_OUT[i]:
                        later_modulation(m)
                        m += 1
            out_residual(3)
            dve.wait_ge(pe_mod, 5)
            STT(scale_h[:, :], aux[2][:, KT:2 * KT], 1.0, n2[:, :], ALU.add, ALU.mult).then_inc(col_ok, 1)
            inverse_rms(1)
            dve.wait_ge(rstd_ok, 2)
            for n in range(2 * TT):
                tt, cols = n % TT, slice(n // TT * (D // 2), (n // TT + 1) * (D // 2))
                TS(xn2[:, tt, cols], x2[:, tt, cols], rstd[:, tt:tt + 1], None, ALU.mult).then_inc(xn_ok, 1)
            split_h(1, h2_f, h2_ready)

            def square(q, i):
                tiles = slice(4 * i, 4 * i + 4)
                r3 = relu[:, :].rearrange("p (k t) -> p k t", k=4)
                dve.wait_ge(evac_act, q * 4 + (N_IN + i + 1))
                TTn(relu[:, :], relu[:, :], relu[:, :], ALU.mult).then_inc(u_step, 1)
                dve.wait_ge(u_step, q * 8 + (2 * i + 1))
                v.tensor_copy(u_hi[:, tiles, :], r3).then_inc(u_step, 1)
                dve.wait_ge(u_step, q * 8 + (2 * i + 2))
                TTn(u_lo[:, tiles, :], r3, u_hi[:, tiles, :].bitcast(f32), ALU.subtract).then_inc(u_ready, 1)

            def down_sum(q, cg, first=False):
                cols = slice(cg * GW, (cg + 1) * GW)
                dve.wait_ge(pe_half, q * 64 + 8 * (G_MLP + 4 + cg + 1))
                if first:
                    v.tensor_copy(y[:, :, cols], bank3[(1 + cg) % 2]).then_inc(evac_dve, 1)
                else:
                    dve.wait_ge(evac_dve, q * 4 + (cg + 1))
                    TTn(y[:, :, cols], y[:, :, cols], bank3[(1 + cg) % 2], ALU.add).then_inc(evac_dve, 1)

            def gate_y():
                dve.wait_ge(gate_row, 8)
                dve.wait_ge(evac_dve, 4 + 4 * (QUARTERS - 1))
                for cg in range(4):
                    cols = slice(cg * GW, (cg + 1) * GW)
                    link(TTn(y[:, :, cols], y[:, :, cols], view(acc[0][:, cols], [[0, TT], [1, GW]]), ALU.mult))
                    TTn(x2[:, :, cols], x2[:, :, cols], y[:, :, cols], ALU.add).then_inc(x2_sum, 1)
                    yield

            def down_last(cg):
                cols = slice(cg * GW, (cg + 1) * GW)
                done = 4 * QUARTERS + cg + 1
                dve.wait_ge(pe_half, 8 * (N_GROUPS - 4 + cg + 1))
                gated(bank3[(1 + cg) % 2], cols, 8 + cg)
                dve.wait_ge(evac_dve, done)
                TTn(x2[:, :, cols], x2[:, :, cols], upd3, ALU.add).then_inc(x2_sum, 1)
                dve.wait_ge(x2_sum, 8 + cg + 1)
                TTn(y[:, :, cols], x2[:, :, cols], view(acc[1][:, cols], [[0, TT], [1, GW]]), ALU.mult)\
                    .then_inc(y_gain, 1)

            def mlp_quarter(q, first=False, final=False):
                gating = gate_y()
                for i in range(8):
                    for j in range(HALVES):
                        if j == 4 and i >= 5:
                            if final:
                                down_last(i - 5)
                            else:
                                down_sum(q, i - 5, first)
                        if j == 4 and i == 0 and not first:
                            down_sum(q - 1, 3, isinstance(q, int) and q == 1)
                        if j == 5 and 1 <= i <= 4:
                            square(q, i - 1)
                        if final and (i, j) in ((4, 6), (4, 7), (5, 2), (5, 3)):
                            next(gating)
                        weight_lo(q * 8 + (G_MLP + i), j)
                        if i < 4 and j == 3:
                            modulation(q * 4 + (5 * KT + i), q * 4 + i, 5, mod_raw[i % 2], mod_full[i % 2],
                                       q * 32 + 16 * ((5 * KT - MOD_FIRST + i) // 2 + 1), first and i == 0)

            mlp_quarter(0, first=True)
            mlp_quarter(1)
            with dve.Fori(2, QUARTERS - 1) as q:
                mlp_quarter(q)
            dve.wait_ge(fg_in, 16)
            mlp_quarter(QUARTERS - 1, final=True)
            down_last(3)
            inverse_rms(2)
            dve.wait_ge(rstd_ok, 3)
            dve.wait_ge(y_gain, 4)
            for i in range(4):
                tt, cols = i // 2, slice(i % 2 * (D // 2), (i % 2 + 1) * (D // 2))
                TS(y_out[i][:, 0:D // 2], y[:, tt, cols], rstd[:, tt:tt + 1], None, ALU.mult).then_inc(y_ok, 1)


def t5_one_hot():
    n = np.arange(S)
    exact = NB // 2
    nf = np.maximum(n, 1).astype(np.float32)
    large = exact + (np.log(nf / np.float32(exact)) / np.float32(math.log(128 / exact))
                     * np.float32(NB - exact)).astype(np.int32)
    bucket = np.where(n < exact, n, np.minimum(large, NB - 1))
    return np.ascontiguousarray((np.arange(NB)[:, None] == bucket[None, :]).astype(np.float32))


def blocks(w):
    n = w.shape[1] // GW
    return w.reshape(4, 4, P, n, GW).transpose(3, 0, 2, 1, 4).reshape(n * 4, P, 4 * GW)


def by_partition(a, tiles):
    return np.ascontiguousarray(np.asarray(a).reshape(tiles, P).T)


def kernel(x, c, w_mod, b_mod, norm1_g, w_in, b_f, w_cmp_k, w_cmp_v, pos_cmp, conv_w, conv_b, conv_ln_g,
           conv_ln_b, w_out, norm2_g, w_mlp1, w_mlp2, rel_bias, final_g):
    import concourse.bacc as _bacc
    from concourse.bass_utils import run_bass_kernel_spmd as _run

    w_in = np.asarray(w_in)[0]
    names = ["fq", "fk", "fv", "f", "nq", "kc", "vc", "ks", "vs", "kw", "vw", "ng", "ca", "cg"]
    d_h, d_kv = NFOX * HD, NKV * HD
    sizes = [d_h, d_h, d_h, NFOX, NNSA * HD] + [d_kv] * 6 + [3 * NNSA, D_CONV, D_CONV]
    at = dict(zip(names, np.split(w_in, np.cumsum(sizes)[:-1], axis=1)))
    transposed = np.concatenate([at[n] for n in ("ca", "cg", "fq", "nq", "fk", "kc", "vc", "ks", "kw")], axis=1)
    straight = np.concatenate([at[n] for n in ("fv", "vs", "vw", "f", "ng")], axis=1)
    tail = straight[:, 2 * GW:]
    b_in = blocks(transposed)
    b_straight = blocks(straight[:, :2 * GW])
    w1, w2 = np.asarray(w_mlp1)[0], np.asarray(w_mlp2)[0]
    stream = [b_in, b_straight[:4], b_straight, blocks(np.asarray(w_out)[0])]
    for q in range(QUARTERS):
        stream += [blocks(w1[:, q * D:(q + 1) * D]), blocks(w2[q * D:(q + 1) * D])]
    w_cmp = [np.asarray(w)[0].reshape(2, CMP_STRIDE, HD, HD).transpose(0, 2, 1, 3) for w in (w_cmp_k, w_cmp_v)]
    host = {
        "x": np.asarray(x).reshape(S, D),
        "c": by_partition(c, KT),
        "w_mod": np.asarray(w_mod)[0].reshape(KT, P, 6, D).transpose(2, 0, 1, 3).reshape(6 * KT, P, D),
        "b_mod": np.asarray(b_mod).reshape(6, D),
        "norm1_g": by_partition(norm1_g, KT),
        "norm2_g": by_partition(norm2_g, KT),
        "final_g": np.asarray(final_g).reshape(1, D),
        "w_main": np.concatenate(stream),
        "w_tail": tail.reshape(4, 4, P, TAIL).transpose(0, 2, 1, 3).reshape(4, P, 4 * TAIL),
        "b_f": np.asarray(b_f).reshape(1, NFOX),
        "w_cmp_k": w_cmp[0],
        "w_cmp_v": w_cmp[1],
        "pos": np.asarray(pos_cmp)[0].T,
        "conv_w": np.asarray(conv_w)[0].reshape(CONV_W, CT, P).transpose(2, 1, 0),
        "conv_b": by_partition(conv_b, CT),
        "conv_ln_g": by_partition(conv_ln_g, CT),
        "conv_ln_b": by_partition(conv_ln_b, CT),
        "rel_bias": np.asarray(rel_bias),
        "bucket_one_hot": t5_one_hot(),
    }
    nc = _bacc.Bacc("TRN2", target_bir_lowering=False, num_devices=1)
    arrays, args = {}, []
    for name, a in host.items():
        a = np.ascontiguousarray(a)
        arrays[f"in_{name}"] = a
        args.append(nc.dram_tensor(f"in_{name}", a.shape, mybir.dt.from_np(a.dtype), kind="ExternalInput").ap())
    out = nc.dram_tensor("out", (S, D), mybir.dt.float32, kind="ExternalOutput").ap()
    order = ["x", "c", "w_mod", "b_mod", "norm1_g", "norm2_g", "final_g", "w_main", "w_tail", "b_f", "w_cmp_k",
             "w_cmp_v", "pos", "conv_w", "conv_b", "conv_ln_g", "conv_ln_b", "rel_bias", "bucket_one_hot"]
    by_name = dict(zip(host, args))
    build(nc, *[by_name[n] for n in order], out)
    r = _run(nc, [arrays], core_ids=[0])
    return r.results[0]["out"].reshape(1, S, D)
```

```python
import math
from contextlib import ExitStack

import numpy as np
import concourse.bass as bass
from concourse import mybir

P = 128
D = 2048
S = 256
TT = S // P
KT = D // P
FF = 4 * D
HD = 64
NFOX = 12
NNSA = 12
NKV = 3
NCMP = 15
NCMP0 = 7
CMP_STRIDE = 16
CMP_LEN = 32
CONV_W = 31
CT = 4
D_CONV = CT * P
GW = 512
TAIL = 176
NB = 32
NEG = -1e30
EPS = 1e-6
QUARTERS = 4
HALVES = 8
N_IN = 11
G_OUT = N_IN
G_MLP = G_OUT + 4
N_GROUPS = G_MLP + 8 * QUARTERS
VCOLS = 2 * GW + TAIL
COL_F = 1152
COL_G = COL_F + NFOX
BPAD = 384
VECTOR_TAPS = [18, 22, 26]
SCALAR_TAPS = [tap for tap in range(CONV_W) if tap not in VECTOR_TAPS]
SUMS = 4 + 8
UNITS = 2 * N_IN
UNIT_HALVES = 4
HALF_K = KT // 2
TAP_UNIT = 14
assert CONV_W == UNIT_HALVES * (UNITS - TAP_UNIT) - 1
SECTIONS = ["sh1", "sc1", "sh2", "g1", "sc2", "g2"]
SECTION_ACC = [0, 1, 0, 1, 0, 0]
MOD_FIRST = KT
MOD_AT = list(range(KT)) + list(range(20, 28))
MOD_IN = len(MOD_AT)
MOD_HEADS = [a for a in range(36) if a not in (9, 10, 11, 12, 13, 16, 24, 28)]
MOD_OUT = [4, 3, 3, 2]
assert MOD_FIRST + MOD_IN + len(MOD_HEADS) + sum(MOD_OUT) == 5 * KT


def view(ap, dims, shift=0):
    return bass.AP(ap.tensor, ap.offset + shift, [list(ap.ap[0])] + [list(d) for d in dims])


def build(nc, x_d, c_d, wmod_d, bmod_d, n1_d, n2_d, fg_d, main_d, tail_d, bf_d, wck_d, wcv_d, pos_d,
          convw_d, convb_d, lng_d, lnb_d, rel_d, onehot_d, out_d):
    f32, f32r = mybir.dt.float32, mybir.dt.float32r
    ALU, ACT, AX = mybir.AluOpType, mybir.ActivationFunctionType, mybir.AxisListType
    bias_scratch = nc.dram_tensor("bias_scratch", (NNSA, BPAD), f32, kind="Internal").ap()

    ctx = ExitStack()
    with ctx:
        def sb(name, shape, dt=f32, where=ctx):
            return where.enter_context(nc.sbuf_tensor(name, shape, dt))

        def sem(name):
            return ctx.enter_context(nc.semaphore(name))

        raw = [sb(f"raw{i}", [P, 4 * GW]) for i in range(4)]
        w_hi = [sb(f"w_hi{i}", [P, 2 * GW], f32r) for i in range(4)]
        w_lo = [sb(f"w_lo{i}", [P, 2 * GW], f32r) for i in range(4)]
        mod_raw = [sb(f"mod_raw{i}", [P, D]) for i in range(2)]
        acc = [sb(f"acc{i}", [P, D]) for i in range(2)]
        ident = sb("ident", [P, P])
        ones = sb("ones", [P, P])
        ones_conv = sb("ones_conv", [P, P])
        tri = sb("tri", [P, P])
        causal = sb("causal", [P, S])
        neg_id = sb("neg_id", [P, NFOX])
        neg_id_r = sb("neg_id_r", [P, NFOX], f32r)
        seen = sb("seen", [P, 1])
        c_col = sb("c_col", [P, KT])
        c_tmp = sb("c_tmp", [P, KT])
        c_act = sb("c_act", [P, KT])
        n1 = sb("n1", [P, KT])
        n2 = sb("n2", [P, KT])
        scale_h = sb("scale_h", [P, KT])
        shift_h = sb("shift_h", [P, KT])
        shift2 = sb("shift2", [P, KT])
        ssq = sb("ssq", [P, 3, TT, 4])
        mean_sq = sb("mean_sq", [P, TT])
        root = sb("root", [P, TT])
        rstd = sb("rstd", [P, TT])
        newton = sb("newton", [P, TT])
        bf_b = sb("bf_b", [P, NFOX])
        convw = sb("convw", [P, CT, CONV_W])
        convb = sb("convb", [P, CT])
        table = sb("table", [P, 3])
        lng = sb("lng", [P, CT])
        lnb = sb("lnb", [P, CT])
        pos_t = sb("pos_t", [P, CMP_LEN])
        rel_t = sb("rel_t", [NB, NNSA])

        region = ExitStack()
        act_hi = sb("act_hi", [P, KT, S], f32r, region)
        act_lo = sb("act_lo", [P, KT, S], f32r, region)
        region.close()
        region = ExitStack()
        bias_t = sb("bias_t", [P, NNSA, S], f32, region)
        wck = sb("wck", [P, CMP_STRIDE, HD], f32, region)
        wcv = sb("wcv", [P, CMP_STRIDE, HD], f32, region)
        cmp_in = sb("cmp_in", [P, 6, S], f32, region)
        v_cmp = sb("v_cmp", [P, NKV, 4 * HD], f32, region)
        k_cmp = sb("k_cmp", [P, NKV, 32], f32, region)
        region.close()
        hold = sb("hold", [P, 2 * KT * S])
        phase = ExitStack()
        x_a = sb("x_a", [P, TT, D], f32, phase)
        sq_a = sb("sq_a", [P, D], f32, phase)
        onehot = sb("onehot", [NB, S], f32, phase)
        bias_p = sb("bias_p", [NNSA, BPAD], f32, phase)
        gap = sb("gap", [P, 24 * S + TT * VCOLS + CT * (CONV_W - 1 + S) + CT * S - (3 * D + S + BPAD)], f32, phase)
        xn_t = sb("xn_t", [P, KT, S], f32, phase)
        h_f = [sb(f"h_f{i}", [P, 2 * S], f32, phase) for i in range(2)]
        phase.close()
        phase = ExitStack()
        z_t = sb("z_t", [P, 24, S], f32, phase)
        val = sb("val", [P, TT, VCOLS], f32, phase)
        conv_in = sb("conv_in", [P, CT, CONV_W - 1 + S], f32, phase)
        conv_y = sb("conv_y", [P, CT, S], f32, phase)
        k_swap = sb("k_swap", [P, 3, S], f32, phase)
        score = [sb(f"score{i}", [P, 3 * P], f32, phase) for i in range(3)]
        prob_t = [sb(f"prob_t{i}", [P, 3 * P], f32, phase) for i in range(2)]
        mix = sb("mix", [P, TT, NFOX * HD + NNSA * HD], f32, phase)
        add_t = sb("add_t", [P, TT * 4 * HD], f32, phase)
        neg_max = sb("neg_max", [P, 72], f32, phase)
        row_sum = sb("row_sum", [P, 72], f32, phase)
        row_r = sb("row_r", [P, 72], f32, phase)
        log_f = sb("log_f", [P, TT, NFOX], f32, phase)
        lf = [sb(f"lf{i}", [P, TT, NFOX], f32, phase) for i in range(5)]
        gate = sb("gate", [P, TT, 3 * NNSA], f32, phase)
        f_q = sb("f_q", [P, TT, NFOX], f32, phase)
        f_hi = sb("f_hi", [P, S], f32r, phase)
        f_lo = sb("f_lo", [P, S], f32r, phase)
        v_cmp_t = sb("v_cmp_t", [HD, NKV, P], f32, phase)
        cmp_m = sb("cmp_m", [P, TT * NNSA], f32, phase)
        cmp_r = sb("cmp_r", [P, TT * NNSA], f32, phase)
        phase.close()
        phase = ExitStack()
        x2 = sb("x2", [P, TT, D], f32, phase)
        upd = sb("upd", [P, TT * GW], f32, phase)
        y = sb("y", [P, TT, D], f32, phase)
        late = ExitStack()
        xn2 = sb("xn2", [P, TT, D], f32, late)
        h2_f = [sb(f"h2_f{i}", [P, 2 * S], f32, late) for i in range(2)]
        late.close()
        u_hi = sb("u_hi", [P, KT, S], f32r, phase)
        u_lo = sb("u_lo", [P, KT, S], f32r, phase)
        relu = sb("relu", [P, 4 * S], f32, phase)
        phase.close()
        y_out = [raw[i] for i in range(4)]
        conv_p = [mix[:, i, 0:CT * S].rearrange("p (k t) -> p k t", k=CT) for i in range(TT)]
        p_cmp_t = z_t[:, 18:21, :]
        p_cmp = z_t[:, 0:3, :].rearrange("p k t -> p (k t)").rearrange("p (t h n) -> p t h n", t=TT, h=NNSA)
        s_cmp = z_t[:, 3:5, :].rearrange("p k t -> p (k t)")[:, 0:TT * NNSA * 16]\
            .rearrange("p (t h n) -> p t h n", t=TT, h=NNSA)
        var_b, root_b, inv_b, newton_b = (conv_in[:, i, 0:S] for i in range(4))

        pair = [ctx.enter_context(nc.psum_tensor(f"pair{i}", [P, 2 * GW], f32)) for i in range(2)]
        aux = [ctx.enter_context(nc.psum_tensor(f"aux{i}", [P, GW], f32)) for i in range(4)]
        t_bank = [pair[1][:, 0:GW], pair[1][:, GW:2 * GW]]
        o_bank = [pair[0][:, 0:GW], pair[0][:, GW:2 * GW]]

        small_in = sem("small_in")
        x_in = sem("x_in")
        consts = sem("consts")
        raw_full = [sem(f"raw_full{i}") for i in range(4)]
        mod_full = [sem(f"mod_full{i}") for i in range(2)]
        hi_done = sem("hi_done")
        lo_done = sem("lo_done")
        pe_half = sem("pe_half")
        evac_act = sem("evac_act")
        evac_dve = sem("evac_dve")
        evac_add = sem("evac_add")
        conv_sig = sem("conv_sig")
        mod_mid = sem("mod_mid")
        mod_step = sem("mod_step")
        acc_zero = sem("acc_zero")
        acc_init = [sem(f"acc_init{i}") for i in range(6)]
        pe_mod = sem("pe_mod")
        c_sig = sem("c_sig")
        act_sq = sem("act_sq")
        act_root = sem("act_root")
        dve_ms = sem("dve_ms")
        rstd_ok = sem("rstd_ok")
        xn_ok = sem("xn_ok")
        xt_ps = sem("xt_ps")
        xt_ok = sem("xt_ok")
        col_ok = sem("col_ok")
        h_ok = sem("h_ok")
        h_ready = sem("h_ready")
        h2_ready = sem("h2_ready")
        mix_ready = sem("mix_ready")
        u_ready = sem("u_ready")
        dve_c = sem("dve_c")
        pool_c = sem("pool_c")
        bias_ps = sem("bias_ps")
        bias_row = sem("bias_row")
        bias_out = sem("bias_out")
        bias_in = sem("bias_in")
        cmp_w_in = sem("cmp_w_in")
        gate_row = sem("gate_row")
        conv_tap = sem("conv_tap")
        conv_sem = sem("conv_sem")
        ln_ps = sem("ln_ps")
        ln_root = sem("ln_root")
        ln_sig = sem("ln_sig")
        ln_sq = sem("ln_sq")
        ln_var = sem("ln_var")
        ln_y = sem("ln_y")
        lf_in = sem("lf_in")
        lf_exp = sem("lf_exp")
        gate_ok = sem("gate_ok")
        lf_ok = sem("lf_ok")
        f_ps = sem("f_ps")
        f_sb = sem("f_sb")
        s_ready = sem("s_ready")
        s_biased = sem("s_biased")
        p_ready = sem("p_ready")
        t_ready = sem("t_ready")
        t_act = sem("t_act")
        o_ready = sem("o_ready")
        o_used = sem("o_used")
        swap_ok = sem("swap_ok")
        cmp_x = sem("cmp_x")
        cmp_ps = sem("cmp_ps")
        cmp_sb = sem("cmp_sb")
        cmp_exp = sem("cmp_exp")
        mix_mul = sem("mix_mul")
        mix_done = sem("mix_done")
        mt_ps = sem("mt_ps")
        mt_hi = sem("mt_hi")
        h_hi = sem("h_hi")
        u_step = sem("u_step")
        x2_in = sem("x2_in")
        x2_sum = sem("x2_sum")
        fg_in = sem("fg_in")
        y_gain = sem("y_gain")
        y_ok = sem("y_ok")
        y_ok_act = sem("y_ok_act")
        y_out_s = sem("y_out_s")

        N_SMALL = 12

        def block_half(tensor, j, width):
            return tensor[(j // 2) % 4][:, (j % 2) * 2 * width:(j % 2 + 1) * 2 * width]

        def result_of(g, bank):
            by_feature = bank[:, :].rearrange("p (k t) -> p k t", k=4)
            if g == 0:
                return conv_in[:, :, CONV_W - 1:], by_feature
            if g == 1:
                return conv_y[:, :, :], by_feature
            if g < 8:
                return z_t[:, 4 * (g - 2):4 * (g - 1), :], by_feature
            at, width = {8: (2 * GW, TAIL), 9: (0, GW), 10: (GW, GW)}[g]
            return val[:, :, at:at + width], bank[:, :].rearrange("p (t n) -> p t n", t=TT)[:, :, 0:width]

        def final_part(i):
            return i // 2, slice(i % 2 * (D // 2), (i % 2 + 1) * (D // 2))

        QUERIES = (2, 3, 4)
        H_AT = [(9, 2), (9, 3), (10, 0), (10, 1)]

        block = ctx.enter_context(nc.Block())

        @block.sync
        def _(sp):
            def weights(g, q, source=None, tail=False):
                if isinstance(g, int) and g == 0:
                    sp.wait_ge(mod_step, MOD_FIRST - 4 + q + 2)
                else:
                    sp.wait_ge(lo_done, (g - 1) * 8 + 2 * q + 2)
                if source is None:
                    source = main_d[g * 4 + q, :, :]
                sp.dma_start(raw[q][:, 0:4 * (TAIL if tail else GW)], source).then_inc(raw_full[q], 16)

            def modulation(m, slot):
                if not (isinstance(m, int) and m < MOD_FIRST + 2):
                    sp.wait_ge(mod_step, m)
                sp.dma_start(mod_raw[slot][:, :], wmod_d[m, :, :]).then_inc(mod_full[slot], 16)

            for m in range(4):
                sp.dma_start(raw[m][:, :], wmod_d[m, :, :]).then_inc(raw_full[m], 16)

            def first_modulation(i):
                for r in range(4):
                    sp.wait_ge(mod_step, i * 4 + (r - 2))
                    sp.dma_start(raw[r][:, :], wmod_d[i * 4 + r, :, :]).then_inc(raw_full[r], 16)

            for tt in range(TT):
                sp.dma_start(x_a[:, tt, :], x_d[tt * P:(tt + 1) * P, :]).then_inc(x_in, 16)
            with sp.Fori(1, MOD_FIRST // 4) as i:
                first_modulation(i)
            m = MOD_FIRST
            for n in range(4 * N_IN):
                half, g = divmod(n // 2, N_IN)
                q = 2 * half + n % 2
                weights(n // 4, n % 4, tail_d[q, :, :] if g == 8 else main_d[g * 4 + q, :, :], g == 8)
                if n in MOD_AT:
                    modulation(m, m % 2)
                    m += 1
            for n in range(len(MOD_HEADS) + MOD_OUT[0]):
                modulation(m, m % 2)
                m += 1
                if n in (8, 12, 16, 20):
                    weights(G_OUT, n // 4 - 2)
            sp.wait_ge(mix_ready, 8)
            for tt in range(TT):
                sp.dma_start(x2[:, tt, :], x_d[tt * P:(tt + 1) * P, :]).then_inc(x2_in, 16)
            for i in range(1, 4):
                for q in range(4):
                    weights(G_OUT + i, q)
                    if q < MOD_OUT[i]:
                        modulation(m, m % 2)
                        m += 1

            def mlp_loads(q):
                for i in range(8):
                    for r in range(4):
                        weights(q * 8 + (G_MLP + i), r)
                        if i < 4 and r == 1:
                            modulation(q * 4 + (5 * KT + i), i % 2)

            mlp_loads(0)
            sp.wait_ge(evac_dve, 4)
            sp.dma_start(acc[1][:, :], fg_d.to_broadcast([P, D])).then_inc(fg_in, 16)
            with sp.Fori(1, QUARTERS) as q:
                mlp_loads(q)
            for i in range(4):
                tt, half = i // 2, i % 2
                sp.wait_ge(y_ok_act if i % 2 else y_ok, i // 2 + 1)
                sp.dma_start(out_d[tt * P:(tt + 1) * P, half * D // 2:(half + 1) * D // 2],
                             y_out[i][:, 0:D // 2]).then_inc(y_out_s, 16)
            sp.wait_ge(y_out_s, 4 * 16)

        @block.gpsimd
        def _(pool):
            n = 0

            def step(ins):
                nonlocal n
                ins.then_inc(pool_c, 1)
                n += 1
                pool.wait_ge(pool_c, n)

            step(nc.gpsimd.memset(ident[:, :], 0.0))
            step(nc.gpsimd.affine_select(out=ident[:, :], in_=ident[:, :], compare_op=ALU.not_equal, fill=1.0,
                                         base=0, pattern=[[-1, P]], channel_multiplier=1))
            step(nc.gpsimd.memset(ones[:, :], 1.0))
            step(nc.gpsimd.memset(ones_conv[:, :], 1.0 / D_CONV))
            step(nc.gpsimd.memset(tri[:, :], 1.0))
            step(nc.gpsimd.affine_select(out=tri[:, :], in_=tri[:, :], compare_op=ALU.is_ge, fill=0.0,
                                         base=0, pattern=[[1, P]], channel_multiplier=-1))
            step(nc.gpsimd.memset(causal[:, :], 0.0))
            step(nc.gpsimd.affine_select(out=causal[:, :], in_=causal[:, :], compare_op=ALU.is_ge, fill=NEG,
                                         base=P, pattern=[[-1, S]], channel_multiplier=1))
            step(nc.gpsimd.memset(neg_id[:, :], 0.0))
            for base in (0, HD):
                step(nc.gpsimd.affine_select(out=neg_id[:, :], in_=neg_id[:, :], compare_op=ALU.not_equal,
                                             fill=-1.0, base=-base, pattern=[[-1, NFOX]], channel_multiplier=1))
            step(nc.gpsimd.memset(seen[:, :], 1.0))
            step(nc.gpsimd.affine_select(out=seen[:, :], in_=seen[:, :], compare_op=ALU.is_ge, fill=0.0,
                                         base=-(CMP_LEN - 1), pattern=[[0, 1]], channel_multiplier=1))
            nc.gpsimd.memset(bias_p[:, :], NEG).then_inc(consts, 1)

            for s, a in enumerate(SECTION_ACC):
                if s >= 2:
                    pool.wait_ge(pe_mod, {2: 3, 3: 4, 4: 5, 5: 7}[s])
                nc.gpsimd.memset(acc[a][:, :], 0.0).then_inc(acc_zero, 1)
                pool.wait_ge(acc_zero, s + 1)
                pool.dma_start(acc[a][0:1, :], bmod_d[s:s + 1, :]).then_inc(acc_init[s], 16)

        @block.scalar
        def _(act):
            A = nc.scalar.activation

            loads = [(c_col[:, :], c_d), (n1[:, :], n1_d), (n2[:, :], n2_d),
                     (rel_t[:, :], rel_d), (onehot[:, :], onehot_d),
                     (bf_b[:, :], bf_d.to_broadcast([P, NFOX])), (convw[:, :, :], convw_d),
                     (convb[:, :], convb_d), (lng[:, :], lng_d), (lnb[:, :], lnb_d),
                     (pos_t[0:HD, :], pos_d), (pos_t[HD:P, :], pos_d)]
            for dst, src in loads:
                act.dma_start(dst, src).then_inc(small_in, 16)
            assert len(loads) == N_SMALL
            act.wait_ge(small_in, 16 * N_SMALL)
            A(c_tmp[:, :], c_col[:, :], ACT.Sigmoid).then_inc(c_sig, 1)

            def sqrt_table(n):
                act.wait_ge(c_sig, 1)
                A(table[:, n:n + 1], c_tmp[:, 0:1], ACT.Sqrt)

            sqrt_table(0)
            act.wait_ge(x_in, 16 * TT)
            for n in range(4 * TT):
                tt, cg = n % TT, n // TT
                A(sq_a[:, n * GW // 2:(n + 1) * GW // 2].bitcast(mybir.dt.bfloat16),
                  x_a[:, tt, cg * GW:(cg + 1) * GW], ACT.Square, accum_out=ssq[:, 0, tt, cg:cg + 1])\
                    .then_inc(act_sq, 1)
            act.wait_ge(dve_ms, 1)
            A(root[:, :], mean_sq[:, :], ACT.Sqrt).then_inc(act_root, 1)
            act.wait_ge(rstd_ok, 1)
            for tt in range(TT):
                A(x_a[:, tt, :], x_a[:, tt, :], ACT.Copy, scale=rstd[:, tt:tt + 1]).then_inc(xn_ok, 1)
            act.wait_ge(bias_ps, 1)
            act.wait_ge(consts, 1)
            A(bias_p[:, P - 1:P - 1 + S], aux[3][0:NNSA, 0:S], ACT.Copy).then_inc(bias_row, 1)
            act.wait_ge(bias_row, 1)
            act.dma_start(bias_scratch[:, :], bias_p[:, :]).then_inc(bias_out, 16)
            for b in range(KT // 2):
                act.wait_ge(xt_ps, b + 1)
                A(xn_t[:, 2 * b:2 * b + 2, :], aux[b % 2][:, :].rearrange("p (k t) -> p k t", k=2),
                  ACT.Copy).then_inc(xt_ok, 1)

            def weight_hi(g, j, width=GW, first=False):
                act.wait_ge(raw_full[j // 2], (g + (1 + MOD_FIRST // 4)) * 16)
                if not (first and j < 4):
                    act.wait_ge(pe_half, g * 8 + j - 3)
                A(w_hi[j % 4][:, 0:2 * width], block_half(raw, j, width), ACT.Copy).then_inc(hi_done, 1)

            def scale_shift(b):
                if b >= 2:
                    act.wait_ge(h_ready, b - 1)
                for k in (2 * b, 2 * b + 1):
                    A(h_f[b % 2][:, (k % 2) * S:(k % 2 + 1) * S], xn_t[:, k, :], ACT.Identity,
                      bias=shift_h[:, k:k + 1], scale=scale_h[:, k:k + 1]).then_inc(h_ok, 1)

            for j in range(2):
                weight_hi(0, j, first=True)
            act.wait_ge(col_ok, 2)
            for b in range(HALF_K // 2):
                scale_shift(b)
                if b < 2:
                    weight_hi(0, 2 + b, first=True)

            def evacuate(g):
                act.wait_ge(pe_half, UNIT_HALVES * (g + 1))
                dst, src = result_of(g, pair[g % 2])
                A(dst, src, ACT.Copy, scale=HD ** -0.5 if g in QUERIES else 1.0).then_inc(evac_act, 1)

            act.wait_ge(bias_out, 16)
            for u in range(UNITS):
                for j in range(UNIT_HALVES):
                    if j == 2 and 1 <= u <= N_IN:
                        evacuate(u - 1)
                    if u == 13 and j == 3:
                        act.wait_ge(evac_add, 2)
                        A(conv_y[:, :, :], conv_y[:, :, :], ACT.Sigmoid).then_inc(conv_sig, 1)
                    tap = UNIT_HALVES * (u - TAP_UNIT) + j - 1
                    if tap in SCALAR_TAPS:
                        n = SCALAR_TAPS.index(tap)
                        act.wait_ge(conv_sem, SCALAR_TAPS[n - 2] + 1 if n > 2 else 1)
                        for ct in range(CT):
                            dst = conv_y[:, ct, :] if tap == 0 else conv_p[n % 2][:, ct, :]
                            last = A(dst, conv_in[:, ct, tap:tap + S], ACT.Copy if tap else ACT.Identity,
                                     scale=convw[:, ct, tap:tap + 1], bias=0.0 if tap else convb[:, ct:ct + 1])
                        last.then_inc(conv_tap, 1)
                    if (u, j) in H_AT:
                        if (u, j) == H_AT[0]:
                            act.wait_ge(col_ok, 4)
                        scale_shift(HALF_K // 2 + H_AT.index((u, j)))
                    if u:
                        weight_hi(u // 2, u % 2 * UNIT_HALVES + j, TAIL if u % N_IN == 8 else GW)
                    if u == 21 and j == 0:
                        act.wait_ge(evac_add, 9)
                        A(gate[:, :, :], val[:, :, COL_G:COL_G + 3 * NNSA], ACT.Sigmoid)\
                            .then_inc(gate_ok, 1)
                        act.wait_ge(lf_in, 1)
                        A(lf[1][:, :, :], lf[1][:, :, :], ACT.Exp, scale=-1.0).then_inc(lf_exp, 1)
            act.wait_ge(pe_half, 8 * N_IN)
            act.wait_ge(bias_out, 16)
            diag = bass.AP(bias_scratch.tensor, bias_scratch.offset, [[1, P], [BPAD, NNSA], [1, S]])
            act.dma_start(bias_t[:, :, :], diag).then_inc(bias_in, 16)
            for h in range(2):
                act.dma_start(wck[h * HD:(h + 1) * HD, :, :], wck_d[h, :, :, :]).then_inc(cmp_w_in, 16)
                act.dma_start(wcv[h * HD:(h + 1) * HD, :, :], wcv_d[h, :, :, :]).then_inc(cmp_w_in, 16)
            def conv_norm(part):
                if part == 0:
                    act.wait_ge(ln_var, 1)
                    A(root_b, var_b, ACT.Sqrt).then_inc(ln_root, 1)
                else:
                    act.wait_ge(ln_y, 1)
                    A(conv_in[:, :, 0:S], conv_y[:, :, :], ACT.Sigmoid).then_inc(ln_sig, 1)

            def attend(a):
                if a < 36:
                    sign = 1.0 if a < NFOX else -1.0
                    act.wait_ge(s_biased, a + 1)
                    A(score[a % 3][:, 0:P], score[a % 3][:, 0:P], ACT.Exp, scale=sign,
                      bias=neg_max[:, 2 * a:2 * a + 1], accum_out=row_sum[:, 2 * a:2 * a + 1])
                    A(score[a % 3][:, P:3 * P], score[a % 3][:, P:3 * P], ACT.Exp, scale=sign,
                      bias=neg_max[:, 2 * a + 1:2 * a + 2], accum_out=row_sum[:, 2 * a + 1:2 * a + 2])\
                        .then_inc(p_ready, 1)
                b = a - 2
                if 0 <= b < 36:
                    act.wait_ge(t_ready, b + 1)
                    if b >= 2:
                        act.wait_ge(o_ready, b - 1)
                    A(prob_t[b % 2][:, :], t_bank[b % 2][:, 0:3 * P], ACT.Copy).then_inc(t_act, 1)

            for a in range(36 + 2):
                attend(a)
                if a >= 36:
                    for j in range(2):
                        weight_hi(G_OUT, 2 * (a - 36) + j)
                if a == 4:
                    act.wait_ge(evac_add, 8)
                    A(k_swap[HD:P, :, :], z_t[0:HD, 21:24, :], ACT.Copy).then_inc(swap_ok, 1)
                    A(k_swap[0:HD, :, :], z_t[HD:P, 21:24, :], ACT.Copy).then_inc(swap_ok, 1)
                if a == 7:
                    conv_norm(0)
                if a == 13:
                    conv_norm(1)
                if a == 26:
                    act.wait_ge(cmp_x, 3)
                    A(p_cmp[:, :, :, 0:16], s_cmp[:, :, :, :], ACT.Exp).then_inc(cmp_exp, 1)

            for b in range(8):
                if b < 6:
                    act.wait_ge(mt_ps, b + 1)
                    A(act_hi[:, 2 * b:2 * b + 2, :], aux[b % 2][:, :].rearrange("p (k t) -> p k t", k=2),
                      ACT.Copy).then_inc(mt_hi, 1)
                else:
                    if b == 6:
                        act.wait_ge(mt_ps, 6)
                    A(act_hi[:, 2 * b:2 * b + 2, :], conv_y[:, 2 * (b - 6):2 * (b - 6) + 2, :],
                      ACT.Copy).then_inc(mt_hi, 1)

            def squares(n, cg, sums, junk):
                act.wait_ge(x2_sum, sums)
                for tt in range(TT):
                    A(junk[tt][:, cg * GW:(cg + 1) * GW], x2[:, tt, cg * GW:(cg + 1) * GW], ACT.Square,
                      accum_out=ssq[:, n, tt, cg:cg + 1]).then_inc(act_sq, 1)

            junk = [xn2[:, tt, :] for tt in range(TT)]
            for i in range(4):
                for j in range(HALVES):
                    if j == 7 and i:
                        squares(1, i - 1, i, junk)
                    if j == 4 and i == 1:
                        act.wait_ge(pe_mod, 6)
                        for cg in range(4):
                            A(acc[1][:, cg * GW:(cg + 1) * GW], aux[cg][:, :], ACT.Copy).then_inc(gate_row, 1)
                    if i or j >= 4:
                        weight_hi(G_OUT + i, j)

            sqrt_table(1)
            for j in range(4):
                weight_hi(G_MLP, j)
            squares(1, 3, 4, junk)
            act.wait_ge(dve_ms, 2)
            A(root[:, :], mean_sq[:, :], ACT.Sqrt).then_inc(act_root, 1)
            act.wait_ge(col_ok, 6)
            for b in range(KT // 2):
                act.wait_ge(xt_ps, KT // 2 + b + 1)
                if b >= 2:
                    act.wait_ge(h2_ready, b - 1)
                for k in (2 * b, 2 * b + 1):
                    A(h2_f[b % 2][:, (k % 2) * S:(k % 2 + 1) * S], aux[b % 2][:, (k % 2) * S:(k % 2 + 1) * S],
                      ACT.Identity, bias=shift2[:, k:k + 1], scale=scale_h[:, k:k + 1]).then_inc(h_ok, 1)

            def mlp_quarter(q, first=False, final=False):
                for i in range(8):
                    g = q * 8 + (G_MLP + i)
                    for j in range(HALVES):
                        if j == 4 and 1 <= i <= 4:
                            act.wait_ge(pe_half, g * 8)
                            if not (first and i == 1):
                                act.wait_ge(u_ready, q * 4 + (i - 1))
                            A(relu[:, :], pair[i % 2][:, :], ACT.Relu).then_inc(evac_act, 1)
                        if j == 7 and final and i >= 5:
                            squares(2, i - 5, SUMS - 4 + (i - 4), mod_raw)
                        if j == 4 and final and i == 4:
                            act.wait_ge(pe_mod, 8)
                            for cg in range(4):
                                A(acc[0][:, cg * GW:(cg + 1) * GW], aux[cg][:, :], ACT.Copy)\
                                    .then_inc(gate_row, 1)
                        if not (first and i == 0 and j < 4):
                            weight_hi(g, j)

            mlp_quarter(0, first=True)
            with act.Fori(1, QUARTERS - 1) as q:
                mlp_quarter(q)
            mlp_quarter(QUARTERS - 1, final=True)
            sqrt_table(2)
            squares(2, 3, SUMS, mod_raw)
            act.wait_ge(dve_ms, 3)
            A(root[:, :], mean_sq[:, :], ACT.Sqrt).then_inc(act_root, 1)
            act.wait_ge(rstd_ok, 3)
            act.wait_ge(y_gain, 4)
            for i in (1, 3):
                tt, cols = final_part(i)
                A(y_out[i][:, 0:D // 2], y[:, tt, cols], ACT.Copy, scale=rstd[:, tt:tt + 1]).then_inc(y_ok_act, 1)

        @block.tensor
        def _(pe):
            mm = nc.tensor.matmul

            def transposed_group(g, par, ready, reach, halves=HALVES, k0=0):
                for j in range(halves):
                    if ready is not None:
                        pe.wait_ge(ready, reach(j))
                    pe.wait_ge(lo_done, g * halves + (j + 1))
                    for kk in range(2):
                        k = k0 + 2 * j + kk
                        begin, end = 2 * j + kk == 0, 2 * j + kk == 2 * halves - 1
                        for m in range(4):
                            out = pair[par][:, m * S:(m + 1) * S]
                            cols = slice(kk * GW + m * P, kk * GW + (m + 1) * P)
                            hi, lo = w_hi[j % 4][:, cols], w_lo[j % 4][:, cols]
                            mm(out, hi, act_hi[:, k, :], start=begin and m % 2 == 0, stop=False,
                               skip_group_check=True)
                            mm(out, hi, act_lo[:, k, :], start=False, stop=False, skip_group_check=True)
                            last = mm(out, lo, act_hi[:, k, :], start=False, stop=end,
                                      skip_group_check=True)
                    last.then_inc(pe_half, 1)

            def straight_group(g, par, a_hi, a_lo, ready, reach, width=GW, halves=HALVES, k0=0):
                for j in range(halves):
                    if ready is not None:
                        pe.wait_ge(ready, reach(j))
                    pe.wait_ge(lo_done, g * halves + (j + 1))
                    for kk in range(2):
                        k = k0 + 2 * j + kk
                        begin, end = 2 * j + kk == 0, 2 * j + kk == 2 * halves - 1
                        for tt in range(TT):
                            out = pair[par][:, tt * GW:tt * GW + width]
                            cols = slice(kk * width, (kk + 1) * width)
                            hi, lo = w_hi[j % 4][:, cols], w_lo[j % 4][:, cols]
                            t_hi, t_lo = a_hi[:, k, tt * P:(tt + 1) * P], a_lo[:, k, tt * P:(tt + 1) * P]
                            mm(out, t_hi, hi, start=begin, stop=False)
                            mm(out, t_hi, lo, start=False, stop=False)
                            last = mm(out, t_lo, hi, start=False, stop=end)
                    last.then_inc(pe_half, 1)

            def columns(a, bank, at, tiles=range(KT)):
                for k in tiles:
                    last = mm(bank[:, at + k:at + k + 1], acc[a][:, k * P:(k + 1) * P], ones[:, 0:1],
                              start=True, stop=True)
                last.then_inc(pe_mod, 1)

            def rows(a, banks):
                for cg in range(4):
                    last = mm(banks[cg], ones[:, :], acc[a][:, cg * GW:(cg + 1) * GW], start=True, stop=True)
                last.then_inc(pe_mod, 1)

            pe.wait_ge(small_in, 16 * N_SMALL)
            mm(aux[3][0:NNSA, 0:S], rel_t[:, :], onehot[:, :], start=True, stop=True).then_inc(bias_ps, 1)
            pe.wait_ge(consts, 1)
            pe.wait_ge(xn_ok, TT)
            for b in range(KT // 2):
                if b >= 2:
                    pe.wait_ge(xt_ok, b - 1)
                for kk in range(2):
                    for tt in range(TT):
                        k = 2 * b + kk
                        last = nc.tensor.transpose(aux[b % 2][:, kk * S + tt * P:kk * S + (tt + 1) * P],
                                                   x_a[:, tt, k * P:(k + 1) * P], ident[:, :])
                last.then_inc(xt_ps, 1)
            first_tiles, last_tiles = range(HALF_K), range(HALF_K, KT)
            pe.wait_ge(mod_step, 8 + 1)
            columns(0, aux[2], 0, first_tiles)
            pe.wait_ge(mod_step, 16 + 1)
            columns(1, aux[2], KT, first_tiles)

            def unit(u, par, half, group=straight_group, width=GW, ready=False):
                h_at = (h_ready, lambda j: half * UNIT_HALVES + j + 1) if ready else (None, None)
                extra = dict(halves=UNIT_HALVES, k0=half * HALF_K)
                if group is straight_group:
                    extra["width"] = width
                group(u, par, *([] if group is transposed_group else [act_hi, act_lo]), *h_at, **extra)

            unit(0, 0, 0, transposed_group, ready=True)
            unit(1, 1, 0, transposed_group)
            with pe.Fori(1, 4) as i:
                for par in range(2):
                    pe.wait_ge(evac_act, i * 2 + (par - 1))
                    unit(i * 2 + par, par, 0, transposed_group)
            for u in range(8, N_IN):
                if u == 9:
                    pe.wait_ge(mod_step, 2 * KT + 1)
                    pe.wait_ge(col_ok, 2)
                    columns(0, aux[2], 0, last_tiles)
                    columns(1, aux[2], KT, last_tiles)
                pe.wait_ge(evac_act, u - 1)
                unit(u, u % 2, 0, width=TAIL if u == 8 else GW)
            for u in (N_IN, N_IN + 1):
                pe.wait_ge(evac_act, u - 1)
                unit(u, u % 2, 1, transposed_group, ready=u == N_IN)
            with pe.Fori(0, 3) as i:
                for par in range(2):
                    pe.wait_ge(evac_add, i * 2 + (par + 1))
                    unit(i * 2 + (13 + par), (13 + par) % 2, 1, transposed_group)
            for u in (19, 20, 21):
                pe.wait_ge(evac_add, u - 12)
                unit(u, u % 2, 1, width=TAIL if u == 19 else GW)

            pe.wait_ge(lf_ok, 1)
            pe.wait_ge(col_ok, 4)
            mm(aux[0][:, 0:NFOX], tri[:, :], log_f[:, 0, :], start=True, stop=True)
            mm(aux[0][:, NFOX:2 * NFOX], ones[:, :], log_f[:, 0, :], start=True, stop=False)
            mm(aux[0][:, NFOX:2 * NFOX], tri[:, :], log_f[:, 1, :], start=False, stop=True)
            for n, base in enumerate((0, HD)):
                out = aux[1 + n][base:base + NFOX, 0:S]
                mm(out[:, 0:P], log_f[:, 0, :], tri[:, :], start=True, stop=True)
                mm(out[:, P:S], log_f[:, 0, :], ones[:, :], start=True, stop=False)
                last = mm(out[:, P:S], log_f[:, 1, :], tri[:, :], start=False, stop=True)
            last.then_inc(f_ps, 1)
            pe.wait_ge(f_sb, 2)

            def key_of(a, base):
                if a < NFOX:
                    return z_t[base:base + HD, 12 + a // 2, :]
                n = (a - NFOX) // NNSA * NKV + (a - NFOX) % NNSA // 4
                if n % 2 == a % 2:
                    return z_t[base:base + HD, 21 + n // 2, :]
                return k_swap[base:base + HD, n // 2, :]

            def scores(a):
                base = HD * (a % 2)
                out = aux[a % 3]
                query = z_t[base:base + HD, a // 2 if a < NFOX else 6 + (a - NFOX) % NNSA // 2, :]
                key = key_of(a, base)
                if a == 0:
                    pe.wait_ge(evac_add, 8)
                if a >= 3:
                    pe.wait_ge(s_biased, a - 2)
                if a == NFOX:
                    pe.wait_ge(swap_ok, 2)
                for tt, (at, n) in enumerate(((0, P), (P, S))):
                    last = mm(out[:, at:at + n], query[:, tt * P:(tt + 1) * P], key[:, 0:n], start=True,
                              stop=a >= NFOX)
                    if a < NFOX:
                        pick = neg_id_r[base:base + NFOX, a:a + 1].to_broadcast([NFOX, P])
                        mm(out[:, at:at + n], pick, f_hi[base:base + NFOX, 0:n], start=False, stop=False)
                        last = mm(out[:, at:at + n], pick, f_lo[base:base + NFOX, 0:n], start=False, stop=True)
                last.then_inc(s_ready, 1)

            def transposes(a):
                pe.wait_ge(p_ready, a + 1)
                if a == 0:
                    pe.wait_ge(evac_add, N_IN)
                if a >= 2:
                    pe.wait_ge(t_act, a - 1)
                for n in range(3):
                    last = nc.tensor.transpose(t_bank[a % 2][:, n * P:(n + 1) * P],
                                               score[a % 3][:, n * P:(n + 1) * P], ident[:, :])
                last.then_inc(t_ready, 1)

            def outputs(a):
                pe.wait_ge(t_act, a + 1)
                unit, r = a // 4, a % 4
                if r == 0 and unit >= 2:
                    pe.wait_ge(o_used, unit - 1)
                at = a * HD if a < NFOX else NFOX * HD + ((a - NFOX) // NNSA * NKV + (a - NFOX) % NNSA // 4) * HD
                out = [o_bank[unit % 2][:, (tt * 4 + r) * HD:(tt * 4 + r + 1) * HD] for tt in range(TT)]
                pt = prob_t[a % 2]
                mm(out[0], pt[:, 0:P], val[:, 0, at:at + HD], start=True, stop=True)
                mm(out[1], pt[:, P:2 * P], val[:, 0, at:at + HD], start=True, stop=False)
                mm(out[1], pt[:, 2 * P:3 * P], val[:, 1, at:at + HD], start=False, stop=True).then_inc(o_ready, 1)

            for a in range(36 + 3):
                if a == 2:
                    pe.wait_ge(conv_sem, CONV_W)
                    for ct in range(CT):
                        last = mm(aux[3][:, 0:S], ones_conv[:, :], conv_y[:, ct, :], start=ct == 0,
                                  stop=ct == CT - 1)
                    last.then_inc(ln_ps, 1)
                if a == 5:
                    pe.wait_ge(ln_sq, 1)
                    for ct in range(CT):
                        last = mm(aux[3][:, S:2 * S], ones_conv[:, :], conv_in[:, ct, 0:S], start=ct == 0,
                                  stop=ct == CT - 1)
                    last.then_inc(ln_ps, 1)
                if a == 14:
                    pe.wait_ge(ln_var, 1)
                    pe.wait_ge(cmp_x, 2)
                    pe.wait_ge(cmp_w_in, 4 * 16)
                    for n, w in enumerate((wck, wcv)):
                        for l in range(CMP_STRIDE):
                            tokens = view(cmp_in[:, 3 * n:3 * n + 3, :],
                                          [[S, NKV], [CMP_STRIDE, NCMP]], l)
                            last = mm(aux[3][0:HD, HD * n:HD * n + NKV * NCMP], w[:, l, :], tokens,
                                      start=l == 0, stop=l == CMP_STRIDE - 1)
                    last.then_inc(cmp_ps, 1)
                if a == 18:
                    pe.wait_ge(cmp_sb, 2)
                    for g in range(NKV):
                        last = nc.tensor.transpose(aux[3][:, P + g * HD:P + (g + 1) * HD], v_cmp_t[:, g, :],
                                                   ident[0:HD, 0:HD])
                    last.then_inc(cmp_ps, 1)
                if a == 21:
                    pe.wait_ge(mod_step, 3 * KT + 1)
                    pe.wait_ge(cmp_sb, 3)
                    columns(0, aux[3], 0)
                if a == 24:
                    pe.wait_ge(cmp_sb, 3)
                    pe.wait_ge(col_ok, 5)
                    for tt in range(TT):
                        for n in range(NNSA // 2):
                            at = (tt * NNSA + 2 * n) * 16
                            last = mm(aux[3][:, at:at + 32], z_t[:, 6 + n, tt * P:(tt + 1) * P],
                                      k_cmp[:, n // 2, :], start=True, stop=True)
                    last.then_inc(cmp_ps, 1)
                if a in (30, 34):
                    tt = (a - 30) // 4
                    pe.wait_ge(cmp_exp, 1)
                    if tt:
                        pe.wait_ge(cmp_sb, 5)
                    for g in range(NKV):
                        last = nc.tensor.transpose(
                            aux[3][:, g * P:(g + 1) * P],
                            p_cmp[:, tt, 4 * g:4 * g + 4, :].rearrange("p h n -> p (h n)"), ident[:, :])
                    last.then_inc(cmp_ps, 1)
                if a < 36:
                    scores(a)
                if 0 <= a - 2 < 36:
                    transposes(a - 2)
                if a == 37:
                    pe.wait_ge(cmp_sb, 6)
                    pe.wait_ge(s_biased, 36)
                    for tt in range(TT):
                        for g in range(NKV):
                            n = tt * NKV + g
                            last = mm(aux[n // 2][:, n % 2 * S:(n % 2 + 1) * S],
                                      view(p_cmp_t, [[1, P]], n * P), v_cmp[:, g, :], start=True, stop=True)
                    last.then_inc(cmp_ps, 1)
                if a >= 3:
                    outputs(a - 3)
            pe.wait_ge(mix_done, 3)
            for b in range(6):
                if b >= 2:
                    pe.wait_ge(mix_ready, b - 1)
                for kk in range(2):
                    for tt in range(TT):
                        k = 2 * b + kk
                        last = nc.tensor.transpose(aux[b % 2][:, kk * S + tt * P:kk * S + (tt + 1) * P],
                                                   mix[:, tt, k * P:(k + 1) * P], ident[:, :])
                last.then_inc(mt_ps, 1)

            for i in range(4):
                if i >= 2:
                    pe.wait_ge(evac_dve, i - 1)
                straight_group(G_OUT + i, (1 + i) % 2, act_hi, act_lo, mix_ready, lambda j: j + 1)
                if i == 0:
                    pe.wait_ge(mod_step, 4 * KT + 1)
                    rows(1, [aux[cg][:, :] for cg in range(4)])
            pe.wait_ge(mod_step, 5 * KT + 1)
            pe.wait_ge(gate_row, 4)
            columns(0, aux[2], KT)
            for b in range(KT // 2):
                pe.wait_ge(xn_ok, TT + (TT if b < 4 else 2 * TT))
                if b >= 2:
                    pe.wait_ge(h_ok, 2 * (KT // 2 + b - 1))
                for kk in range(2):
                    for tt in range(TT):
                        k = 2 * b + kk
                        last = nc.tensor.transpose(aux[b % 2][:, kk * S + tt * P:kk * S + (tt + 1) * P],
                                                   xn2[:, tt, k * P:(k + 1) * P], ident[:, :])
                last.then_inc(xt_ps, 1)

            def mlp_up(q):
                with pe.Fori(0, 2) as i:
                    for par in range(2):
                        pe.wait_ge(evac_dve, q * 4 + (3 + par))
                        pe.wait_ge(evac_act, q * 4 + i * 2 + (N_IN - 1 + par))
                        transposed_group(q * 8 + i * 2 + (G_MLP + par), (1 + par) % 2, h2_ready, lambda j: j + 1)

            def mlp_down(q, i, par):
                pe.wait_ge(evac_act, q * 4 + (N_IN + 3 + par))
                pe.wait_ge(evac_dve, q * 4 + i + 3)
                straight_group(q * 8 + i + (G_MLP + 4), (1 + par) % 2, u_hi, u_lo, u_ready,
                               lambda j: q * 4 + (j // 2 + 1))

            with pe.Fori(0, QUARTERS - 1) as q:
                mlp_up(q)
                with pe.Fori(0, 2) as i:
                    for par in range(2):
                        mlp_down(q, i * 2 + par, par)
            mlp_up(QUARTERS - 1)
            pe.wait_ge(mod_step, 6 * KT + 1)
            rows(0, [aux[cg][:, :] for cg in range(4)])
            for i in range(4):
                mlp_down(QUARTERS - 1, i, i % 2)

        @block.vector
        def _(dve):
            v = nc.vector
            TS, TTn, STT = v.tensor_scalar, v.tensor_tensor, v.scalar_tensor_tensor
            chain = [0]

            def link(ins):
                ins.then_inc(dve_c, 1)
                chain[0] += 1
                dve.wait_ge(dve_c, chain[0])

            def weight_lo(g, j, width=GW):
                dve.wait_ge(hi_done, g * 8 + (j + 1))
                TTn(w_lo[j % 4][:, 0:2 * width], block_half(raw, j, width),
                    w_hi[j % 4][:, 0:2 * width].bitcast(f32), ALU.subtract).then_inc(lo_done, 1)

            def early_modulation(m, src, full, arrivals):
                half, section, n = m // KT, m // 8 % 2, m % 8
                dve.wait_ge(full, arrivals)
                if half == 0 and n == 0:
                    dve.wait_ge(acc_init[section], 16)
                out = acc[section][:, half * (D // 2):(half + 1) * (D // 2)]
                dve.wait_ge(mod_step, m + 1)
                STT(out, src[:, 0:D // 2], c_act[:, 2 * n:2 * n + 1], out, ALU.mult, ALU.add).then_inc(mod_mid, 1)
                dve.wait_ge(mod_mid, m + 1)
                STT(out, src[:, D // 2:D], c_act[:, 2 * n + 1:2 * n + 2], out, ALU.mult, ALU.add)\
                    .then_inc(mod_step, 1)

            def modulation(m, k, section, src, full, arrivals, first=False):
                dve.wait_ge(full, arrivals)
                if first:
                    dve.wait_ge(acc_init[section], 16)
                dve.wait_ge(mod_step, m + 1)
                out = acc[SECTION_ACC[section]][:, :]
                STT(out, src[:, :], c_act[:, bass.ds(k, 1)], out, ALU.mult, ALU.add).then_inc(mod_step, 1)

            def later_modulation(m):
                n = m - MOD_FIRST
                modulation(m, m % KT, m // KT, mod_raw[n % 2], mod_full[n % 2], 16 * (n // 2 + 1), m % KT == 0)

            def inverse_rms(n):
                dve.wait_ge(act_sq, 4 * TT * (n + 1))
                link(v.tensor_reduce(newton[:, :], ssq[:, n, :, :], AX.X, ALU.add))
                TS(mean_sq[:, :], newton[:, :], 1.0 / D, EPS, ALU.mult, ALU.add).then_inc(dve_ms, 1)
                dve.wait_ge(act_root, n + 1)
                link(v.reciprocal(rstd[:, :], root[:, :]))
                link(TTn(newton[:, :], rstd[:, :], rstd[:, :], ALU.mult))
                link(TTn(newton[:, :], newton[:, :], mean_sq[:, :], ALU.mult))
                link(TS(newton[:, :], newton[:, :], -0.5, 1.5, ALU.mult, ALU.add))
                TTn(rstd[:, :], rstd[:, :], newton[:, :], ALU.mult).then_inc(rstd_ok, 1)

            dve.wait_ge(c_sig, 1)
            TTn(c_act[:, :], c_tmp[:, :], c_col[:, :], ALU.mult).then_inc(mod_step, 1)

            for m in range(MOD_FIRST):
                if m == 10:
                    inverse_rms(0)
                early_modulation(m, raw[m % 4], raw_full[m % 4], 16 * (m // 4 + 1))
            first_tiles, last_tiles = slice(0, HALF_K), slice(HALF_K, KT)

            def scale_shift(tiles):
                shift, scale = (slice(at + tiles.start, at + tiles.stop) for at in (0, KT))
                v.tensor_copy(shift_h[:, tiles], aux[2][:, shift]).then_inc(col_ok, 1)
                STT(scale_h[:, tiles], aux[2][:, scale], 1.0, n1[:, tiles], ALU.add, ALU.mult).then_inc(col_ok, 1)

            for j in range(2):
                weight_lo(0, j)
            dve.wait_ge(pe_mod, 2)
            scale_shift(first_tiles)

            def split_h(n, source, ready, pairs=range(KT // 2)):
                for b in pairs:
                    dve.wait_ge(h_ok, KT * n + 2 * b + 2)
                    src = source[b % 2][:, :].rearrange("p (k t) -> p k t", k=2)
                    v.tensor_copy(act_hi[:, 2 * b:2 * b + 2, :], src).then_inc(h_hi, 1)
                    dve.wait_ge(h_hi, KT // 2 * n + b + 1)
                    TTn(act_lo[:, 2 * b:2 * b + 2, :], src, act_hi[:, 2 * b:2 * b + 2, :].bitcast(f32),
                        ALU.subtract).then_inc(ready, 1)

            def add_tap(tap):
                if tap < 0:
                    dve.wait_ge(conv_sig, 1)
                    TTn(conv_in[:, :, CONV_W - 1:], conv_in[:, :, CONV_W - 1:], conv_y[:, :, :], ALU.mult)\
                        .then_inc(conv_sem, 1)
                elif tap in VECTOR_TAPS:
                    dve.wait_ge(conv_sem, tap)
                    for ct in range(CT):
                        last = STT(conv_y[:, ct, :], conv_in[:, ct, tap:tap + S], convw[:, ct, tap:tap + 1],
                                   conv_y[:, ct, :], ALU.mult, ALU.add)
                    last.then_inc(conv_sem, 1)
                elif tap > 0:
                    n = SCALAR_TAPS.index(tap)
                    dve.wait_ge(conv_tap, n + 1)
                    dve.wait_ge(conv_sem, tap)
                    TTn(conv_y[:, :, :], conv_y[:, :, :], conv_p[n % 2], ALU.add).then_inc(conv_sem, 1)

            def add_result(u):
                dve.wait_ge(pe_half, UNIT_HALVES * (u + 1))
                dve.wait_ge(evac_act, u - N_IN + 1)
                dst, src = result_of(u - N_IN, pair[u % 2])
                if u - N_IN in QUERIES:
                    STT(dst, src, HD ** -0.5, dst, ALU.mult, ALU.add).then_inc(evac_add, 1)
                else:
                    TTn(dst, dst, src, ALU.add).then_inc(evac_add, 1)

            for b in range(HALF_K // 2):
                split_h(0, h_f, h_ready, [b])
                if b < 2:
                    weight_lo(0, 2 + b)
            dve.wait_ge(bias_out, 16)
            link(v.memset(conv_in[:, :, 0:CONV_W - 1], 0.0))
            m = MOD_FIRST

            for u in range(UNITS):
                for j in range(UNIT_HALVES):
                    if j == 2 and u > N_IN:
                        add_result(u - 1)
                    if (u, j) == (TAP_UNIT, 0):
                        add_tap(-1)
                    if u:
                        weight_lo(u // 2, u % 2 * UNIT_HALVES + j, TAIL if u % N_IN == 8 else GW)
                    if UNIT_HALVES * (u - TAP_UNIT) + j - 1 > 0:
                        add_tap(UNIT_HALVES * (u - TAP_UNIT) + j - 1)
                    if j % 2 and 2 * u + j // 2 in MOD_AT:
                        i = m - MOD_FIRST
                        if m < 2 * KT:
                            early_modulation(m, mod_raw[i % 2], mod_full[i % 2], 16 * (i // 2 + 1))
                        else:
                            later_modulation(m)
                        m += 1
                    if (u, j) == (9, 1):
                        dve.wait_ge(pe_mod, 4)
                        scale_shift(last_tiles)
                    if (u, j) in H_AT:
                        b = HALF_K // 2 + H_AT.index((u, j))
                        split_h(0, h_f, h_ready, [b])
                    if u == 20 and j == 3:
                        dve.wait_ge(evac_add, 9)
                        link(TTn(lf[0][:, :, :], val[:, :, COL_F:COL_F + NFOX],
                                 view(bf_b[:, :], [[0, TT], [1, NFOX]]), ALU.add))
                        STT(lf[1][:, :, :], lf[0][:, :, :], -1.0, lf[0][:, :, :], ALU.mult, ALU.max)\
                            .then_inc(lf_in, 1)
                    if u == 21 and j == 2:
                        e, r, r2, s = (lf[i][:, :, :] for i in (1, 2, 3, 4))
                        dve.wait_ge(lf_exp, 1)
                        link(TS(r, e, 2.0, None, ALU.add))
                        link(v.reciprocal(r, r))
                        link(TTn(r, r, e, ALU.mult))
                        link(TTn(r2, r, r, ALU.mult))
                        link(TS(s, r2, 1.0 / 15, None, ALU.mult))
                        for odd in (13, 11, 9, 7, 5, 3):
                            link(STT(s, s, 1.0 / odd, r2, ALU.add, ALU.mult))
                        link(STT(s, s, 1.0, r, ALU.add, ALU.mult))
                        link(TS(lf[0][:, :, :], lf[0][:, :, :], 0.0, None, ALU.min))
                        STT(log_f[:, :, :], s, -2.0, lf[0][:, :, :], ALU.mult, ALU.add).then_inc(lf_ok, 1)
                    if u == 21 and j == 3:
                        dve.wait_ge(gate_ok, 1)
            add_result(UNITS - 1)

            dve.wait_ge(f_ps, 1)
            v.tensor_copy(f_q[:, :, :], aux[0][:, 0:2 * NFOX].rearrange("p (t h) -> p t h", t=TT)).then_inc(f_sb, 1)
            dve.wait_ge(consts, 1)
            v.tensor_copy(neg_id_r[:, :], neg_id[:, :])
            for bank, base in ((aux[1], 0), (aux[2], HD)):
                part = slice(base, base + NFOX)
                link(v.tensor_copy(f_hi[part, :], bank[part, 0:S]))
                last = TTn(f_lo[part, :], bank[part, 0:S], f_hi[part, :].bitcast(f32), ALU.subtract)
            last.then_inc(f_sb, 1)
            dve.wait_ge(f_sb, 2)

            def bias_of(h, tt):
                n = (tt + 1) * P
                return view(bias_t[:, h, :], [[-1, n]], n - 1)

            def cmp_bias(tt, count):
                at = S - 1 - (CMP_LEN - 1) if tt else P - 1 - (CMP_LEN - 1)
                return view(bias_t[:, :, :], [[S, NNSA], [-CMP_STRIDE, count]], at)

            def compress_inputs(n):
                dve.wait_ge(evac_add, 8)
                dst, tokens, blocks = ((0, 0, 16), (1, 16, 15))[n]
                for odd in range(2):
                    src = z_t[odd * HD:(odd + 1) * HD, 18:21, :]
                    pos = view(pos_t[odd * HD:(odd + 1) * HD, :], [[0, 3], [0, blocks], [1, 16]], 16 * dst)
                    out = view(cmp_in[dst * HD:(dst + 1) * HD, odd:odd + 1, :],
                               [[2 * S, 3], [16, blocks], [1, 16]])
                    last = TTn(out, view(src, [[S, 3], [16, blocks], [1, 16]], tokens), pos, ALU.add)
                last.then_inc(cmp_x, 1)

            def outputs(unit):
                a = 4 * unit
                dve.wait_ge(o_ready, a + 4)
                link(v.reciprocal(row_r[:, 2 * a:2 * a + 8], row_sum[:, 2 * a:2 * a + 8]))
                if a >= NFOX:
                    h = (a - NFOX) % NNSA
                    branch = 1 + (a - NFOX) // NNSA
                    g = view(gate[:, :, :], [[3, 4], [3 * NNSA, TT]], 3 * h + branch)
                    r = view(row_r[:, :], [[2, 4], [1, TT]], 2 * a)
                    link(TTn(r, r, g, ALU.mult))
                    at = NFOX * HD + h * HD
                else:
                    at = a * HD
                r = view(row_r[:, :], [[1, TT], [2, 4], [0, HD]], 2 * a)
                out = view(mix[:, :, :], [[(NFOX + NNSA) * HD, TT], [HD, 4], [1, HD]], at)
                bank = view(o_bank[unit % 2], [[4 * HD, TT], [HD, 4], [1, HD]])
                if a < 24:
                    TTn(out, bank, r, ALU.mult).then_inc(o_used, 1)
                else:
                    t = view(add_t[:, :], [[4 * HD, TT], [HD, 4], [1, HD]])
                    TTn(t, bank, r, ALU.mult).then_inc(o_used, 1)
                    dve.wait_ge(o_used, unit + 1)
                    link(TTn(out, out, t, ALU.add))

            for a in range(36 + 5):
                if a < 36:
                    sc, ps = score[a % 3], aux[a % 3]
                    dve.wait_ge(s_ready, a + 1)
                    if a >= 3:
                        dve.wait_ge(t_ready, a - 2)
                    if a < NFOX:
                        for tt, (at, n) in enumerate(((0, P), (P, S))):
                            biased = STT(sc[:, at:at + n], ps[:, at:at + n], f_q[:, tt, a:a + 1],
                                         causal[:, S - n:S], ALU.add, ALU.add)
                        link(biased)
                        for tt, (at, n) in enumerate(((0, P), (P, S))):
                            last = v.tensor_reduce(neg_max[:, 2 * a + tt:2 * a + tt + 1], sc[:, at:at + n],
                                                   AX.X, ALU.max, negate=True)
                    else:
                        if a == NFOX:
                            dve.wait_ge(bias_in, 16)
                        h = (a - NFOX) % NNSA
                        for tt, (at, n) in enumerate(((0, P), (P, S))):
                            last = v.tensor_tensor_reduce(
                                out=sc[:, at:at + n], in0=ps[:, at:at + n], in1=bias_of(h, tt), scale=-1.0,
                                scalar=3e38, op0=ALU.add, op1=ALU.min,
                                accum_out=neg_max[:, 2 * a + tt:2 * a + tt + 1])
                    last.then_inc(s_biased, 1)
                if a == 39:
                    for j in range(4):
                        weight_lo(G_OUT, j)
                if a >= 5 and (a - 5) % 4 == 3:
                    outputs((a - 5) // 4)
                if a in MOD_HEADS:
                    later_modulation(m)
                    m += 1
                if a == 22:
                    dve.wait_ge(pe_mod, 5)
                    v.tensor_copy(shift2[:, :], aux[3][:, 0:KT]).then_inc(col_ok, 1)
                if a == 2:
                    dve.wait_ge(ln_ps, 1)
                    link(TTn(conv_y[:, :, :], conv_y[:, :, :], view(aux[3][:, 0:S], [[0, CT], [1, S]]),
                             ALU.subtract))
                    TTn(conv_in[:, :, 0:S], conv_y[:, :, :], conv_y[:, :, :], ALU.mult).then_inc(ln_sq, 1)
                if a in (12, 13):
                    dve.wait_ge(pe_half, 8 * N_IN)
                    compress_inputs(a - 12)
                if a == 6:
                    dve.wait_ge(ln_ps, 2)
                    TS(var_b, aux[3][:, S:2 * S], EPS, None, ALU.add).then_inc(ln_var, 1)
                if a == 9:
                    dve.wait_ge(ln_root, 1)
                    link(v.reciprocal(inv_b, root_b))
                    link(TTn(newton_b, inv_b, inv_b, ALU.mult))
                    link(TTn(newton_b, newton_b, var_b, ALU.mult))
                    link(TS(newton_b, newton_b, -0.5, 1.5, ALU.mult, ALU.add))
                    link(TTn(inv_b, inv_b, newton_b, ALU.mult))
                if a == 10:
                    link(TTn(conv_y[:, :, :], conv_y[:, :, :], view(conv_in[:, 2, 0:S], [[0, CT], [1, S]]),
                             ALU.mult))
                if a == 11:
                    for ct in range(CT):
                        last = TS(conv_y[:, ct, :], conv_y[:, ct, :], lng[:, ct:ct + 1], lnb[:, ct:ct + 1],
                                  ALU.mult, ALU.add)
                    last.then_inc(ln_y, 1)
                if a == 16:
                    dve.wait_ge(ln_sig, 1)
                    link(TTn(conv_y[:, :, :], conv_y[:, :, :], conv_in[:, :, 0:S], ALU.mult))
                if a == 15:
                    v.memset(v_cmp[:, :, :], 0.0)
                    v.memset(k_cmp[:, :, :], 0.0)
                    link(v.memset(v_cmp_t[:, :, :], 0.0))
                    link(v.memset(s_cmp[:, :, :, :], NEG))
                    link(v.memset(p_cmp[:, :, :, 16:32], 0.0))
                    dve.wait_ge(cmp_ps, 1)
                    kc = aux[3][0:HD, 0:NKV * NCMP].rearrange("p (g n) -> p g n", g=NKV)
                    v.tensor_copy(k_cmp[0:HD, :, 0:NCMP], kc)
                    v.tensor_copy(k_cmp[HD:P, :, 16:16 + NCMP], kc).then_inc(cmp_sb, 1)
                    for g in range(NKV):
                        last = v.tensor_copy(view(v_cmp_t[:, g, :], [[32, 4], [1, NCMP]]),
                                             view(aux[3][0:HD, :], [[0, 4], [1, NCMP]], HD + g * NCMP))
                    last.then_inc(cmp_sb, 1)
                if a == 19:
                    dve.wait_ge(cmp_ps, 2)
                    for r in range(4):
                        rows_r = slice(32 * r, 32 * r + 32)
                        last = v.tensor_copy(v_cmp[rows_r, :, r * HD:(r + 1) * HD],
                                             aux[3][rows_r, P:P + NKV * HD].rearrange("p (g d) -> p g d", g=NKV))
                    last.then_inc(cmp_sb, 1)
                if a == 23:
                    dve.wait_ge(cmp_ps, 3)
                    for tt, count in enumerate((NCMP0, NCMP)):
                        last = TTn(s_cmp[:, tt, :, 0:count],
                                   view(aux[3][:, :], [[16, NNSA], [1, count]], tt * NNSA * 16),
                                   cmp_bias(tt, count), ALU.add)
                    last.then_inc(cmp_sb, 1)
                    dve.wait_ge(cmp_sb, 4)
                    flat = s_cmp[:, :, :, :].rearrange("p t h n -> p (t h) n")
                    link(v.tensor_reduce(cmp_m[:, :], flat, AX.X, ALU.max))
                    TTn(flat, flat, view(cmp_m[:, :], [[1, TT * NNSA], [0, 16]]), ALU.subtract).then_inc(cmp_x, 1)
                if a == 27:
                    dve.wait_ge(cmp_exp, 1)
                    probs = view(p_cmp[:, :, :, :], [[32, TT * NNSA], [1, 16]])
                    link(v.tensor_reduce(cmp_m[:, :], probs, AX.X, ALU.add))
                    link(v.reciprocal(cmp_r[:, :], cmp_m[:, :]))
                    r3 = cmp_r[:, :].rearrange("p (t h) -> p t h", t=TT)
                    link(TTn(r3, r3, view(gate[:, :, :], [[3 * NNSA, TT], [3, NNSA]]), ALU.mult))
                    link(TS(cmp_r[:, 0:NNSA], cmp_r[:, 0:NNSA], seen[:, 0:1], None, ALU.mult))
                if a in (31, 35):
                    tt = (a - 31) // 4
                    dve.wait_ge(cmp_ps, 4 + tt)
                    v.tensor_copy(view(p_cmp_t, [[1, NKV * P]], tt * NKV * P), aux[3][:, 0:NKV * P])\
                        .then_inc(cmp_sb, 1)
            dve.wait_ge(cmp_ps, 6)
            for n in range(3):
                units = [divmod(2 * n + i, NKV) for i in range(2)]
                for i, (tt, g) in enumerate(units):
                    TTn(view(add_t[:, :], [[HD, 4], [1, HD]], i * S),
                        view(aux[n][:, :], [[HD, 4], [1, HD]], i * S),
                        view(cmp_r[:, :], [[1, 4], [0, HD]], tt * NNSA + 4 * g), ALU.mult).then_inc(mix_mul, 1)
                dve.wait_ge(mix_mul, 2 * n + 2)
                for i, (tt, g) in enumerate(units):
                    out = mix[:, tt, NFOX * HD + g * 4 * HD:NFOX * HD + (g + 1) * 4 * HD]
                    last = TTn(out, out, add_t[:, i * S:(i + 1) * S], ALU.add)
                last.then_inc(mix_done, 1)
                dve.wait_ge(mix_done, n + 1)
            for b in range(8):
                dve.wait_ge(mt_hi, b + 1)
                src = (aux[b % 2][:, :].rearrange("p (k t) -> p k t", k=2) if b < 6
                       else conv_y[:, 2 * (b - 6):2 * (b - 6) + 2, :])
                TTn(act_lo[:, 2 * b:2 * b + 2, :], src, act_hi[:, 2 * b:2 * b + 2, :].bitcast(f32),
                    ALU.subtract).then_inc(mix_ready, 1)

            def gated(bank3, row, cols, done):
                gate3 = view(row[:, cols], [[0, TT], [1, GW]])
                if done:
                    dve.wait_ge(x2_sum, done)
                TTn(upd3, bank3, gate3, ALU.mult).then_inc(evac_dve, 1)

            upd3 = upd[:, :].rearrange("p (t n) -> p t n", t=TT)
            bank3 = [pair[i][:, :].rearrange("p (t n) -> p t n", t=TT) for i in range(2)]

            def out_residual(i):
                dve.wait_ge(pe_half, 8 * (G_OUT + i + 1))
                if i == 0:
                    dve.wait_ge(x2_in, 16 * TT)
                    dve.wait_ge(gate_row, 4)
                cols = slice(i * GW, (i + 1) * GW)
                gated(bank3[(1 + i) % 2], acc[1], cols, i)
                dve.wait_ge(evac_dve, i + 1)
                TTn(x2[:, :, cols], x2[:, :, cols], upd3, ALU.add).then_inc(x2_sum, 1)

            m = MOD_FIRST + MOD_IN + len(MOD_HEADS)
            for i in range(4):
                for j in range(HALVES):
                    if j == 4 and i:
                        out_residual(i - 1)
                    if i or j >= 4:
                        weight_lo(G_OUT + i, j)
                    if j % 2 and j // 2 < MOD_OUT[i]:
                        later_modulation(m)
                        m += 1
            for j in range(3):
                weight_lo(G_MLP, j)
            out_residual(3)
            weight_lo(G_MLP, 3)
            dve.wait_ge(pe_mod, 7)
            STT(scale_h[:, :], aux[2][:, KT:2 * KT], 1.0, n2[:, :], ALU.add, ALU.mult).then_inc(col_ok, 1)
            inverse_rms(1)
            dve.wait_ge(rstd_ok, 2)
            for n in range(2 * TT):
                tt, cols = n % TT, slice(n // TT * (D // 2), (n // TT + 1) * (D // 2))
                TS(xn2[:, tt, cols], x2[:, tt, cols], rstd[:, tt:tt + 1], None, ALU.mult).then_inc(xn_ok, 1)
            split_h(1, h2_f, h2_ready)

            def square(q, i):
                tiles = slice(4 * i, 4 * i + 4)
                r3 = relu[:, :].rearrange("p (k t) -> p k t", k=4)
                dve.wait_ge(evac_act, q * 4 + (N_IN + i + 1))
                TTn(relu[:, :], relu[:, :], relu[:, :], ALU.mult).then_inc(u_step, 1)
                dve.wait_ge(u_step, q * 8 + (2 * i + 1))
                v.tensor_copy(u_hi[:, tiles, :], r3).then_inc(u_step, 1)
                dve.wait_ge(u_step, q * 8 + (2 * i + 2))
                TTn(u_lo[:, tiles, :], r3, u_hi[:, tiles, :].bitcast(f32), ALU.subtract).then_inc(u_ready, 1)

            def down_sum(q, cg, first=False):
                cols = slice(cg * GW, (cg + 1) * GW)
                dve.wait_ge(pe_half, q * 64 + 8 * (G_MLP + 4 + cg + 1))
                if first:
                    v.tensor_copy(y[:, :, cols], bank3[(1 + cg) % 2]).then_inc(evac_dve, 1)
                else:
                    dve.wait_ge(evac_dve, q * 4 + (cg + 1))
                    TTn(y[:, :, cols], y[:, :, cols], bank3[(1 + cg) % 2], ALU.add).then_inc(evac_dve, 1)

            def gate_y():
                dve.wait_ge(gate_row, 8)
                dve.wait_ge(evac_dve, 4 + 4 * (QUARTERS - 1))
                for cg in range(4):
                    cols = slice(cg * GW, (cg + 1) * GW)
                    link(TTn(y[:, :, cols], y[:, :, cols], view(acc[0][:, cols], [[0, TT], [1, GW]]), ALU.mult))
                    TTn(x2[:, :, cols], x2[:, :, cols], y[:, :, cols], ALU.add).then_inc(x2_sum, 1)
                    yield

            def down_last(cg):
                cols = slice(cg * GW, (cg + 1) * GW)
                done = 4 * QUARTERS + cg + 1
                dve.wait_ge(pe_half, 8 * (N_GROUPS - 4 + cg + 1))
                gated(bank3[(1 + cg) % 2], acc[0], cols, 8 + cg)
                dve.wait_ge(evac_dve, done)
                TTn(x2[:, :, cols], x2[:, :, cols], upd3, ALU.add).then_inc(x2_sum, 1)
                dve.wait_ge(x2_sum, 8 + cg + 1)
                TTn(y[:, :, cols], x2[:, :, cols], view(acc[1][:, cols], [[0, TT], [1, GW]]), ALU.mult)\
                    .then_inc(y_gain, 1)

            def mlp_quarter(q, first=False, final=False):
                gating = gate_y()
                for i in range(8):
                    for j in range(HALVES):
                        if j == 4 and i >= 5:
                            if final:
                                down_last(i - 5)
                            else:
                                down_sum(q, i - 5, first)
                        if j == 4 and i == 0 and not first:
                            down_sum(q - 1, 3, isinstance(q, int) and q == 1)
                        if j == 5 and 1 <= i <= 4:
                            square(q, i - 1)
                        if final and (i, j) in ((4, 6), (4, 7), (5, 2), (5, 3)):
                            next(gating)
                        if not (first and i == 0 and j < 4):
                            weight_lo(q * 8 + (G_MLP + i), j)
                        if i < 4 and j == 3:
                            modulation(q * 4 + (5 * KT + i), q * 4 + i, 5, mod_raw[i % 2], mod_full[i % 2],
                                       q * 32 + 16 * ((5 * KT - MOD_FIRST + i) // 2 + 1), first and i == 0)

            mlp_quarter(0, first=True)
            mlp_quarter(1)
            with dve.Fori(2, QUARTERS - 1) as q:
                mlp_quarter(q)
            dve.wait_ge(fg_in, 16)
            mlp_quarter(QUARTERS - 1, final=True)
            down_last(3)
            inverse_rms(2)
            dve.wait_ge(rstd_ok, 3)
            dve.wait_ge(y_gain, 4)
            for i in (0, 2):
                tt, cols = final_part(i)
                TS(y_out[i][:, 0:D // 2], y[:, tt, cols], rstd[:, tt:tt + 1], None, ALU.mult).then_inc(y_ok, 1)


def t5_one_hot():
    n = np.arange(S)
    exact = NB // 2
    nf = np.maximum(n, 1).astype(np.float32)
    large = exact + (np.log(nf / np.float32(exact)) / np.float32(math.log(128 / exact))
                     * np.float32(NB - exact)).astype(np.int32)
    bucket = np.where(n < exact, n, np.minimum(large, NB - 1))
    return np.ascontiguousarray((np.arange(NB)[:, None] == bucket[None, :]).astype(np.float32))


def blocks(w):
    n = w.shape[1] // GW
    return w.reshape(4, 4, P, n, GW).transpose(3, 0, 2, 1, 4).reshape(n * 4, P, 4 * GW)


def by_partition(a, tiles):
    return np.ascontiguousarray(np.asarray(a).reshape(tiles, P).T)


def kernel(x, c, w_mod, b_mod, norm1_g, w_in, b_f, w_cmp_k, w_cmp_v, pos_cmp, conv_w, conv_b, conv_ln_g,
           conv_ln_b, w_out, norm2_g, w_mlp1, w_mlp2, rel_bias, final_g):
    import concourse.bacc as _bacc
    from concourse.bass_utils import run_bass_kernel_spmd as _run

    w_in = np.asarray(w_in)[0]
    order6 = [["sh1", "sc1", "g1", "sh2", "sc2", "g2"].index(n) for n in SECTIONS]
    mod = np.asarray(w_mod)[0].reshape(KT, P, 6, D).transpose(2, 0, 1, 3)[order6]
    early = mod[:2].reshape(2, KT // 2, 2, P, 2, D // 2).transpose(4, 0, 1, 3, 2, 5)
    names = ["fq", "fk", "fv", "f", "nq", "kc", "vc", "ks", "vs", "kw", "vw", "ng", "ca", "cg"]
    d_h, d_kv = NFOX * HD, NKV * HD
    sizes = [d_h, d_h, d_h, NFOX, NNSA * HD] + [d_kv] * 6 + [3 * NNSA, D_CONV, D_CONV]
    at = dict(zip(names, np.split(w_in, np.cumsum(sizes)[:-1], axis=1)))
    transposed = np.concatenate([at[n] for n in ("ca", "cg", "fq", "nq", "fk", "kc", "vc", "ks", "kw")], axis=1)
    straight = np.concatenate([at[n] for n in ("fv", "vs", "vw", "f", "ng")], axis=1)
    tail = straight[:, 2 * GW:]
    b_in = blocks(transposed)
    b_straight = blocks(straight[:, :2 * GW])
    w1, w2 = np.asarray(w_mlp1)[0], np.asarray(w_mlp2)[0]
    stream = [b_in, b_straight[:4], b_straight, blocks(np.asarray(w_out)[0])]
    for q in range(QUARTERS):
        stream += [blocks(w1[:, q * D:(q + 1) * D]), blocks(w2[q * D:(q + 1) * D])]
    w_cmp = [np.asarray(w)[0].reshape(2, CMP_STRIDE, HD, HD).transpose(0, 2, 1, 3) for w in (w_cmp_k, w_cmp_v)]
    host = {
        "x": np.asarray(x).reshape(S, D),
        "c": by_partition(c, KT),
        "w_mod": np.concatenate([early.reshape(2 * KT, P, D), mod[2:].reshape(4 * KT, P, D)]),
        "b_mod": np.asarray(b_mod).reshape(6, D)[order6],
        "norm1_g": by_partition(norm1_g, KT),
        "norm2_g": by_partition(norm2_g, KT),
        "final_g": np.asarray(final_g).reshape(1, D),
        "w_main": np.concatenate(stream),
        "w_tail": tail.reshape(4, 4, P, TAIL).transpose(0, 2, 1, 3).reshape(4, P, 4 * TAIL),
        "b_f": np.asarray(b_f).reshape(1, NFOX),
        "w_cmp_k": w_cmp[0],
        "w_cmp_v": w_cmp[1],
        "pos": np.asarray(pos_cmp)[0].T,
        "conv_w": np.asarray(conv_w)[0].reshape(CONV_W, CT, P).transpose(2, 1, 0),
        "conv_b": by_partition(conv_b, CT),
        "conv_ln_g": by_partition(conv_ln_g, CT),
        "conv_ln_b": by_partition(conv_ln_b, CT),
        "rel_bias": np.asarray(rel_bias),
        "bucket_one_hot": t5_one_hot(),
    }
    nc = _bacc.Bacc("TRN2", target_bir_lowering=False, num_devices=1)
    arrays, args = {}, []
    for name, a in host.items():
        a = np.ascontiguousarray(a)
        arrays[f"in_{name}"] = a
        args.append(nc.dram_tensor(f"in_{name}", a.shape, mybir.dt.from_np(a.dtype), kind="ExternalInput").ap())
    out = nc.dram_tensor("out", (S, D), mybir.dt.float32, kind="ExternalOutput").ap()
    order = ["x", "c", "w_mod", "b_mod", "norm1_g", "norm2_g", "final_g", "w_main", "w_tail", "b_f", "w_cmp_k",
             "w_cmp_v", "pos", "conv_w", "conv_b", "conv_ln_g", "conv_ln_b", "rel_bias", "bucket_one_hot"]
    by_name = dict(zip(host, args))
    build(nc, *[by_name[n] for n in order], out)
    r = _run(nc, [arrays], core_ids=[0])
    return r.results[0]["out"].reshape(1, S, D)
```
